# Optimizing a Trainium2 kernel written in Bass

```python
import math
import jax
import jax.numpy as jnp
from jax import lax
import numpy as np

D_MODEL = 1024
BATCH = 1
SEQ = 256
DEPTH = 2
DEC_BATCH = 8
DEC_SEQ = 1
PAST_LEN = 256
PAGE_SIZE = 128

N_HEADS = 16
HEAD_DIM = D_MODEL // N_HEADS
MOBA_BLOCK = 256
MOBA_TOPK = 3
QUERY_CHUNK = 64
CONV_WIDTH = 31
D_FF = 2816
N_EXPERTS = 8
MOE_TOPK = 2
D_FF_EXPERT = 3584
EXPERT_GROUP = 128
N_ATTN_LAYERS = (DEPTH + 1) // 2
N_CONV_LAYERS = DEPTH // 2
LN_EPS = 1e-5
DEEPNORM_ALPHA = (2 * DEPTH) ** 0.25
DEEPNORM_BETA = (8 * DEPTH) ** -0.25

kernel_name = 'moba_conformer_moe_decoder_step'

def _layernorm(x, g, b):
    xf = x.astype(jnp.float32)
    mu = jnp.mean(xf, axis=-1, keepdims=True)
    var = jnp.mean(jnp.square(xf - mu), axis=-1, keepdims=True)
    y = (xf - mu) * lax.rsqrt(var + LN_EPS) * g.astype(jnp.float32) + b.astype(jnp.float32)
    return y.astype(x.dtype)

def _adaln(c, w, b):
    m = (jax.nn.silu(c) @ w + b).reshape(c.shape[0], 6, 1, D_MODEL)
    return [m[:, k] for k in range(6)]

def _modulate(x, shift, scale):
    return x * (1 + scale) + shift

def _alibi_slopes():
    return 2.0 ** (-8.0 * jnp.arange(1, N_HEADS + 1, dtype=jnp.float32) / N_HEADS)

def _qkv(h, w_qkv):
    n, t, _ = h.shape
    qkv = (h @ w_qkv).reshape(n, t, 3, N_HEADS, HEAD_DIM)
    return qkv[:, :, 0], qkv[:, :, 1], qkv[:, :, 2]

def _moba_core(q, qpos, k_seq, v_seq):
    nq = q.shape[0]
    seq_len = k_seq.shape[0]
    nb = -(-seq_len // MOBA_BLOCK)
    pad = nb * MOBA_BLOCK - seq_len
    kb = jnp.pad(k_seq, ((0, pad), (0, 0), (0, 0))).reshape(nb, MOBA_BLOCK, N_HEADS, HEAD_DIM).transpose(2, 0, 1, 3)
    vb = jnp.pad(v_seq, ((0, pad), (0, 0), (0, 0))).reshape(nb, MOBA_BLOCK, N_HEADS, HEAD_DIM).transpose(2, 0, 1, 3)
    kmean = jnp.mean(kb, axis=2, dtype=jnp.float32)
    own = qpos // MOBA_BLOCK
    gate = jnp.einsum('qhd,hnd->qhn', q.astype(jnp.float32), kmean)
    fully_past = jnp.arange(nb)[None, None, :] < own[:, None, None]
    gate = jnp.where(fully_past, gate, -jnp.inf)
    kk = min(MOBA_TOPK, nb)
    _, top = lax.top_k(gate, kk)
    sel_ok = jnp.broadcast_to(jnp.arange(kk)[None, None, :] < own[:, None, None], (nq, N_HEADS, kk))
    blocks = jnp.concatenate([top, jnp.broadcast_to(own[:, None, None], (nq, N_HEADS, 1)).astype(top.dtype)], axis=-1)
    blk_ok = jnp.concatenate([sel_ok, jnp.ones((nq, N_HEADS, 1), dtype=bool)], axis=-1)
    hidx = jnp.arange(N_HEADS)[None, :, None]
    kg = kb[hidx, blocks]
    vg = vb[hidx, blocks]
    kpos = blocks[..., None] * MOBA_BLOCK + jnp.arange(MOBA_BLOCK)
    dist = qpos[:, None, None, None] - kpos
    ok = blk_ok[..., None] & (dist >= 0)
    s = jnp.einsum('qhd,qhjkd->qhjk', q, kg, preferred_element_type=jnp.float32) * (HEAD_DIM ** -0.5)
    s = s - _alibi_slopes()[None, :, None, None] * dist.astype(jnp.float32)
    s = jnp.where(ok, s, -jnp.inf)
    p = jax.nn.softmax(s.reshape(nq, N_HEADS, -1), axis=-1).reshape(s.shape)
    return jnp.einsum('qhjk,qhjkd->qhd', p.astype(vg.dtype), vg).astype(q.dtype)

def _moba_prompt(q, k, v):
    b, s = q.shape[:2]
    nc = s // QUERY_CHUNK
    q_items = q.reshape(b * nc, QUERY_CHUNK, N_HEADS, HEAD_DIM)
    pos_items = jnp.tile(jnp.arange(s, dtype=jnp.int32).reshape(nc, QUERY_CHUNK), (b, 1))
    b_items = jnp.repeat(jnp.arange(b, dtype=jnp.int32), nc)
    out = lax.map(lambda it: _moba_core(it[0], it[1], k[it[2]], v[it[2]]), (q_items, pos_items, b_items))
    return out.reshape(b, s, N_HEADS, HEAD_DIM)

def _moba_sample(q, k_new, v_new, cache_k, cache_v, layer, page_table):
    ds = q.shape[1]
    past_len = page_table.shape[1] * PAGE_SIZE
    qpos = past_len + jnp.arange(ds, dtype=jnp.int32)

    def one(it):
        qn, kn, vn, pt = it
        k_seq = jnp.concatenate([cache_k[layer, pt].reshape(past_len, N_HEADS, HEAD_DIM), kn.astype(cache_k.dtype)], axis=0)
        v_seq = jnp.concatenate([cache_v[layer, pt].reshape(past_len, N_HEADS, HEAD_DIM), vn.astype(cache_v.dtype)], axis=0)
        return _moba_core(qn, qpos, k_seq, v_seq)

    return lax.map(one, (q, k_new, v_new, page_table))

def _conv_module(h, hist, w_pw1, b_pw1, w_dw, b_dw, ln_gain, ln_bias, w_pw2, b_pw2):
    a, g = jnp.split(h @ w_pw1 + b_pw1, 2, axis=-1)
    u = a * jax.nn.sigmoid(g)
    up = jnp.concatenate([hist.astype(u.dtype), u], axis=1)
    y = lax.conv_general_dilated(up, w_dw[:, None, :].astype(u.dtype), (1,), 'VALID',
                                 dimension_numbers=('NWC', 'WIO', 'NWC'),
                                 feature_group_count=D_MODEL) + b_dw
    y = jax.nn.silu(_layernorm(y, ln_gain, ln_bias))
    return y @ w_pw2 + b_pw2, up[:, -(CONV_WIDTH - 1):]

def _swiglu(h, w1, w3, w2):
    return (jax.nn.silu(h @ w1) * (h @ w3)) @ w2

def _moe(h, w_router, b_router, w1, w3, w2):
    t, d = h.shape
    logits = (h @ w_router + b_router).astype(jnp.float32)
    top_l, top_e = lax.top_k(logits, MOE_TOPK)
    gates = jax.nn.softmax(top_l, axis=-1)
    n_assign = t * MOE_TOPK
    e_flat = top_e.reshape(-1)
    t_flat = jnp.repeat(jnp.arange(t, dtype=jnp.int32), MOE_TOPK)
    g_flat = gates.reshape(-1)
    order = jnp.argsort(e_flat)
    e_s, t_s, g_s = e_flat[order], t_flat[order], g_flat[order]
    counts = jnp.bincount(e_flat, length=N_EXPERTS)
    starts = jnp.cumsum(counts) - counts
    padded = (counts + EXPERT_GROUP - 1) // EXPERT_GROUP * EXPERT_GROUP
    pad_end = jnp.cumsum(padded)
    pad_start = pad_end - padded
    slot = pad_start[e_s] + jnp.arange(n_assign) - starts[e_s]
    n_grp = -(-n_assign // EXPERT_GROUP) + N_EXPERTS
    buf = jnp.zeros((n_grp * EXPERT_GROUP, d), h.dtype).at[slot].set(h[t_s])
    grp_e = jnp.minimum(jnp.searchsorted(pad_end, jnp.arange(n_grp) * EXPERT_GROUP, side='right'), N_EXPERTS - 1)

    def expert_group(args):
        xg, e = args
        return (jax.nn.silu(xg @ w1[e]) * (xg @ w3[e])) @ w2[e]

    out = lax.map(expert_group, (buf.reshape(n_grp, EXPERT_GROUP, d), grp_e)).reshape(-1, d)
    return jax.ops.segment_sum(out[slot] * g_s[:, None].astype(h.dtype), t_s, num_segments=t)

def setup_inputs(seed: int = 0) -> dict:
    key = jax.random.key(seed)
    ks = jax.random.split(key, 32)
    D = D_MODEL
    n_pages = PAST_LEN // PAGE_SIZE
    n_phys = (DEC_BATCH * n_pages * 5) // 4

    def nrm(k, shape, scale):
        return jax.random.normal(k, shape, jnp.float32) * scale

    page_table = jax.random.permutation(ks[5], n_phys)[: DEC_BATCH * n_pages].reshape(DEC_BATCH, n_pages).astype(jnp.int32)
    return {
        'x_prompt': nrm(ks[0], (BATCH, SEQ, D), 1.0),
        'x_sample': nrm(ks[1], (DEC_BATCH, DEC_SEQ, D), 1.0),
        'cache_k': nrm(ks[2], (N_ATTN_LAYERS, n_phys, PAGE_SIZE, N_HEADS, HEAD_DIM), 1.0),
        'cache_v': nrm(ks[3], (N_ATTN_LAYERS, n_phys, PAGE_SIZE, N_HEADS, HEAD_DIM), 1.0),
        'state_conv': nrm(ks[4], (N_CONV_LAYERS, DEC_BATCH, CONV_WIDTH - 1, D), 0.5),
        'page_table': page_table,
        'c_prompt': nrm(ks[6], (BATCH, D), 1.0),
        'c_sample': nrm(ks[7], (DEC_BATCH, D), 1.0),
        'ada_w': nrm(ks[8], (DEPTH, D, 6 * D), 0.5 * D ** -0.5),
        'ada_b': nrm(ks[9], (DEPTH, 6 * D), 0.02),
        'ln_g': 1.0 + nrm(ks[10], (DEPTH, 2, D), 0.02),
        'ln_b': nrm(ks[11], (DEPTH, 2, D), 0.02),
        'attn_w_qkv': nrm(ks[12], (N_ATTN_LAYERS, D, 3 * D), D ** -0.5),
        'attn_w_o': nrm(ks[13], (N_ATTN_LAYERS, D, D), DEEPNORM_BETA * D ** -0.5),
        'conv_w_pw1': nrm(ks[14], (N_CONV_LAYERS, D, 2 * D), D ** -0.5),
        'conv_b_pw1': nrm(ks[15], (N_CONV_LAYERS, 2 * D), 0.02),
        'conv_w_dw': nrm(ks[16], (N_CONV_LAYERS, CONV_WIDTH, D), CONV_WIDTH ** -0.5),
        'conv_b_dw': nrm(ks[17], (N_CONV_LAYERS, D), 0.02),
        'conv_ln_g': 1.0 + nrm(ks[18], (N_CONV_LAYERS, D), 0.02),
        'conv_ln_b': nrm(ks[19], (N_CONV_LAYERS, D), 0.02),
        'conv_w_pw2': nrm(ks[20], (N_CONV_LAYERS, D, D), DEEPNORM_BETA * D ** -0.5),
        'conv_b_pw2': nrm(ks[21], (N_CONV_LAYERS, D), 0.02),
        'ffn_w1': nrm(ks[22], (N_ATTN_LAYERS, D, D_FF), D ** -0.5),
        'ffn_w3': nrm(ks[23], (N_ATTN_LAYERS, D, D_FF), D ** -0.5),
        'ffn_w2': nrm(ks[24], (N_ATTN_LAYERS, D_FF, D), DEEPNORM_BETA * D_FF ** -0.5),
        'moe_w_router': nrm(ks[25], (N_CONV_LAYERS, D, N_EXPERTS), D ** -0.5),
        'moe_b_router': nrm(ks[26], (N_CONV_LAYERS, N_EXPERTS), 0.01),
        'moe_w1': nrm(ks[27], (N_CONV_LAYERS, N_EXPERTS, D, D_FF_EXPERT), D ** -0.5),
        'moe_w3': nrm(ks[28], (N_CONV_LAYERS, N_EXPERTS, D, D_FF_EXPERT), D ** -0.5),
        'moe_w2': nrm(ks[29], (N_CONV_LAYERS, N_EXPERTS, D_FF_EXPERT, D), DEEPNORM_BETA * D_FF_EXPERT ** -0.5),
    }

def reference(x_prompt, x_sample, cache_k, cache_v, state_conv, page_table, c_prompt, c_sample,
              ada_w, ada_b, ln_g, ln_b, attn_w_qkv, attn_w_o,
              conv_w_pw1, conv_b_pw1, conv_w_dw, conv_b_dw, conv_ln_g, conv_ln_b, conv_w_pw2, conv_b_pw2,
              ffn_w1, ffn_w3, ffn_w2, moe_w_router, moe_b_router, moe_w1, moe_w3, moe_w2):
    b, s, d = x_prompt.shape
    db, ds, _ = x_sample.shape
    yp, ys = x_prompt, x_sample
    kp_l, vp_l, ks_l, vs_l, cp_l, cs_l = [], [], [], [], [], []
    for i in range(DEPTH):
        j = i // 2
        shm_p, scm_p, gm_p, shf_p, scf_p, gf_p = _adaln(c_prompt, ada_w[i], ada_b[i])
        shm_s, scm_s, gm_s, shf_s, scf_s, gf_s = _adaln(c_sample, ada_w[i], ada_b[i])
        hp = _modulate(yp, shm_p, scm_p)
        hs = _modulate(ys, shm_s, scm_s)
        if i % 2 == 0:
            qp, kp, vp = _qkv(hp, attn_w_qkv[j])
            qs, kq, vq = _qkv(hs, attn_w_qkv[j])
            mp = _moba_prompt(qp, kp, vp).reshape(b, s, d) @ attn_w_o[j]
            ms = _moba_sample(qs, kq, vq, cache_k, cache_v, j, page_table).reshape(db, ds, d) @ attn_w_o[j]
            kp_l.append(kp)
            vp_l.append(vp)
            ks_l.append(kq)
            vs_l.append(vq)
        else:
            conv_args = (conv_w_pw1[j], conv_b_pw1[j], conv_w_dw[j], conv_b_dw[j],
                         conv_ln_g[j], conv_ln_b[j], conv_w_pw2[j], conv_b_pw2[j])
            mp, cp = _conv_module(hp, jnp.zeros((b, CONV_WIDTH - 1, d), hp.dtype), *conv_args)
            ms, cs = _conv_module(hs, state_conv[j], *conv_args)
            cp_l.append(cp)
            cs_l.append(cs)
        yp = _layernorm(DEEPNORM_ALPHA * yp + (1 + gm_p) * mp, ln_g[i, 0], ln_b[i, 0])
        ys = _layernorm(DEEPNORM_ALPHA * ys + (1 + gm_s) * ms, ln_g[i, 0], ln_b[i, 0])
        hp = _modulate(yp, shf_p, scf_p)
        hs = _modulate(ys, shf_s, scf_s)
        if i % 2 == 0:
            fp = _swiglu(hp, ffn_w1[j], ffn_w3[j], ffn_w2[j])
            fs = _swiglu(hs, ffn_w1[j], ffn_w3[j], ffn_w2[j])
        else:
            fp = _moe(hp.reshape(b * s, d), moe_w_router[j], moe_b_router[j], moe_w1[j], moe_w3[j], moe_w2[j]).reshape(b, s, d)
            fs = _moe(hs.reshape(db * ds, d), moe_w_router[j], moe_b_router[j], moe_w1[j], moe_w3[j], moe_w2[j]).reshape(db, ds, d)
        yp = _layernorm(DEEPNORM_ALPHA * yp + (1 + gf_p) * fp, ln_g[i, 1], ln_b[i, 1])
        ys = _layernorm(DEEPNORM_ALPHA * ys + (1 + gf_s) * fs, ln_g[i, 1], ln_b[i, 1])
    return (yp, ys, jnp.stack(kp_l), jnp.stack(vp_l), jnp.stack(ks_l), jnp.stack(vs_l), jnp.stack(cp_l), jnp.stack(cs_l))


_drawn_inputs = setup_inputs


def setup_inputs(seed=0):
    import zlib

    import numpy as np

    out = dict(_drawn_inputs(seed))
    spreads = {}
    factors = {'conv_b_pw1': 2.754,
     'conv_b_dw': 2.699,
     'conv_ln_g': 13.896,
     'conv_ln_b': 26.953,
     'conv_b_pw2': 3.435,
     'moe_b_router': 10.621}
    for name, (base, spread) in spreads.items():
        noise = np.random.default_rng([zlib.crc32(name.encode()), seed]).standard_normal(out[name].shape)
        drawn = base * np.exp(spread * noise) if base else spread * noise
        out[name] = jnp.asarray(drawn.astype(out[name].dtype))
    for name, factor in factors.items():
        out[name] = (out[name] * factor).astype(out[name].dtype)
    return out
```

```python
from contextlib import ExitStack

import concourse.bass as bass
from concourse import mybir

F32 = mybir.dt.float32
F32R = mybir.dt.float32r
I32 = mybir.dt.int32
U32 = mybir.dt.uint32
ALU = mybir.AluOpType
ACT = mybir.ActivationFunctionType
AX = mybir.AxisListType

P = 128
D = 1024
KC = D // P
TP = 256
NS = 8
T = TP + NS
TILES = ((0, 128), (128, 128), (256, NS))
H, HD = 16, 64
PAST = 256
PAGES = PAST // P
CW = 31
FF = 2816
FM = FF // P
NE = 8
FE = 3584
EJ = FE // 512
GROUPS = 3
ITEMS = GROUPS * NE
MORE = ITEMS - NE
ALPHA = float(4.0 ** 0.25)
EPS = 1e-5
MASKED = -1e30

RING = 7
SLOTW = 4096
UNITS = 4
UW = SLOTW // UNITS
SPLITS = 4
TURN = 2
NBANK = 8

PRM_LNG, PRM_LNB, PRM_PW1, PRM_BDW, PRM_CLG, PRM_CLB, PRM_PW2, PRM_DW = 96, 128, 160, 176, 184, 192, 200, 256

EXPERT_SLOTS = [("w1", 0), ("w3", 0)]
for _j in range(1, EJ):
    EXPERT_SLOTS += [("w1", _j), ("w3", _j), ("w2", _j - 1)]
EXPERT_SLOTS += [("w2", EJ - 1)]
ES = len(EXPERT_SLOTS)
EU = ES * UNITS


def last_unit(kind, j):
    return UNITS * (EXPERT_SLOTS.index((kind, j)) + 1) - 1


def build(nc, x_prompt, x_sample, cache_k, cache_v, state_conv, page_table, c_prompt, c_sample,
          ada_w, ada_b, ln_g, ln_b, attn_w_qkv, attn_w_o, conv_w_pw1, conv_b_pw1, conv_w_dw,
          conv_b_dw, conv_ln_g, conv_ln_b, conv_w_pw2, conv_b_pw2, ffn_w1, ffn_w3, ffn_w2,
          moe_w_router, moe_b_router, moe_w1, moe_w3, moe_w2,
          y_prompt, y_sample, nk_prompt, nv_prompt, nk_sample, nv_sample, nc_prompt, nc_sample):
    ctx = ExitStack()
    with ctx:
        def sb(name, shape, dt=F32, at=ctx):
            return at.enter_context(nc.sbuf_tensor(name, shape, dt))

        sems = {}

        def ev(name):
            if name not in sems:
                sems[name] = ctx.enter_context(nc.semaphore(name))
            return sems[name]

        ring = sb("ring", [P, RING, SLOTW])
        xT = sb("xT", [P, KC, T])
        hT = sb("hT", [P, KC, T])
        zT = sb("zT", [P, KC, T])
        prm = sb("prm", [P, 512])
        adaT = sb("adaT", [P, 2, 48, 9])
        ident = sb("ident", [P, P])
        ones = sb("ones", [P, P])
        mean_w = sb("mean_w", [P, P])
        before = sb("before", [P, P])
        iota_slot = sb("iota_slot", [P, P])
        iota_e = sb("iota_e", [P, NE])
        iota_place = sb("iota_place", [P, MORE + 1])
        below = sb("below", [P, MORE])
        expert_v = sb("expert_v", [P, MORE])
        eps_t = sb("eps_t", [P, 1])
        std = sb("std", [P, T])
        rstd = sb("rstd", [P, T])
        t8 = sb("t8", [P, KC, NS])
        wr = sb("wr", [P, KC, NE])
        br = sb("br", [1, NE])
        attnT = hT
        banks = ctx.enter_context(nc.psum_tensor("banks", [P, NBANK, 512], F32))

        pre = ExitStack()
        arena_w = 14800
        arena = sb("arena", [P, arena_w], at=pre)

        def carve(start):
            at = [start]

            def take(n, parts=P):
                a = at[0]
                at[0] += n
                assert at[0] <= arena_w, at[0]
                return arena[0:parts, a:a + n]
            return take

        A = carve(0)
        qkT = A(2 * KC * T).rearrange("p (c t) -> p c t", t=T)
        v_tok = A(2 * D).rearrange("p (i n) -> p i n", i=2)
        v_s = A(D, NS)
        kx = A(2 * D)
        kx_tok = kx.rearrange("p (i n) -> p i n", i=2)
        kx_s = A(D)
        scT = A(2 * P).rearrange("p (g r) -> p g r", g=2)
        S_p = A(2 * 384).rearrange("p (i n) -> p i n", i=2)
        P_p = A(2 * 384).rearrange("p (i n) -> p i n", i=2)
        PT_p = A(2 * 384).rearrange("p (i n) -> p i n", i=2)
        dist_p = A(384)
        dist_s = A(PAST)
        arow = A(2 * 512).rearrange("p (i n) -> p i n", i=2)
        e16 = A(16)
        e8 = A(NS)
        e8T = rstd[0:NS, 0:P]
        slope8 = A(H)
        slope8_c = A(1)
        st_p = A(16)
        ss = A(H, NS)
        t16 = A(H)
        s_self = A(8)
        S_s = S_p[:, 0, 0:PAST]
        diag = S_p[:, 1, 0:P]
        P_s = P_p[:, 0, 0:PAST]
        PT_s = PT_p[:, 0, 0:PAST].rearrange("p (g r) -> p g r", g=2)
        PD = std[0:NS, 0:P]
        pv_s = std[:, P:2 * P]
        cT = A(KC * 9).rearrange("p (c n) -> p c n", n=9)
        r_off = 2 * KC * T + 2 * D + D + 2 * D + D + 2 * P + 4 * 384
        rows = arena[:, r_off:r_off + 512].rearrange("p (i n) -> p i n", i=4)
        c_off = 2 * KC * T + 2 * D + D + 2 * D + D + 2 * P
        c_rows = arena[0:9, c_off:c_off + D]
        zflat = zT[:, :, :].rearrange("p c t -> p (c t)")
        q_s = zflat[0:NS, 0:D]
        prod = zflat[:, D:2 * D].rearrange("p (g n) -> p g n", g=2)
        sq = arena[:, 0:KC * T].rearrange("p (c t) -> p c t", t=T)

        B = carve(0)
        gT = B(FM * T).rearrange("p (c t) -> p c t", t=T)
        sg = B(2 * T).rearrange("p (i t) -> p i t", i=2)

        C = carve(0)
        st_rows = C(2 * D).rearrange("p (i n) -> p i n", i=2)
        _ = C(KC * T - 2 * D)
        up = C(KC * (CW - 1 + TP)).rearrange("p (c t) -> p c t", c=KC)
        us = C(KC * NS * CW).rearrange("p (c n j) -> p c n j", c=KC, n=NS)
        ydw = C(KC * T).rearrange("p (c t) -> p c t", t=T)
        sgc = C(2 * T).rearrange("p (i t) -> p i t", i=2)
        us_prod = C(NS * CW).rearrange("p (n j) -> p n j", n=NS)
        tmp_c = C(T)
        u_p = C(D, CW - 1)
        u_s = C(D, NS)
        pre.close()

        moe = ExitStack()
        w_hi = sb("w_hi", [P, SPLITS, UW], F32R, at=moe)
        w_lo = sb("w_lo", [P, SPLITS, UW], F32R, at=moe)
        x_hi = sb("x_hi", [P, KC * P], F32R, at=moe)
        x_lo = sb("x_lo", [P, KC * P], F32R, at=moe)
        g_hi = sb("g_hi", [P, 2, 4 * P], F32R, at=moe)
        g_lo = sb("g_lo", [P, 2, 4 * P], F32R, at=moe)
        g_tok = sb("g_tok", [P, 512], at=moe)
        h_tok = sb("h_tok", [P, 3, D], at=moe)
        logit = sb("logit", [P, 3, NE], at=moe)
        top = sb("top", [P, 3, 8], at=moe)
        topi = sb("topi", [P, 3, 8], U32, at=moe)
        topf = sb("topf", [P, 3, 2], at=moe)
        dif = sb("dif", [P, 3], at=moe)
        edif = sb("edif", [P, 3], at=moe)
        gts = sb("gts", [P, 3, 2], at=moe)
        oh = sb("oh", [P, 2, 3, NE], at=moe)
        sel = sb("sel", [P, 3, NE], at=moe)
        rank_w = sb("rank_w", [P, 3, ITEMS + 1], at=moe)
        gate_w = sb("gate_w", [P, 3, ITEMS + 1], at=moe)
        rank_c = sb("rank_c", [P, 3], at=moe)
        rank_n = sb("rank_n", [P, 3], at=moe)
        gate_c = sb("gate_c", [P, 3], at=moe)
        more_f = sb("more_f", [P, MORE], at=moe)
        scan = sb("scan", [P, 2, 2 * MORE], at=moe)
        place = sb("place", [P, MORE], at=moe)
        at_place = sb("at_place", [P, MORE + 1, MORE], at=moe)
        at_value = sb("at_value", [P, MORE + 1, MORE], at=moe)
        n_items = sb("n_items", [P, 1], I32, at=moe)
        column_of = sb("column_of", [P, ITEMS + 1], I32, at=moe)
        expert_of = sb("expert_of", [P, ITEMS + 1], I32, at=moe)
        list_f = sb("list_f", [P, 2, ITEMS + 1], at=moe)
        hflat = hT[:, :, :].rearrange("p c t -> p (c t)")
        out_sb = hflat[:, 0:D]
        sel_t = hflat[:, D:D + 384].rearrange("p (i n) -> p i n", i=3)
        gsel_t = hflat[:, D + 384:D + 768].rearrange("p (i n) -> p i n", i=3)
        gs = hflat[:, D + 768:D + 768 + T]
        moe.close()

        stream = []
        w_qkv, w_o = attn_w_qkv[0], attn_w_o[0]

        def block(name, w, c0, cols, k0=0, kn=KC):
            src = w[k0 * P:(k0 + kn) * P, c0:c0 + cols].rearrange("(k p) n -> p k n", p=P)
            stream.append((name, [(0, kn * cols, kn, src, None)], "pe"))

        def pages(name, cache, n0, consumer):
            loads = []
            for n in range(n0, n0 + 2):
                for g in range(PAGES):
                    loads.append((((n - n0) * PAGES + g) * D, D, 1, cache, (n, g)))
            stream.append((name, loads, consumer))

        def ada(layer, j):
            block(("ada", layer, j), ada_w[layer], j * 512, 512)

        fillers = [(0, j) for j in range(4, 12)] + [(1, j) for j in range(12)]
        filler_at = []
        for c in range(KC):
            filler_at += [(c, 0), (c, 1)] + ([(c, 2)] if c < 4 else [])
        assert len(filler_at) == len(fillers)
        for j in range(4):
            ada(0, j)
        for j in range(6):
            block(("qkv", j), w_qkv, j * 512, 512)
        for (c, k), (layer, j) in zip(filler_at, fillers):
            if k == 0 and c % 2 == 0:
                pages(("K", c // 2), cache_k[0], c, "dve")
            ada(layer, j)
        for i in range(4):
            pages(("V", i), cache_v[0], 2 * i, "pe")
        for j in range(2):
            block(("wo", j), w_o, j * 512, 512)
        for j in range(6):
            block(("f1", j), ffn_w1[0], j * 512, min(512, FF - j * 512))
            block(("f3", j), ffn_w3[0], j * 512, min(512, FF - j * 512))
        for cb in range(4):
            for kh in range(2):
                block(("f2", cb, kh), ffn_w2[0], cb * 256, 256, kh * FM // 2, FM // 2)
        for j in range(2):
            block(("p1", j), conv_w_pw1[0], j * 512, 512)
            block(("p1g", j), conv_w_pw1[0], D + j * 512, 512)
        for j in range(2):
            block(("p2", j), conv_w_pw2[0], j * 512, 512)
        NPRE = len(stream)
        index = {s[0]: n for n, s in enumerate(stream)}
        loaded = []
        per_pos = [0] * RING
        used = {}
        for n, (_n, loads, _who) in enumerate(stream):
            per_pos[n % RING] += 16 * len(loads)
            loaded.append(per_pos[n % RING])
        slot_sem = [ev(f"slot{i}_loaded") for i in range(RING)]

        def pos_of(k):
            return (NPRE + k) % RING

        def moe_loaded(k):
            return per_pos[pos_of(k)] + 16 * (k // RING + 1)

        def slot_of(name, w=512):
            return ring[:, index[name] % RING, :].rearrange("p (k n) -> p k n", n=w)

        def wait_slot(eng, name):
            n = index[name]
            eng.wait_ge(slot_sem[n % RING], loaded[n])

        psum_filled, psum_drained = ev("psum_filled"), ev("psum_drained")
        order = []
        where = {}

        block_ = ctx.enter_context(nc.Block())

        def passes(eng, item):
            with eng.Fori(0, NE) as w:
                item(w)
            eng.wait_ge(ev("moe_list_ready"), 1)
            items = eng.value_load(n_items[0:1, 0:1], min_val=NE, max_val=ITEMS)
            with eng.Fori(NE, ITEMS) as w:
                with eng.If(items > w):
                    item(w)
                eng.nop()

        class Steps:

            def __init__(self, eng, sem):
                self.eng, self.sem, self.n, self.open = eng, sem, {}, {}

            def __call__(self, ins, sem=None, by=1):
                sem = self.sem if sem is None else sem
                ins.then_inc(sem, by)
                key = id(sem)
                self.n[key] = self.n.get(key, 0) + by
                self.open[key] = sem

            def settle(self):
                for key, sem in self.open.items():
                    self.eng.wait_ge(sem, self.n[key])
                self.open = {}

            def announce(self, name):
                self.settle()
                self.eng.sem_inc(ev(name), 1)

        @block_.tensor
        def _(pe):
            def group(name):
                n = len(order)
                if n >= NBANK:
                    pe.wait_ge(psum_drained, n - NBANK + 1)
                order.append(name)
                where[name] = n
                return banks[:, n % NBANK, :]

            def filled(ins):
                ins.then_inc(psum_filled, 1)

            def slot_done(name):
                used[index[name]] = len(order)

            def dense(name, slots, rhs, width=512, m_of=4):
                for s in slots:
                    wait_slot(pe, s)
                for m in range(m_of):
                    for i, s in enumerate(slots):
                        bk = group((name[i], m))
                        for k in range(KC):
                            mm = pe.matmul(bk[:, 0:T], slot_of(s, width)[:, k, m * P:(m + 1) * P], rhs[:, k, :],
                                           start=(k == 0), stop=(k == KC - 1))
                        filled(mm)
                for s in slots:
                    slot_done(s)

            pending = []

            def ada_rows(layer, j):
                name = ("ada", layer, j)
                wait_slot(pe, name)
                bk = group(name)
                for k in range(KC):
                    mm = pe.matmul(bk[0:9, :], cT[:, k, :], slot_of(name)[:, k, :], start=(k == 0), stop=(k == KC - 1))
                filled(mm)
                slot_done(name)
                pending.append((layer, j))

            def ada_turn():
                layer, j = pending.pop(0)
                i = layer * 12 + j
                pe.wait_ge(ev("ada_row_kept"), i + 1)
                bk = group(("adaT", layer, j))
                for m in range(4):
                    mm = pe.transpose(bk[:, 9 * m:9 * m + 9], arow[0:9, i % 2, m * P:(m + 1) * P], ident[0:9, 0:9])
                filled(mm)

            def filler():
                layer, j = todo.pop(0)
                ada_rows(layer, j)
                if len(pending) > 1:
                    ada_turn()

            def turn(name, src, parts, n):
                for half in range(2):
                    bk = group((name, half))
                    for i in range(4):
                        mm = pe.transpose(bk[0:parts, i * P:(i + 1) * P], src(half * 4 + i), ident[:, :])
                    filled(mm)

            def norm(i, z, s):
                pe.wait_ge(ev("ln_input_ready"), i + 1)
                bk = group(("mean", i))
                for k in range(KC):
                    mm = pe.matmul(bk[:, 0:T], mean_w[:, :], z[:, k, :], start=(k == 0), stop=(k == KC - 1))
                filled(mm)
                pe.wait_ge(ev("ln_squares_ready"), i + 1)
                bk = group(("var", i))
                for k in range(KC):
                    mm = pe.matmul(bk[:, 0:T], mean_w[:, :], s[:, k, :], start=(k == 0), stop=(k == KC - 1))
                filled(mm)

            pe.wait_ge(ev("constants_ready"), 1)
            pe.wait_ge(ev("params_loaded"), 16 * 10)
            bk = group("prm")
            for i, r in enumerate((128, 80, 128, 120)):
                mm = pe.transpose(bk[:, i * P:i * P + r], rows[0:r, i, :], ident[0:r, 0:r])
            filled(mm)
            pe.wait_ge(ev("silu_c_ready"), 1)
            bk = group("cT")
            for k in range(KC):
                mm = pe.transpose(bk[:, 9 * k:9 * k + 9], c_rows[:, k * P:(k + 1) * P], ident[0:9, 0:9])
            filled(mm)
            pe.wait_ge(ev("x_loaded"), 16 * 2)
            for k in range(KC):
                bk = group(("xT", k))
                for i, (t0, tn) in enumerate(TILES):
                    src = kx_tok[:, i, k * P:(k + 1) * P] if i < 2 else kx_s[0:NS, k * P:(k + 1) * P]
                    mm = pe.transpose(bk[:, t0:t0 + tn], src, ident[0:tn, 0:tn])
                filled(mm)
            pe.wait_ge(ev("cT_ready"), 1)
            for j in range(4):
                ada_rows(0, j)
                if len(pending) > 1:
                    ada_turn()
            ada_turn()
            pe.wait_ge(ev("h_ready"), 1)
            for j in range(4):
                dense([("qk", j)], [("qkv", j)], hT)
            for half in range(2):
                name = ("qkv", 4 + half)
                wait_slot(pe, name)
                for i, (t0, tn) in enumerate(TILES):
                    bk = group(("v", half, i))
                    for k in range(KC):
                        mm = pe.matmul(bk[0:tn, :], hT[:, k, t0:t0 + tn], slot_of(name)[:, k, :],
                                       start=(k == 0), stop=(k == KC - 1))
                    filled(mm)
                slot_done(name)
            pe.wait_ge(ev("qk_ready"), 1)
            for i, (t0, tn) in enumerate(TILES):
                turn(("k_tok", i), lambda c: qkT[:, KC + c, t0:t0 + tn], tn, 2)
            turn("q_s", lambda c: qkT[:, c, TP:T], NS, 2)
            todo = list(fillers)
            for c in range(KC):
                for hh in range(2):
                    bk = group(("qk_scores", c, hh))
                    r = slice(hh * HD, (hh + 1) * HD)
                    pe.matmul(bk[:, 0:P], qkT[r, c, 0:P], qkT[r, KC + c, 0:P], start=True, stop=True)
                    mm = pe.matmul(bk[:, P:P + TP], qkT[r, c, P:TP], qkT[r, KC + c, 0:TP], start=True, stop=True)
                    filled(mm)
                pe.wait_ge(ev("q_s_ready"), 1)
                for half in range(2):
                    bk = group(("q_all", c, half))
                    filled(pe.matmul(bk[:, :], ident[0:NS, c:c + 1].to_broadcast([NS, P]), q_s[:, half * 512:(half + 1) * 512], start=True, stop=True))
                filler()
                for hh in range(2):
                    pe.wait_ge(ev("probs_ready"), 2 * c + hh + 1)
                    bk = group(("probsT", c, hh))
                    pe.transpose(bk[:, 0:P], P_p[:, hh, 0:P], ident[:, :])
                    pe.transpose(bk[:, P:TP], P_p[:, hh, P:TP], ident[:, :])
                    filled(pe.transpose(bk[:, TP:384], P_p[:, hh, TP:384], ident[:, :]))
                filler()
                pe.wait_ge(ev("probsT_ready"), c + 1)
                bk = group(("attn", c))
                for hh in range(2):
                    r, cols = slice(hh * HD, (hh + 1) * HD), slice((2 * c + hh) * HD, (2 * c + hh + 1) * HD)
                    pe.matmul(bk[r, 0:TP], v_tok[:, 0, cols], PT_p[:, hh, 0:TP], start=True, stop=False)
                    mm = pe.matmul(bk[r, P:TP], v_tok[:, 1, cols], PT_p[:, hh, TP:384], start=False, stop=True)
                filled(mm)
                if c < 4:
                    filler()
            ada_turn()
            pe.wait_ge(ev("sample_scores_ready"), 1)
            bk = group("scores_s")
            for g in range(PAGES):
                mm = pe.transpose(bk[:, g * P:(g + 1) * P], scT[:, g, :], ident[:, :])
            filled(mm)
            pe.wait_ge(ev("self_scores_ready"), 1)
            bk = group("self_s")
            filled(pe.matmul(bk[:, 0:H], e8T[:, :], ss[:, :], start=True, stop=True))
            pe.wait_ge(ev("sample_probs_ready"), 1)
            bk = group("probsT_s")
            for g in range(PAGES):
                mm = pe.transpose(bk[:, g * P:(g + 1) * P], P_s[:, g * P:(g + 1) * P], ident[:, :])
            filled(mm)
            bk = group("PD")
            filled(pe.matmul(bk[0:NS, 0:P], e8[:, :], diag[:, :], start=True, stop=True))
            pe.wait_ge(ev("sample_probsT_ready"), 1)
            for i in range(NS // 2):
                name = ("V", i)
                wait_slot(pe, name)
                V = ring[:, index[name] % RING, :].rearrange("p (n g d) -> p n g d", n=2, g=PAGES)
                bk = group(("pv_s", i))
                for c in range(KC):
                    for n in range(2):
                        o, r = (c * 2 + n) * 2, (2 * i + n) * H + 2 * c
                        for g in range(PAGES):
                            mm = pe.matmul(bk[:, o:o + 2], V[:, n, g, c * P:(c + 1) * P], PT_s[:, g, r:r + 2],
                                           start=(g == 0), stop=(g == PAGES - 1))
                filled(mm)
                slot_done(name)
            bk = group("self_pv")
            for c in range(KC):
                mm = pe.matmul(bk[:, c * 2 * NS:(c + 1) * 2 * NS], v_s[:, c * P:(c + 1) * P],
                               PD[:, :].rearrange("k (n h) -> k n h", h=H)[:, :, 2 * c:2 * c + 2], start=True, stop=True)
            filled(mm)
            pe.wait_ge(ev("attn_ready"), 1)
            for j in range(2):
                dense([("wo", j)], [("wo", j)], attnT)
            norm(0, zT, sq)
            pe.wait_ge(ev("h_ready"), 2)
            for j in range(6):
                n = min(512, FF - 512 * j)
                dense([("f1", j), ("f3", j)], [("f1", j), ("f3", j)], hT, n, n // P)
            pe.wait_ge(ev("g_ready"), 1)
            for cb in range(4):
                two = [group(("f2", cb, m)) for m in range(2)]
                for kh in range(2):
                    name = ("f2", cb, kh)
                    wait_slot(pe, name)
                    w = ring[:, index[name] % RING, 0:11 * 256].rearrange("p (k n) -> p k n", n=256)
                    for m in range(2):
                        for k in range(11):
                            mm = pe.matmul(two[m][:, 0:T], w[:, k, m * P:(m + 1) * P], gT[:, kh * 11 + k, :],
                                           start=(kh == 0 and k == 0), stop=(kh == 1 and k == 10))
                        if kh == 1:
                            filled(mm)
                    slot_done(name)
            norm(1, zT, sq)
            pe.wait_ge(ev("state_loaded"), 32)
            pe.wait_ge(ev("ln_done"), 2)
            for k in range(KC):
                bk = group(("stT", k))
                for i in range(2):
                    mm = pe.transpose(bk[:, i * 120:(i + 1) * 120], st_rows[0:120, i, k * P:(k + 1) * P], ident[0:120, 0:120])
                filled(mm)
            pe.wait_ge(ev("h_ready"), 3)
            for j in range(2):
                dense([("p1", j), ("p1g", j)], [("p1", j), ("p1g", j)], hT)
            pe.wait_ge(ev("u_ready"), 1)
            turn("u_p", lambda c: up[:, c, TP:TP + CW - 1], CW - 1, 2)
            turn("u_s", lambda c: us[:, c, :, CW - 1], NS, 2)
            norm(2, ydw, sq)
            pe.wait_ge(ev("conv_ready"), KC)
            for j in range(2):
                dense([("p2", j)], [("p2", j)], ydw)
            norm(3, zT, sq)
            pe.wait_ge(ev("h_ready"), 4)
            pe.wait_ge(ev("router_loaded"), 32)
            bk = group("logits")
            for i, (t0, tn) in enumerate(TILES):
                pe.matmul(bk[0:tn, 8 * i:8 * i + 8], ones[0:1, 0:tn], br[:, :], start=True, stop=False)
                for k in range(KC):
                    mm = pe.matmul(bk[0:tn, 8 * i:8 * i + 8], hT[:, k, t0:t0 + tn], wr[:, k, :], start=False, stop=(k == KC - 1))
            filled(mm)
            for i, (t0, tn) in enumerate(TILES):
                turn(("h_tok", i), lambda c: hT[:, c, t0:t0 + tn], tn, 2)
            pe.wait_ge(ev("selected_ready"), 1)
            bk = group("ranks")
            for i, (t0, tn) in enumerate(TILES):
                for b in range(i):
                    pe.matmul(bk[0:tn, 8 * i:8 * i + 8], ones[:, 0:tn], sel[:, b, :], start=(b == 0), stop=False)
                mm = pe.matmul(bk[0:tn, 8 * i:8 * i + 8], before[0:tn, 0:tn], sel[0:tn, i, :], start=(i == 0), stop=True)
            for i, (t0, tn) in enumerate(TILES):
                mm = pe.matmul(bk[:, 24:32], ones[0:tn, :], sel[0:tn, i, :], start=(i == 0), stop=(i == 2))
            filled(mm)

            h1 = [banks[:, 0, :], banks[:, 2, :]]
            h3 = [banks[:, 1, :], banks[:, 3, :]]
            out_b = banks[:, 4:6, :].rearrange("p b n -> p (b n)")
            gT_b = banks[:, 6, :]
            gs_b = banks[:, 7, :]
            xT_b = banks[:, 2:4, :].rearrange("p b n -> p (b n)")

            def gather():
                for k in range(KC):
                    for i, (t0, tn) in enumerate(TILES):
                        mm = pe.matmul(xT_b[:, k * P:(k + 1) * P], h_tok[0:tn, i, k * P:(k + 1) * P], sel_t[0:tn, i, :],
                                       start=(i == 0), stop=(i == 2))
                mm.then_inc(ev("moe_x_filled"), 1)

            pe.wait_ge(psum_drained, len(order))
            pe.wait_ge(ev("moe_sel_ready"), 1)
            gather()
            pe.sem_inc(ev("moe_units_used"), SPLITS)

            def expert(w):
                pe.wait_ge(ev("moe_x_lo_ready"), w + 1)
                for s, (kind, j) in enumerate(EXPERT_SLOTS):
                    for u in range(UNITS):
                        n = s * UNITS + u
                        pe.wait_ge(ev("moe_lo_ready"), EU * w + n + 1)
                        hi, lo = w_hi[:, n % SPLITS, :], w_lo[:, n % SPLITS, :]
                        if kind == "w2":
                            if u == 0:
                                pe.wait_ge(ev("moe_g_lo_ready"), EJ * w + j + 1)
                            if u == 0 and j == 0:
                                pe.wait_ge(ev("moe_out_kept"), w + 1)
                            a = slice(u * P, (u + 1) * P)
                            for half in range(2):
                                b = slice(half * 512, (half + 1) * 512)
                                for k, (x, y) in enumerate(((g_hi, hi), (g_hi, lo), (g_lo, hi))):
                                    mm = pe.matmul(out_b[:, b], x[:, j % 2, a], y[:, b], start=(j == 0 and u == 0 and k == 0),
                                                   stop=(j == EJ - 1 and u == UNITS - 1 and k == 2))
                        else:
                            bk = (h1 if kind == "w1" else h3)[j % 2]
                            if u == 0 and kind == "w1" and j >= 2:
                                pe.wait_ge(ev("moe_g_ready"), EJ * w + j - 1)
                            for kk in range(2):
                                a = slice((2 * u + kk) * P, (2 * u + kk + 1) * P)
                                b = slice(kk * 512, (kk + 1) * 512)
                                for k, (x, y) in enumerate(((x_hi, hi), (x_hi, lo), (x_lo, hi))):
                                    mm = pe.matmul(bk[:, :], x[:, a], y[:, b], start=(u == 0 and kk == 0 and k == 0),
                                                   stop=(u == 3 and kk == 1 and k == 2))
                        mm.then_inc(ev("moe_units_used"), 1)
                        if n == 12:
                            pe.wait_ge(ev("moe_gsel_ready"), w + 2)
                            for i, (t0, tn) in enumerate(TILES):
                                mm = pe.transpose(gs_b[:, t0:t0 + tn], gsel_t[0:tn, i, :], ident[0:tn, 0:tn])
                            mm.then_inc(ev("moe_gs_filled"), 1)
                        for jj in range(EJ):
                            if n == last_unit("w3", jj) + TURN:
                                pe.wait_ge(ev("moe_g_ready"), EJ * w + jj + 1)
                                if jj == 0:
                                    pe.wait_ge(ev("moe_y_added"), KC * w + 1)
                                for i in range(4):
                                    mm = pe.transpose(gT_b[:, i * P:(i + 1) * P], g_tok[:, i * P:(i + 1) * P], ident[:, :])
                                mm.then_inc(ev("moe_gT_filled"), 1)
                pe.wait_ge(ev("moe_sel_ready"), w + 2)
                gather()
                pe.wait_ge(ev("moe_out_kept"), w + 2)
                pe.wait_ge(ev("moe_gs_kept"), w + 1)
                for k in range(KC):
                    if k >= 2:
                        pe.wait_ge(ev("moe_y_added"), KC * w + k)
                    bk = (gT_b, gs_b)[k % 2]
                    pe.matmul(bk[:, 0:T], out_sb[:, k * P:(k + 1) * P], gs[:, :], start=True, stop=True)\
                      .then_inc(ev("moe_y_filled"), 1)

            passes(pe, expert)
            norm(4, zT, hT)
            pe.wait_ge(ev("y_ready"), 1)
            for i, (t0, tn) in enumerate(TILES):
                turn(("y", i), lambda c: xT[:, c, t0:t0 + tn], tn, 2)


        @block_.scalar
        def _(act):
            def see(name):
                n = where[name]
                act.wait_ge(psum_filled, n + 1)
                return banks[:, n % NBANK, :]

            def free(name):
                act.wait_ge(psum_drained, where[name] + 1)

            def norm(i, z, s):
                act.wait_ge(ev("ln_centered"), i + 1)
                act.activation(s, z, ACT.Square).then_inc(ev("ln_squares_ready"), 1)
                bk = see(("var", i))
                act.activation(std[:, :], bk[:, 0:T], ACT.Sqrt, bias=eps_t[:, 0:1]).then_inc(ev("ln_std_ready"), 1)

            act.wait_ge(ev("c_loaded"), 32)
            act.activation(c_rows, c_rows, ACT.Silu).then_inc(ev("silu_c_ready"), 1)
            for c in range(KC):
                for hh in range(2):
                    act.wait_ge(ev("scores_ready"), 2 * c + hh + 1)
                    for i, cols in enumerate((slice(0, P), slice(P, 384))):
                        k = 2 * hh + i
                        last = act.activation(P_p[:, hh, cols], S_p[:, hh, cols], ACT.Exp, bias=st_p[:, 4 + k:5 + k],
                                              scale=0.125, accum_out=st_p[:, 8 + k:9 + k])
                        last.then_inc(ev("exps_ready"), 1)
            act.wait_ge(ev("sample_max_ready"), 1)
            act.activation(P_s, S_s, ACT.Exp, bias=s_self[:, 3:4], scale=0.125,
                           accum_out=s_self[:, 4:5]).then_inc(ev("sample_exps_ready"), 1)
            act.activation(s_self[:, 5:6], s_self[:, 0:1], ACT.Exp, bias=s_self[:, 3:4],
                           scale=0.125).then_inc(ev("sample_exps_ready"), 1)
            norm(0, zT[:, :, :], sq)
            act.wait_ge(ev("kv_stored"), 64)
            for m in range(FM):
                if m >= 2:
                    free((("f3", (m - 2) // 4), (m - 2) % 4))
                bk = see((("f1", m // 4), m % 4))
                act.activation(sg[:, m % 2, :], bk[:, 0:T], ACT.Silu).then_inc(ev("silu_ready"), 1)
            norm(1, zT[:, :, :], sq)
            for m in range(KC):
                if m >= 2:
                    free((("p1g", (m - 2) // 4), (m - 2) % 4))
                bk = see((("p1g", m // 4), m % 4))
                act.activation(sgc[:, m % 2, :], bk[:, 0:T], ACT.Sigmoid,
                               bias=prm[:, PRM_PW1 + KC + m:PRM_PW1 + KC + m + 1]).then_inc(ev("sigmoid_ready"), 1)
            norm(2, ydw, sq)
            act.wait_ge(ev("conv_normed"), 1)
            for c in range(KC):
                act.activation(ydw[:, c, :], ydw[:, c, :], ACT.Silu, scale=prm[:, PRM_CLG + c:PRM_CLG + c + 1],
                               bias=prm[:, PRM_CLB + c:PRM_CLB + c + 1]).then_inc(ev("conv_ready"), 1)
            norm(3, zT[:, :, :], sq)
            act.wait_ge(ev("top_ready"), 1)
            act.activation(edif[:, :], dif[:, :], ACT.Exp).then_inc(ev("gate_exps_ready"), 1)

            out_b = banks[:, 4:6, :].rearrange("p b n -> p (b n)")
            xT_b = banks[:, 2:4, :].rearrange("p b n -> p (b n)")

            def gathered(n):
                act.wait_ge(ev("moe_x_filled"), n)
                act.copy(x_hi[:, :], xT_b).then_inc(ev("moe_x_hi_ready"), 1)

            act.wait_ge(ev("u_stored"), 32)
            act.sem_inc(ev("moe_out_kept"), 1)
            gathered(1)

            def expert(w):
                def unit_used(n):
                    act.wait_ge(ev("moe_units_used"), EU * w + SPLITS + n + 1)

                for n in range(EU):
                    s = n // UNITS
                    if n % UNITS == 0:
                        act.wait_ge(slot_sem[pos_of(s)], w * (16 * ES // RING) + moe_loaded(s))
                    act.wait_ge(ev("moe_units_used"), EU * w + n + 1)
                    o = (n % UNITS) * UW
                    act.copy(w_hi[:, n % SPLITS, :], ring[:, pos_of(s), o:o + UW]).then_inc(ev("moe_hi_ready"), 1)
                    for j in range(EJ):
                        if n == last_unit("w1", j) + SPLITS - 1:
                            unit_used(last_unit("w1", j))
                            act.activation(g_tok[:, :], banks[:, 2 * (j % 2), :], ACT.Silu)\
                               .then_inc(ev("moe_silu_ready"), 1)
                        if n == last_unit("w3", j) + TURN + SPLITS - 1:
                            act.wait_ge(ev("moe_gT_filled"), EJ * w + j + 1)
                            act.copy(g_hi[:, j % 2, :], banks[:, 6, :]).then_inc(ev("moe_g_hi_ready"), 1)
                unit_used(EU - 1)
                act.copy(out_sb, out_b).then_inc(ev("moe_out_kept"), 1)
                gathered(w + 2)

            passes(act, expert)
            norm(4, zT[:, :, :], hT[:, :, :])

        @block_.vector
        def _(dve):
            step = Steps(dve, ev("vector_step"))
            settle, announce = step.settle, step.announce
            taken = [0]

            def take(name):
                n = taken[0]
                assert order[n] == name, (order[n], name)
                taken[0] += 1
                dve.wait_ge(psum_filled, n + 1)
                return banks[:, n % NBANK, :]

            def drained(ins, by=1):
                step(ins, psum_drained, by)

            def ada_row(layer, j):
                bk = take(("ada", layer, j))
                drained(dve.tensor_copy(arow[0:9, (layer * 12 + j) % 2, :], bk[0:9, :]))
                announce("ada_row_kept")
                pending.append((layer, j))

            def ada_turn():
                layer, j = pending.pop(0)
                bk = take(("adaT", layer, j))
                plus = 1.0 if (4 * j // KC) % 3 else 0.0
                bias = prm[:, layer * 48 + 4 * j:layer * 48 + 4 * j + 4].unsqueeze(2).to_broadcast([P, 4, 9])
                drained(dve.scalar_tensor_tensor(adaT[:, layer, 4 * j:4 * j + 4, :], bk[:, 0:36].rearrange("p (m n) -> p m n", n=9),
                                                 plus, bias, ALU.add, ALU.add))

            def filler():
                layer, j = todo.pop(0)
                ada_row(layer, j)
                if len(pending) > 1:
                    ada_turn()

            def col(layer, k, c):
                return adaT[:, layer, k * KC + c, 0:1]

            def cols_s(layer, k):
                return adaT[:, layer, k * KC:(k + 1) * KC, 1:9]

            def modulate(layer, k):
                settle()
                for c in range(KC):
                    step(dve.tensor_scalar(hT[:, c, 0:TP], xT[:, c, 0:TP], col(layer, k + 1, c), col(layer, k, c),
                                           ALU.mult, ALU.add))
                step(dve.tensor_tensor(t8[:, :, :], xT[:, :, TP:T], cols_s(layer, k + 1), ALU.mult))
                settle()
                step(dve.tensor_tensor(hT[:, :, TP:T], t8[:, :, :], cols_s(layer, k), ALU.add))
                announce("h_ready")

            def residual_start():
                settle()
                step(dve.tensor_scalar(zT[:, :, :], xT[:, :, :], ALPHA, None, ALU.mult))
                settle()

            def residual_chunk(layer, k, c, src, done):
                step(dve.scalar_tensor_tensor(zT[:, c, 0:TP], src[:, 0:TP], col(layer, k, c), zT[:, c, 0:TP], ALU.mult, ALU.add))
                done(dve.tensor_tensor(t8[:, c, :], src[:, TP:T], adaT[:, layer, k * KC + c, 1:9], ALU.mult))

            def residual_end():
                settle()
                step(dve.tensor_tensor(zT[:, :, TP:T], zT[:, :, TP:T], t8[:, :, :], ALU.add))
                announce("ln_input_ready")

            def norm(i, z, g, b, out):
                bk = take(("mean", i))
                drained(dve.tensor_tensor(z, z, bk[:, 0:T].unsqueeze(1).to_broadcast([P, KC, T]), ALU.subtract))
                announce("ln_centered")
                take(("var", i))
                dve.wait_ge(ev("ln_std_ready"), i + 1)
                drained(dve.reciprocal(rstd[:, :], std[:, :]))
                settle()
                step(dve.tensor_tensor(z, z, rstd[:, :].unsqueeze(1).to_broadcast([P, KC, T]), ALU.mult))
                settle()
                if out is not None:
                    for c in range(KC):
                        step(dve.tensor_scalar(out[:, c, :], z[:, c, :], prm[:, g + c:g + c + 1], prm[:, b + c:b + c + 1],
                                               ALU.mult, ALU.add))
                announce("ln_done")

            dve.wait_ge(ev("constants_ready"), 1)
            bk = take("prm")
            step(dve.tensor_copy(prm[:, 0:208], bk[:, 0:208]))
            drained(dve.tensor_copy(prm[:, 256:504], bk[:, 256:504]))
            step(dve.tensor_tensor(t16, e16, slope8, ALU.mult))
            settle()
            step(dve.tensor_reduce(slope8_c, t16, AX.X, ALU.add))
            bk = take("cT")
            drained(dve.tensor_copy(cT, bk[:, 0:72].rearrange("p (c n) -> p c n", n=9)))
            announce("cT_ready")
            for k in range(KC):
                bk = take(("xT", k))
                drained(dve.tensor_copy(xT[:, k, :], bk[:, 0:T]))
            pending = []
            for j in range(4):
                ada_row(0, j)
                if len(pending) > 1:
                    ada_turn()
            ada_turn()
            modulate(0, 0)
            for j in range(4):
                for m in range(4):
                    bk = take((("qk", j), m))
                    drained(dve.tensor_copy(qkT[:, 4 * j + m, :], bk[:, 0:T]))
            announce("qk_ready")
            for half in range(2):
                for i, (t0, tn) in enumerate(TILES):
                    bk = take(("v", half, i))
                    dst = v_tok[:, i, half * 512:(half + 1) * 512] if i < 2 else v_s[:, half * 512:(half + 1) * 512]
                    drained(dve.tensor_copy(dst, bk[0:tn, :]))
            announce("v_ready")
            for i, (t0, tn) in enumerate(TILES):
                for half in range(2):
                    bk = take((("k_tok", i), half))
                    cols = slice(half * 512, (half + 1) * 512)
                    drained(dve.tensor_copy(kx_tok[:, i, cols] if i < 2 else kx_s[0:NS, cols], bk[0:tn, :]))
            announce("k_ready")
            for half in range(2):
                bk = take(("q_s", half))
                drained(dve.tensor_copy(q_s[:, half * 512:(half + 1) * 512], bk[0:NS, :]))
            announce("q_s_ready")
            todo = list(fillers)
            for c in range(KC):
                for hh in range(2):
                    bk = take(("qk_scores", c, hh))
                    slope = 2.0 ** (-8.0 * (2 * c + hh + 1) / H)
                    drained(dve.scalar_tensor_tensor(S_p[:, hh, :], dist_p, 8.0 * slope, bk[:, 0:384], ALU.mult, ALU.add))
                    settle()
                    for i, cols in enumerate((slice(0, P), slice(P, 384))):
                        k = 2 * hh + i
                        step(dve.tensor_reduce(st_p[:, k:k + 1], S_p[:, hh, cols], AX.X, ALU.max))
                    settle()
                    step(dve.tensor_scalar(st_p[:, 4 + 2 * hh:6 + 2 * hh], st_p[:, 2 * hh:2 * hh + 2], -0.125, None, ALU.mult))
                    announce("scores_ready")
                name = ("K", c // 2)
                wait_slot(dve, name)
                K = ring[:, index[name] % RING, :].rearrange("p (n g d) -> p n g d", n=2, g=PAGES)
                for half in range(2):
                    bk = take(("q_all", c, half))
                    drained(dve.tensor_tensor(prod, K[:, c % 2, :, half * 512:(half + 1) * 512],
                                              bk.unsqueeze(1).to_broadcast([P, PAGES, 512]), ALU.mult))
                    settle()
                    r = c * H + half * 8
                    ins = dve.tensor_reduce(scT[:, :, r:r + 8], prod.rearrange("p g (h d) -> p g h d", d=HD), AX.X, ALU.add)
                    step(ins, ev("key_slots_used") if c % 2 and half else None)
                    settle()
                for hh in range(2):
                    dve.wait_ge(ev("exps_ready"), 4 * c + 2 * hh + 2)
                    step(dve.reciprocal(st_p[:, 12 + 2 * hh:14 + 2 * hh], st_p[:, 8 + 2 * hh:10 + 2 * hh]))
                    settle()
                    for i, cols in enumerate((slice(0, P), slice(P, 384))):
                        k = 12 + 2 * hh + i
                        step(dve.tensor_scalar(P_p[:, hh, cols], P_p[:, hh, cols], st_p[:, k:k + 1], None, ALU.mult))
                    announce("probs_ready")
                filler()
                for hh in range(2):
                    bk = take(("probsT", c, hh))
                    drained(dve.tensor_copy(PT_p[:, hh, :], bk[:, 0:384]))
                announce("probsT_ready")
                filler()
                bk = take(("attn", c))
                drained(dve.tensor_copy(attnT[:, c, 0:TP], bk[:, 0:TP]))
                if c < 4:
                    filler()
            ada_turn()
            settle()
            prod8 = zflat[0:NS, D:2 * D]
            dve.sem_inc(ev("sample_scores_ready"), 1)
            step(dve.tensor_tensor(prod8, q_s, kx_s[0:NS, :], ALU.mult))
            settle()
            step(dve.tensor_reduce(ss, prod8.rearrange("n (h d) -> n h d", d=HD), AX.X, ALU.add))
            announce("self_scores_ready")
            bk = take("scores_s")
            drained(dve.scalar_tensor_tensor(S_s, dist_s, slope8_c, bk[:, 0:PAST], ALU.mult, ALU.add))
            bk = take("self_s")
            drained(dve.tensor_tensor(t16, bk[:, 0:H], e16, ALU.mult))
            settle()
            step(dve.tensor_reduce(s_self[:, 0:1], t16, AX.X, ALU.add))
            step(dve.tensor_reduce(s_self[:, 1:2], S_s, AX.X, ALU.max))
            settle()
            step(dve.tensor_tensor(s_self[:, 2:3], s_self[:, 0:1], s_self[:, 1:2], ALU.max))
            settle()
            step(dve.tensor_scalar(s_self[:, 3:4], s_self[:, 2:3], -0.125, None, ALU.mult))
            announce("sample_max_ready")
            dve.wait_ge(ev("sample_exps_ready"), 2)
            step(dve.tensor_tensor(s_self[:, 6:7], s_self[:, 4:5], s_self[:, 5:6], ALU.add))
            settle()
            step(dve.reciprocal(s_self[:, 7:8], s_self[:, 6:7]))
            settle()
            step(dve.tensor_scalar(P_s, P_s, s_self[:, 7:8], None, ALU.mult))
            step(dve.tensor_tensor(s_self[:, 2:3], s_self[:, 5:6], s_self[:, 7:8], ALU.mult))
            settle()
            step(dve.tensor_scalar(diag, ident[:, :], s_self[:, 2:3], None, ALU.mult))
            announce("sample_probs_ready")
            bk = take("probsT_s")
            drained(dve.tensor_copy(PT_s, bk[:, 0:PAST].rearrange("p (g r) -> p g r", g=2)))
            bk = take("PD")
            drained(dve.tensor_copy(PD, bk[0:NS, 0:P]))
            announce("sample_probsT_ready")
            pv = pv_s.rearrange("p (c n r) -> p c n r", c=KC, n=NS)
            for i in range(NS // 2):
                bk = take(("pv_s", i))
                drained(dve.tensor_copy(pv[:, :, 2 * i:2 * i + 2, :].rearrange("p c n r -> p c (n r)"),
                                        bk[:, 0:32].rearrange("p (c m) -> p c m", c=KC)))
            bk = take("self_pv")
            settle()
            drained(dve.tensor_tensor(pv_s, pv_s, bk[:, 0:P], ALU.add))
            settle()
            for r in range(2):
                step(dve.tensor_copy(attnT[r * HD:(r + 1) * HD, :, TP:T], pv[r * HD:(r + 1) * HD, :, :, r]))
            announce("attn_ready")
            residual_start()
            for c in range(KC):
                residual_chunk(0, 2, c, take((("wo", c // 4), c % 4)), drained)
            residual_end()
            norm(0, zT[:, :, :], PRM_LNG, PRM_LNB, xT)
            modulate(0, 3)
            dve.wait_ge(ev("kv_stored"), 64)
            for m in range(FM):
                take((("f1", m // 4), m % 4))
                bk = take((("f3", m // 4), m % 4))
                dve.wait_ge(ev("silu_ready"), m + 1)
                drained(dve.tensor_tensor(gT[:, m, :], sg[:, m % 2, :], bk[:, 0:T], ALU.mult), 2)
            announce("g_ready")
            residual_start()
            for c in range(KC):
                residual_chunk(0, 5, c, take(("f2", c // 2, c % 2)), drained)
            residual_end()
            norm(1, zT[:, :, :], PRM_LNG + KC, PRM_LNB + KC, xT)
            step(dve.memset(up[:, :, 0:CW - 1], 0.0))
            for k in range(KC):
                bk = take(("stT", k))
                drained(dve.tensor_copy(us[:, k, :, 0:CW - 1], bk[:, 0:240].rearrange("p (n j) -> p n j", n=NS)))
            modulate(1, 0)

            def w_dw(j, c):
                return prm[:, PRM_DW + j * KC + c:PRM_DW + j * KC + c + 1]

            for c in range(KC):
                ba = take((("p1", c // 4), c % 4))
                take((("p1g", c // 4), c % 4))
                dve.wait_ge(ev("sigmoid_ready"), c + 1)
                bias = prm[:, PRM_PW1 + c:PRM_PW1 + c + 1]
                step(dve.scalar_tensor_tensor(up[:, c, CW - 1:CW - 1 + TP], ba[:, 0:TP], bias, sgc[:, c % 2, 0:TP], ALU.add, ALU.mult))
                drained(dve.scalar_tensor_tensor(us[:, c, :, CW - 1], ba[:, TP:T], bias, sgc[:, c % 2, TP:T], ALU.add, ALU.mult), 2)
                settle()
                b_dw = prm[:, PRM_BDW + c:PRM_BDW + c + 1]
                step(dve.tensor_tensor(us_prod, us[:, c, :, :],
                                       prm[:, PRM_DW + c:PRM_DW + c + (CW - 1) * KC + 1:KC].unsqueeze(1).to_broadcast([P, NS, CW]),
                                       ALU.mult))
                step(dve.tensor_scalar(ydw[:, c, 0:TP], up[:, c, 0:TP], w_dw(0, c), b_dw, ALU.mult, ALU.add))
                settle()
                step(dve.tensor_reduce(t8[:, c, :], us_prod, AX.X, ALU.add))
                for j in range(1, CW):
                    step(dve.scalar_tensor_tensor(ydw[:, c, 0:TP], up[:, c, j:j + TP], w_dw(j, c), ydw[:, c, 0:TP], ALU.mult, ALU.add))
                    settle()
                step(dve.tensor_scalar(ydw[:, c, TP:T], t8[:, c, :], b_dw, None, ALU.add))
            announce("u_ready")
            for half in range(2):
                bk = take(("u_p", half))
                drained(dve.tensor_copy(u_p[:, half * 512:(half + 1) * 512], bk[0:CW - 1, :]))
            for half in range(2):
                bk = take(("u_s", half))
                drained(dve.tensor_copy(u_s[:, half * 512:(half + 1) * 512], bk[0:NS, :]))
            announce("u_tok_ready")
            dve.sem_inc(ev("ln_input_ready"), 1)
            norm(2, ydw, None, None, None)
            dve.sem_inc(ev("conv_normed"), 1)
            residual_start()
            for c in range(KC):
                bk = take((("p2", c // 4), c % 4))
                drained(dve.tensor_scalar(tmp_c, bk[:, 0:T], prm[:, PRM_PW2 + c:PRM_PW2 + c + 1], None, ALU.add))
                settle()
                residual_chunk(1, 2, c, tmp_c, step)
                settle()
            residual_end()
            norm(3, zT[:, :, :], PRM_LNG + 2 * KC, PRM_LNB + 2 * KC, xT)
            modulate(1, 3)
            dve.wait_ge(ev("u_stored"), 32)
            step(dve.tensor_scalar(xT[:, :, :], xT[:, :, :], ALPHA, None, ALU.mult))
            step(dve.memset(zT[:, :, :], 0.0), ev("moe_y_added"))
            step(dve.memset(logit[:, :, :], 0.0))
            step(dve.memset(rank_w[:, :, :], -1.0))
            step(dve.memset(gate_w[:, :, :], 0.0))
            settle()
            bk = take("logits")
            for i, (t0, tn) in enumerate(TILES):
                (drained if i == 2 else step)(dve.tensor_copy(logit[0:tn, i, :], bk[0:tn, 8 * i:8 * i + 8]))
            settle()
            for i in range(3):
                step(dve.max(top[:, i, :], logit[:, i, :]))
            settle()
            for i in range(3):
                step(dve.max_index(topi[:, i, :], top[:, i, :], logit[:, i, :]))
            step(dve.tensor_tensor(dif[:, :], top[:, :, 1], top[:, :, 0], ALU.subtract))
            announce("top_ready")
            step(dve.tensor_copy(topf[:, :, :], topi[:, :, 0:2]))
            settle()
            for k in range(2):
                for i in range(3):
                    step(dve.tensor_scalar(oh[:, k, i, :], iota_e[:, :], topf[:, i, k:k + 1], None, ALU.is_equal))
            settle()
            step(dve.tensor_tensor(sel[:, :, :], oh[:, 0, :, :], oh[:, 1, :, :], ALU.add))
            announce("selected_ready")
            dve.wait_ge(ev("gate_exps_ready"), 1)
            step(dve.tensor_scalar(dif[:, :], edif[:, :], 1.0, None, ALU.add))
            settle()
            step(dve.reciprocal(gts[:, :, 0], dif[:, :]))
            settle()
            step(dve.tensor_tensor(gts[:, :, 1], edif[:, :], gts[:, :, 0], ALU.mult))
            settle()
            for i in range(3):
                step(dve.tensor_scalar(gate_w[:, i, 0:NE], oh[:, 0, i, :], gts[:, i, 0:1], None, ALU.mult))
            settle()
            for i in range(3):
                step(dve.scalar_tensor_tensor(gate_w[:, i, 0:NE], oh[:, 1, i, :], gts[:, i, 1:2], gate_w[:, i, 0:NE],
                                              ALU.mult, ALU.add))
            settle()
            for g in range(1, GROUPS):
                step(dve.tensor_copy(gate_w[:, :, g * NE:(g + 1) * NE], gate_w[:, :, 0:NE]))
            for i, (t0, tn) in enumerate(TILES):
                for half in range(2):
                    bk = take((("h_tok", i), half))
                    drained(dve.tensor_copy(h_tok[0:tn, i, half * 512:(half + 1) * 512], bk[0:tn, :]))
            bk = take("ranks")
            for i, (t0, tn) in enumerate(TILES):
                step(dve.scalar_tensor_tensor(rank_w[0:tn, i, 0:NE], bk[0:tn, 8 * i:8 * i + 8], 1.0, sel[0:tn, i, :],
                                              ALU.add, ALU.mult))
            step(dve.memset(scan[:, :, :], 0.0))
            settle()
            for g in range(1, GROUPS):
                (drained if g == GROUPS - 1 else step)(
                    dve.tensor_scalar(more_f[:, (g - 1) * NE:g * NE], bk[:, 24:32], float(P * g), None, ALU.is_gt))
            settle()
            step(dve.tensor_copy(scan[:, 0, MORE:], more_f[:, :]))
            for i, (t0, tn) in enumerate(TILES):
                step(dve.tensor_scalar(rank_w[0:tn, i, 0:NE], rank_w[0:tn, i, 0:NE], -1.0, None, ALU.add))
            settle()
            a = 0
            while 1 << a < MORE:
                step(dve.tensor_tensor(scan[:, 1 - a % 2, MORE:], scan[:, a % 2, MORE:],
                                       scan[:, a % 2, MORE - (1 << a):2 * MORE - (1 << a)], ALU.add))
                settle()
                a += 1
            total = scan[:, a % 2, MORE:]
            step(dve.tensor_scalar(n_items[:, :], total[:, MORE - 1:MORE], float(NE), None, ALU.add))
            step(dve.scalar_tensor_tensor(place[:, :], total, float(NE), more_f[:, :], ALU.add, ALU.mult))
            settle()
            step(dve.tensor_scalar(place[:, :], place[:, :], -1.0, None, ALU.add))
            step(dve.memset(list_f[:, :, :], 0.0))
            settle()
            step(dve.tensor_tensor(at_place[:, :, :], iota_place[:, :].unsqueeze(2).to_broadcast([P, MORE + 1, MORE]),
                                   place[:, :].unsqueeze(1).to_broadcast([P, MORE + 1, MORE]), ALU.is_equal))
            step(dve.tensor_copy(list_f[:, 0, 0:NE], iota_e[:, :]))
            settle()
            for k, value in ((0, below), (1, expert_v)):
                step(dve.tensor_tensor(at_value[:, :, :], at_place[:, :, :],
                                       value[:, :].unsqueeze(1).to_broadcast([P, MORE + 1, MORE]), ALU.mult))
                settle()
                step(dve.tensor_reduce(list_f[:, k, NE:], at_value[:, :, :], AX.X, ALU.add))
                settle()
            step(dve.tensor_scalar(list_f[:, 0, NE:], list_f[:, 0, NE:], float(ITEMS), None, ALU.add))
            settle()
            step(dve.tensor_copy(column_of[:, :], list_f[:, 0, :]))
            step(dve.tensor_copy(expert_of[:, :], list_f[:, 1, :]))
            for g in range(1, GROUPS):
                step(dve.tensor_scalar(rank_w[:, :, g * NE:(g + 1) * NE], rank_w[:, :, 0:NE], float(-P * g), None, ALU.add))
            announce("moe_list_ready")

            xT_b = banks[:, 2:4, :].rearrange("p b n -> p (b n)")
            moe_step = ev("moe_vector_step")

            def select(n, w):
                dve.wait_ge(moe_step, n)
                for i in range(3):
                    last = dve.tensor_scalar(sel_t[:, i, :], iota_slot[:, :], rank_c[:, i:i + 1], None, ALU.is_equal)
                    if i == 2:
                        last.then_inc(ev("moe_sel_ready"), 1)
                    else:
                        last.then_inc(ev("moe_sel_parts"), 1)

            def gathered(n):
                dve.wait_ge(ev("moe_x_hi_ready"), n)
                dve.tensor_tensor(x_lo[:, :], xT_b, x_hi[:, :].bitcast(F32), ALU.subtract).then_inc(ev("moe_x_lo_ready"), 1)

            dve.tensor_copy(rank_c[:, :], rank_w[:, :, 0]).then_inc(moe_step, 1)
            select(1, 0)
            dve.sem_inc(ev("moe_gsel_ready"), 1)
            gathered(1)

            def expert(w):
                for n in range(EU):
                    s, o = n // UNITS, (n % UNITS) * UW
                    dve.wait_ge(ev("moe_hi_ready"), EU * w + n + 1)
                    dve.tensor_tensor(w_lo[:, n % SPLITS, :], ring[:, pos_of(s), o:o + UW],
                                      w_hi[:, n % SPLITS, :].bitcast(F32), ALU.subtract).then_inc(ev("moe_lo_ready"), 1)
                    if n == 4:
                        dve.wait_ge(ev("moe_gsel_ready"), w + 1)
                        dve.wait_ge(ev("moe_gsel_parts"), 2 * w + 2)
                        c = dve.value_load(column_of[0:1, bass.ds(w, 1)], min_val=0, max_val=ITEMS)
                        dve.tensor_copy(gate_c[:, :], gate_w[:, :, bass.ds(c, 1)].rearrange("p i o -> p (i o)")).then_inc(moe_step, 1)
                        dve.wait_ge(moe_step, 2 * w + 2)
                        for i in range(3):
                            last = dve.tensor_scalar(gsel_t[:, i, :], iota_slot[:, :], rank_c[:, i:i + 1], gate_c[:, i:i + 1],
                                                     ALU.is_equal, ALU.mult)
                            last.then_inc(ev("moe_gsel_ready" if i == 2 else "moe_gsel_parts"), 1)
                    if n == 12 + SPLITS - 1:
                        dve.wait_ge(ev("moe_gs_filled"), w + 1)
                        dve.tensor_copy(gs, banks[:, 7, 0:T]).then_inc(ev("moe_gs_kept"), 1)
                    if n == 30:
                        dve.wait_ge(ev("moe_gsel_ready"), w + 2)
                        dve.wait_ge(ev("moe_gsel_parts"), 2 * w + 4)
                        dve.wait_ge(ev("moe_sel_parts"), 2 * w + 2)
                        c = dve.value_load(column_of[0:1, bass.ds(w + 1, 1)], min_val=0, max_val=ITEMS)
                        dve.tensor_copy(rank_c[:, :], rank_w[:, :, bass.ds(c, 1)].rearrange("p i o -> p (i o)")).then_inc(moe_step, 1)
                        select(2 * w + 3, w + 1)
                    for j in range(EJ):
                        if n == last_unit("w3", j) + SPLITS - 1:
                            dve.wait_ge(ev("moe_units_used"), EU * w + SPLITS + last_unit("w3", j) + 1)
                            dve.wait_ge(ev("moe_silu_ready"), EJ * w + j + 1)
                            dve.tensor_tensor(g_tok[:, :], g_tok[:, :], banks[:, 2 * (j % 2) + 1, :], ALU.mult)\
                               .then_inc(ev("moe_g_ready"), 1)
                        if n == last_unit("w3", j) + TURN + SPLITS - 1:
                            dve.wait_ge(ev("moe_g_hi_ready"), EJ * w + j + 1)
                            dve.tensor_tensor(g_lo[:, j % 2, :], banks[:, 6, :], g_hi[:, j % 2, :].bitcast(F32), ALU.subtract)\
                               .then_inc(ev("moe_g_lo_ready"), 1)
                gathered(w + 2)
                for k in range(KC):
                    dve.wait_ge(ev("moe_y_filled"), KC * w + k + 1)
                    if k == 0:
                        dve.wait_ge(ev("moe_y_added"), KC * w + 1)
                    dve.tensor_tensor(zT[:, k, :], zT[:, k, :], banks[:, 6 + k % 2, 0:T], ALU.add)\
                       .then_inc(ev("moe_y_added"), 1)

            dve.sem_inc(ev("moe_gsel_parts"), 2)
            passes(dve, expert)
            dve.drain()
            for c in range(KC):
                step(dve.tensor_tensor(t8[:, c, :], zT[:, c, TP:T], adaT[:, 1, 5 * KC + c, 1:9], ALU.mult))
                step(dve.scalar_tensor_tensor(zT[:, c, 0:TP], zT[:, c, 0:TP], col(1, 5, c), xT[:, c, 0:TP], ALU.mult, ALU.add))
            settle()
            step(dve.tensor_tensor(zT[:, :, TP:T], xT[:, :, TP:T], t8[:, :, :], ALU.add))
            announce("ln_input_ready")
            norm(4, zT[:, :, :], PRM_LNG + 3 * KC, PRM_LNB + 3 * KC, xT)
            dve.sem_inc(ev("y_ready"), 1)
            for i, (t0, tn) in enumerate(TILES):
                for half in range(2):
                    bk = take((("y", i), half))
                    drained(dve.tensor_copy(h_tok[0:tn, i, half * 512:(half + 1) * 512], bk[0:tn, :]))
                announce("y_tok_ready")

        @block_.sync
        def _(sp):
            sp.dma_start(c_rows[0:1, :], c_prompt).then_inc(ev("c_loaded"), 16)
            sp.dma_start(c_rows[1:9, :], c_sample).then_inc(ev("c_loaded"), 16)
            for dst, src in (
                    (rows[0:96, 0, :], ada_b.rearrange("l (r p) -> (l r) p", p=P)),
                    (rows[96:128, 0, :], ln_g.rearrange("l s (c p) -> (l s c) p", p=P)),
                    (rows[0:32, 1, :], ln_b.rearrange("l s (c p) -> (l s c) p", p=P)),
                    (rows[32:48, 1, :], conv_b_pw1.rearrange("l (c p) -> (l c) p", p=P)),
                    (rows[48:56, 1, :], conv_b_dw.rearrange("l (c p) -> (l c) p", p=P)),
                    (rows[56:64, 1, :], conv_ln_g.rearrange("l (c p) -> (l c) p", p=P)),
                    (rows[64:72, 1, :], conv_ln_b.rearrange("l (c p) -> (l c) p", p=P)),
                    (rows[72:80, 1, :], conv_b_pw2.rearrange("l (c p) -> (l c) p", p=P)),
                    (rows[0:128, 2, :], conv_w_dw.rearrange("l j (c p) -> (l j c) p", p=P)[0:128, :]),
                    (rows[0:120, 3, :], conv_w_dw.rearrange("l j (c p) -> (l j c) p", p=P)[128:248, :])):
                sp.dma_start(dst, src).then_inc(ev("params_loaded"), 16)
            sp.dma_start(kx_tok, x_prompt[0].rearrange("(i p) d -> p i d", p=P)).then_inc(ev("x_loaded"), 16)
            sp.dma_start(kx_s[0:NS, :], x_sample[:, 0, :]).then_inc(ev("x_loaded"), 16)
            sp.dma_start(wr[:, :, :], moe_w_router[0].rearrange("(k p) e -> p k e", p=P)).then_inc(ev("router_loaded"), 16)
            sp.dma_start(br[:, :], moe_b_router).then_inc(ev("router_loaded"), 16)

            def ring_free(n):
                if n >= RING:
                    name, _loads, who = stream[n - RING]
                    if who == "dve":
                        sp.wait_ge(ev("key_slots_used"), name[1] + 1)
                    else:
                        sp.wait_ge(psum_filled, used[n - RING])

            for n, (_name, loads, _who) in enumerate(stream):
                ring_free(n)
                for at, width, kn, src, page in loads:
                    if page is None:
                        dst = ring[:, n % RING, at:at + width].rearrange("p (k n) -> p k n", k=kn)
                    else:
                        seq, g = page
                        phys = sp.value_load(page_table[seq:seq + 1, g:g + 1], min_val=0, max_val=src.shape[0] - 1)
                        dst = ring[:, n % RING, at:at + width]
                        src = src[bass.ds(phys, 1)].rearrange("o s h d -> (o s) (h d)")
                    sp.dma_start(dst, src).then_inc(slot_sem[n % RING], 16)

            def expert_load(e, s):
                kind, j = EXPERT_SLOTS[s]
                if kind == "w2":
                    src = moe_w2[0][bass.ds(e, 1), j * 512:(j + 1) * 512, :].rearrange("o (k p) n -> p (o k) n", p=P)
                else:
                    w = moe_w1 if kind == "w1" else moe_w3
                    src = w[0][bass.ds(e, 1), :, j * 512:(j + 1) * 512].rearrange("o (k p) n -> p (o k) n", p=P)
                dst = ring[:, pos_of(s), :].rearrange("p (k n) -> p k n", n=src.shape[-1])
                sp.dma_start(dst, src).then_inc(slot_sem[pos_of(s)], 16)

            def expert(e, w, s):
                sp.wait_ge(ev("moe_lo_ready"), EU * w + UNITS * (s - RING + 1))
                expert_load(e, s)

            for s in range(ES):
                if s < RING:
                    ring_free(NPRE + s)
                    expert_load(0, s)
                else:
                    expert(0, 0, s)
            with sp.Fori(1, NE) as w:
                for s in range(ES):
                    expert(w, w, s)
            sp.wait_ge(ev("moe_list_ready"), 1)
            items = sp.value_load(n_items[0:1, 0:1], min_val=NE, max_val=ITEMS)
            with sp.Fori(NE, ITEMS) as w:
                with sp.If(items > w):
                    e = sp.value_load(expert_of[0:1, bass.ds(w, 1)], min_val=0, max_val=NE - 1)
                    for s in range(ES):
                        expert(e, w, s)
                sp.nop()
            for i, (t0, tn) in enumerate(TILES):
                sp.wait_ge(ev("y_tok_ready"), i + 1)
                dst = y_prompt[0, t0:t0 + tn, :] if i < 2 else y_sample[:, 0, :]
                sp.dma_start(dst, h_tok[0:tn, i, :]).then_inc(ev("y_stored"), 16)
            sp.wait_ge(ev("y_stored"), 16 * 3)

        @block_.gpsimd
        def _(pool):
            step = Steps(pool, ev("pool_step"))

            def do(ins):
                step(ins)
                step.settle()

            do(pool.memset(ident[:, :], 0.0))
            do(pool.affine_select(out=ident[:, :], in_=ident[:, :], compare_op=ALU.not_equal, fill=1.0,
                                  base=0, pattern=[[-1, P]], channel_multiplier=1))
            do(pool.memset(ones[:, :], 1.0))
            do(pool.memset(mean_w[:, :], 1.0 / D))
            do(pool.memset(before[:, :], 1.0))
            do(pool.affine_select(out=before[:, :], in_=before[:, :], compare_op=ALU.is_gt, fill=0.0,
                                  base=0, pattern=[[1, P]], channel_multiplier=-1))
            do(pool.iota(iota_slot[:, :], pattern=[[1, P]], base=0, channel_multiplier=0, allow_small_or_imprecise_dtypes=True))
            do(pool.iota(iota_e[:, :], pattern=[[1, NE]], base=0, channel_multiplier=0, allow_small_or_imprecise_dtypes=True))
            do(pool.iota(iota_place[:, :], pattern=[[1, MORE + 1]], base=NE, channel_multiplier=0, allow_small_or_imprecise_dtypes=True))
            do(pool.iota(below[:, :], pattern=[[1, MORE]], base=NE - ITEMS, channel_multiplier=0, allow_small_or_imprecise_dtypes=True))
            do(pool.iota(expert_v[:, :], pattern=[[0, GROUPS - 1], [1, NE]], base=0, channel_multiplier=0, allow_small_or_imprecise_dtypes=True))
            do(pool.memset(eps_t[:, :], EPS))
            for q0, kn, at in ((0, P, 0), (P, TP, P)):
                d = dist_p[:, at:at + kn]
                do(pool.iota(d, pattern=[[1, kn]], base=-q0, channel_multiplier=-1, allow_small_or_imprecise_dtypes=True))
                do(pool.affine_select(out=d, in_=d, compare_op=ALU.is_ge, fill=MASKED, base=q0, pattern=[[-1, kn]],
                                      channel_multiplier=1))
            do(pool.iota(dist_s, pattern=[[1, PAST]], base=-PAST, channel_multiplier=0, allow_small_or_imprecise_dtypes=True))
            do(pool.memset(e16, 0.0))
            for n in range(NS):
                do(pool.affine_select(out=e16, in_=e16, compare_op=ALU.not_equal, fill=1.0, base=-H * n,
                                      pattern=[[-1, H]], channel_multiplier=1))
            for m, pattern, mult in ((e8, [[-H, NS]], 1), (e8T, [[1, P]], -H)):
                do(pool.memset(m, 1.0))
                do(pool.affine_select(out=m, in_=m, compare_op=ALU.is_ge, fill=0.0, base=0, pattern=pattern,
                                      channel_multiplier=mult))
                do(pool.affine_select(out=m, in_=m, compare_op=ALU.is_ge, fill=0.0, base=H - 1,
                                      pattern=[[-pattern[0][0], pattern[0][1]]], channel_multiplier=-mult))
            for h in range(H):
                do(pool.memset(slope8[:, h:h + 1], 8.0 * 2.0 ** (-8.0 * (h + 1) / H)))
            for _i in range(1):
                pool.sem_inc(ev("constants_ready"), 1)

            def store(dst, src, name="kv_stored"):
                pool.dma_start(dst, src).then_inc(ev(name), 16)

            store(nc_sample[0, :, 0:CW - 2, :], state_conv[0, :, 1:CW - 1, :], "state_stored")
            pool.wait_ge(ev("v_ready"), 1)
            store(nv_prompt[0, 0].rearrange("(i p) h d -> p i (h d)", p=P), v_tok)
            store(nv_sample[0, :, 0].rearrange("n h d -> n (h d)"), v_s)
            pool.wait_ge(ev("k_ready"), 1)
            store(nk_prompt[0, 0].rearrange("(i p) h d -> p i (h d)", p=P), kx_tok)
            store(nk_sample[0, :, 0].rearrange("n h d -> n (h d)"), kx_s[0:NS, :])
            pool.wait_ge(ev("ln_done"), 2)
            for i in range(2):
                pool.dma_start(st_rows[0:120, i, :], state_conv[0].rearrange("n j d -> (n j) d")[120 * i:120 * (i + 1), :])\
                    .then_inc(ev("state_loaded"), 16)
            pool.wait_ge(ev("u_tok_ready"), 1)
            store(nc_prompt[0, 0], u_p, "u_stored")
            store(nc_sample[0, :, CW - 2, :], u_s, "u_stored")
            pool.wait_ge(ev("state_stored"), 16)
            pool.wait_ge(ev("kv_stored"), 64)
            pool.wait_ge(ev("u_stored"), 32)


_INS = ['x_prompt', 'x_sample', 'cache_k', 'cache_v', 'state_conv', 'page_table', 'c_prompt', 'c_sample',
        'ada_w', 'ada_b', 'ln_g', 'ln_b', 'attn_w_qkv', 'attn_w_o', 'conv_w_pw1', 'conv_b_pw1', 'conv_w_dw',
        'conv_b_dw', 'conv_ln_g', 'conv_ln_b', 'conv_w_pw2', 'conv_b_pw2', 'ffn_w1', 'ffn_w3', 'ffn_w2',
        'moe_w_router', 'moe_b_router', 'moe_w1', 'moe_w3', 'moe_w2']
_OUTS = [((1, TP, D), 'float32'), ((NS, 1, D), 'float32'),
         ((1, 1, TP, H, HD), 'float32'), ((1, 1, TP, H, HD), 'float32'),
         ((1, NS, 1, H, HD), 'float32'), ((1, NS, 1, H, HD), 'float32'),
         ((1, 1, CW - 1, D), 'float32'), ((1, NS, CW - 1, D), 'float32')]


def kernel(**inputs):
    import numpy as _np
    import concourse.bacc as _bacc
    from concourse import mybir as _mybir
    from concourse.bass_utils import run_bass_kernel_spmd as _run

    nc = _bacc.Bacc("TRN2", target_bir_lowering=False, num_devices=1, dynamic_dma_scratch_size=4096)
    arrays, args = {}, []
    for name in _INS:
        a = _np.ascontiguousarray(inputs[name])
        arrays[f"in_{name}_dram"] = a
        args.append(nc.dram_tensor(f"in_{name}_dram", a.shape, _mybir.dt.from_np(a.dtype), kind="ExternalInput").ap())
    for i, (shape, dtype) in enumerate(_OUTS):
        dt = _mybir.dt.from_np(_np.dtype(dtype))
        args.append(nc.dram_tensor(f"out_{i}_dram", shape, dt, kind="ExternalOutput").ap())
    build(nc, *args)
    r = _run(nc, [arrays], core_ids=[0])
    return tuple(r.results[0][f"out_{i}_dram"] for i in range(len(_OUTS)))
```

```python
from contextlib import ExitStack

import concourse.bass as bass
from concourse import mybir

F32 = mybir.dt.float32
F32R = mybir.dt.float32r
I32 = mybir.dt.int32
U32 = mybir.dt.uint32
ALU = mybir.AluOpType
ACT = mybir.ActivationFunctionType
AX = mybir.AxisListType

P = 128
D = 1024
KC = D // P
TP = 256
NS = 8
T = TP + NS
TILES = ((0, 128), (128, 128), (256, NS))
H, HD = 16, 64
PAST = 256
PAGES = PAST // P
CW = 31
FF = 2816
FM = FF // P
NE = 8
FE = 3584
EJ = FE // 512
GROUPS = 3
ITEMS = GROUPS * NE
MORE = ITEMS - NE
PE_TAPS = 12
ALPHA = float(4.0 ** 0.25)
EPS = 1e-5
MASKED = -1e30

RING = 7
SLOTW = 2048
UNITS = 2
UW = SLOTW // UNITS
SPLITS = 4
AHEAD = SPLITS // UNITS
TURN = 2
NBANK = 6

PRM_LNG, PRM_LNB, PRM_PW1, PRM_BDW, PRM_CLG, PRM_CLB, PRM_PW2, PRM_DW = 96, 128, 160, 176, 184, 192, 200, 256

EXPERT_SLOTS = []
for _j in range(EJ + 1):
    _kinds = (["w1", "w3"] if _j < EJ else []) + (["w2"] if _j else [])
    EXPERT_SLOTS += [(_k, _j - (_k == "w2"), _h) for _k in _kinds for _h in range(2)]
ES = len(EXPERT_SLOTS)
EU = ES * UNITS


def last_unit(kind, j):
    return UNITS * (EXPERT_SLOTS.index((kind, j, 1)) + 1) - 1


def build(nc, x_prompt, x_sample, cache_k, cache_v, state_conv, page_table, c_prompt, c_sample,
          ada_w, ada_b, ln_g, ln_b, attn_w_qkv, attn_w_o, conv_w_pw1, conv_b_pw1, conv_w_dw,
          conv_b_dw, conv_ln_g, conv_ln_b, conv_w_pw2, conv_b_pw2, ffn_w1, ffn_w3, ffn_w2,
          moe_w_router, moe_b_router, moe_w1, moe_w3, moe_w2,
          y_prompt, y_sample, nk_prompt, nv_prompt, nk_sample, nv_sample, nc_prompt, nc_sample):
    ctx = ExitStack()
    with ctx:
        def sb(name, shape, dt=F32, at=ctx):
            return at.enter_context(nc.sbuf_tensor(name, shape, dt))

        sems = {}

        def ev(name):
            if name not in sems:
                sems[name] = ctx.enter_context(nc.semaphore(name))
            return sems[name]

        ring = sb("ring", [P, RING, SLOTW])
        xT = sb("xT", [P, KC, T])
        hT = sb("hT", [P, KC, T])
        h_hi = sb("h_hi", [P, KC, T], F32R)
        h_lo = sb("h_lo", [P, KC, T], F32R)
        w_hi = sb("w_hi", [P, SPLITS, UW], F32R)
        w_lo = sb("w_lo", [P, SPLITS, UW], F32R)
        zT = sb("zT", [P, KC, T])
        prm = sb("prm", [P, 512])
        adaT = sb("adaT", [P, 2, 48, 9])
        ident = sb("ident", [P, P])
        ones = sb("ones", [P, P])
        mean_w = sb("mean_w", [P, P])
        before = sb("before", [P, P])
        iota_slot = sb("iota_slot", [P, P])
        iota_e = sb("iota_e", [P, NE])
        iota_place = sb("iota_place", [P, MORE + 1])
        below = sb("below", [P, MORE])
        expert_v = sb("expert_v", [P, MORE])
        eps_t = sb("eps_t", [P, 1])
        std = sb("std", [P, T])
        rstd = sb("rstd", [P, T])
        t8 = sb("t8", [P, KC, NS])
        wr = sb("wr", [P, KC, NE])
        br = sb("br", [1, NE])
        pages_sb = sb("pages_sb", [1, NS * PAGES], I32)
        arow = sb("arow", [P, 2, 512])
        cT_sb = sb("cT_sb", [P, KC * 32])
        cT = cT_sb[:, :].rearrange("p (c n) -> p c n", n=32)
        fold = sb("fold", [P, 9])[:, :]
        banks = ctx.enter_context(nc.psum_tensor("banks", [P, 8, 512], F32))

        pre = ExitStack()
        arena_w = 14900
        arena = sb("arena", [P, arena_w], at=pre)

        def carve(start):
            at = [start]

            def take(n, parts=P):
                a = at[0]
                at[0] += n
                assert at[0] <= arena_w, at[0]
                return arena[0:parts, a:a + n]
            return take

        A = carve(0)
        qkT = A(2 * KC * T).rearrange("p (c t) -> p c t", t=T)
        v_tok = A(2 * D).rearrange("p (i n) -> p i n", i=2)
        v_s = A(D, NS)
        kx = A(2 * D)
        kx_tok = kx.rearrange("p (i n) -> p i n", i=2)
        kx_s = A(D)
        scT = A(2 * P).rearrange("p (g r) -> p g r", g=2)
        S_p = A(2 * 384).rearrange("p (i n) -> p i n", i=2)
        P_p = A(2 * 384).rearrange("p (i n) -> p i n", i=2)
        pt_flat = A(2 * 384)
        PT_p = pt_flat.rearrange("p (i n) -> p i n", i=2)
        dist_p = A(384)
        dist_s = A(PAST)
        e16 = A(16)
        e8 = A(NS)
        e8T = rstd[0:NS, 0:P]
        slope8 = A(H)
        slope8_c = A(1)
        st_p = A(16)
        ss = A(H, NS)
        t16 = A(H)
        s_self = A(8)
        S_s = S_p[:, 0, 0:PAST]
        diag = S_p[:, 1, 0:P]
        P_s = P_p[:, 0, 0:PAST]
        PT_s = pt_flat[:, 0:PAGES * NS * 32].rearrange("p (g q e r) -> p g q e r", g=PAGES, q=4, e=2)
        PD = std[0:NS, 0:P]
        r_off = 2 * KC * T + 2 * D + D + 2 * D + D + 2 * P + 4 * 384
        rows = arena[:, r_off:r_off + 512].rearrange("p (i n) -> p i n", i=4)
        c_off = 2 * KC * T + 2 * D + D + 2 * D + D + 2 * P
        c_rows = arena[0:9, c_off:c_off + D]
        zflat = zT[:, :, :].rearrange("p c t -> p (c t)")
        q_s = zflat[0:NS, 0:D]
        prod = zflat[:, D:2 * D].rearrange("p (g n) -> p g n", g=2)
        own_pv = zflat[:, 0:D]
        sq = arena[:, 0:KC * T].rearrange("p (c t) -> p c t", t=T)

        B = carve(0)
        sg = B(2 * T).rearrange("p (i t) -> p i t", i=2)
        gm = B(2 * T).rearrange("p (i t) -> p i t", i=2)

        C = carve(0)
        st_rows = C(2 * D).rearrange("p (i n) -> p i n", i=2)
        _ = C(KC * T - 2 * D)
        up = C(KC * (CW - 1 + TP)).rearrange("p (c t) -> p c t", c=KC)
        us = C(KC * NS * CW).rearrange("p (c n j) -> p c n j", c=KC, n=NS)
        ydw = C(KC * T).rearrange("p (c t) -> p c t", t=T)
        sgc = C(2 * T).rearrange("p (i t) -> p i t", i=2)
        us_prod = C(NS * CW).rearrange("p (n j) -> p n j", n=NS)
        tmp_c = C(T)
        dw_diag = C(4 * P).rearrange("p (i n) -> p i n", i=4)
        u_p = C(D, CW - 1)
        u_s = C(D, NS)
        pre.close()

        ffn = ExitStack()
        _below = sb("_below_g", [P, KC * T], at=ffn)
        g_hi_f = sb("g_hi_f", [P, FM, T], F32R, at=ffn)
        g_lo_f = sb("g_lo_f", [P, FM, T], F32R, at=ffn)
        ffn.close()

        moe = ExitStack()
        x_hi = sb("x_hi", [P, KC * P], F32R, at=moe)
        x_lo = sb("x_lo", [P, KC * P], F32R, at=moe)
        g_hi = sb("g_hi", [P, 2, 4 * P], F32R, at=moe)
        g_lo = sb("g_lo", [P, 2, 4 * P], F32R, at=moe)
        g_tok = sb("g_tok", [P, 512], at=moe)
        h_tok = sb("h_tok", [P, 3, D], at=moe)
        logit = sb("logit", [P, 3, NE], at=moe)
        top = sb("top", [P, 3, 8], at=moe)
        topi = sb("topi", [P, 3, 8], U32, at=moe)
        topf = sb("topf", [P, 3, 2], at=moe)
        dif = sb("dif", [P, 3], at=moe)
        edif = sb("edif", [P, 3], at=moe)
        gts = sb("gts", [P, 3, 2], at=moe)
        oh = sb("oh", [P, 2, 3, NE], at=moe)
        sel = sb("sel", [P, 3, NE], at=moe)
        rank_w = sb("rank_w", [P, 3, ITEMS + 1], at=moe)
        gate_w = sb("gate_w", [P, 3, ITEMS + 1], at=moe)
        rank_c = sb("rank_c", [P, 3], at=moe)
        rank_n = sb("rank_n", [P, 3], at=moe)
        gate_c = sb("gate_c", [P, 3], at=moe)
        more_f = sb("more_f", [P, MORE], at=moe)
        scan = sb("scan", [P, 2, 2 * MORE], at=moe)
        place = sb("place", [P, MORE], at=moe)
        at_place = sb("at_place", [P, MORE + 1, MORE], at=moe)
        at_value = sb("at_value", [P, MORE + 1, MORE], at=moe)
        n_items = sb("n_items", [P, 2], I32, at=moe)
        column_of = sb("column_of", [P, ITEMS + 1], I32, at=moe)
        expert_of = sb("expert_of", [P, ITEMS + 1], I32, at=moe)
        list_f = sb("list_f", [P, 2, ITEMS + 1], at=moe)
        hflat = hT[:, :, :].rearrange("p c t -> p (c t)")
        out_sb = hflat[:, 0:D]
        sel_t = hflat[:, D:D + 384].rearrange("p (i n) -> p i n", i=3)
        gsel_t = hflat[:, D + 384:D + 768].rearrange("p (i n) -> p i n", i=3)
        gs = hflat[:, D + 768:D + 768 + T]
        moe.close()

        stream = []
        w_qkv, w_o = attn_w_qkv[0], attn_w_o[0]

        def block(name, w, c0, k0=0, kn=KC, split=True):
            src = w[k0 * P:(k0 + kn) * P, c0:c0 + 256].rearrange("(k p) n -> p k n", p=P)
            stream.append((name, [(0, kn * 256, kn, src, None)], "split" if split else "pe"))

        def ada(layer, j):
            for half in range(2):
                block(("ada", layer, j, half), ada_w[layer], j * 512 + half * 256, split=False)

        def pages(name, cache, n, consumer):
            stream.append((name, [(g * D, D, 1, cache, (n, g)) for g in range(PAGES)], consumer))

        fillers = [(0, j) for j in range(4, 12)] + [(1, j) for j in range(12)]
        filler_at = []
        for c in range(KC):
            filler_at.append((c, 0))
        late = fillers[KC:]
        for j in range(4):
            ada(0, j)
        for j in range(12):
            block(("qkv", j), w_qkv, j * 256)
        for (c, k), (layer, j) in zip(filler_at, fillers):
            if k == 0:
                pages(("K", c), cache_k[0], c, "dve")
            ada(layer, j)
        for n in (*range(0, NS, 2), *range(1, NS, 2)):
            pages(("V", n), cache_v[0], n, "pe")
        for j in range(4):
            block(("wo", j), w_o, j * 256)
        for j in range(FF // 256):
            block(("f1", j), ffn_w1[0], j * 256)
            block(("f3", j), ffn_w3[0], j * 256)
            ada(*late[j])
        ada(*late[-1])
        for cb in range(4):
            for kb in range(3):
                block(("f2", cb, kb), ffn_w2[0], cb * 256, kb * KC, min(KC, FM - kb * KC))
        for j in range(4):
            block(("p1", j), conv_w_pw1[0], j * 256)
            block(("p1g", j), conv_w_pw1[0], D + j * 256)
        for j in range(4):
            block(("p2", j), conv_w_pw2[0], j * 256)
        NPRE = len(stream)
        index = {s[0]: n for n, s in enumerate(stream)}
        loaded = []
        per_pos = [0] * RING
        splits = [s[0] for s in stream if s[2] == "split"]
        split_no = {name: q for q, name in enumerate(splits)}
        used = {}
        freed = {}
        for n, (_n, loads, _who) in enumerate(stream):
            per_pos[n % RING] += 16 * len(loads)
            loaded.append(per_pos[n % RING])
        slot_sem = [ev(f"slot{i}_loaded") for i in range(RING)]

        def pos_of(k):
            return (NPRE + k) % RING

        def moe_loaded(k):
            return per_pos[pos_of(k)] + 16 * (k // RING + 1)

        def slot_of(name, w=256):
            return ring[:, index[name] % RING, :].rearrange("p (k n) -> p k n", n=w)

        def wait_slot(eng, name):
            n = index[name]
            eng.wait_ge(slot_sem[n % RING], loaded[n])

        psum_filled, psum_drained = ev("psum_filled"), ev("psum_drained")
        order = []
        where = {}

        block_ = ctx.enter_context(nc.Block())

        def passes(eng, item):
            item(0, first=True)
            with eng.Fori(1, NE) as w:
                item(w)
            eng.wait_ge(ev("moe_list_ready"), 1)
            items = eng.value_load(n_items[0:1, 0:1], min_val=NE, max_val=ITEMS)
            with eng.Fori(NE, ITEMS) as w:
                with eng.If(items > w):
                    item(w)
                eng.nop()
            return eng.value_load(n_items[0:1, 1:2], min_val=NE - 1, max_val=ITEMS - 1)

        class Steps:

            def __init__(self, eng, sem):
                self.eng, self.sem, self.n, self.open = eng, sem, {}, {}

            def __call__(self, ins, sem=None, by=1):
                sem = self.sem if sem is None else sem
                ins.then_inc(sem, by)
                key = id(sem)
                self.n[key] = self.n.get(key, 0) + by
                self.open[key] = sem

            def add(self, sem, by):
                self.settle()
                self.eng.sem_inc(sem, by)
                self.n[id(sem)] = self.n.get(id(sem), 0) + by

            def reach(self, behind):
                self.eng.wait_ge(self.sem, self.n[id(self.sem)] - behind)

            def settle(self):
                for key, sem in self.open.items():
                    self.eng.wait_ge(sem, self.n[key])
                self.open = {}

            def announce(self, name):
                self.settle()
                self.eng.sem_inc(ev(name), 1)

        @block_.tensor
        def _(pe):
            def group(name):
                n = len(order)
                if n >= NBANK:
                    pe.wait_ge(psum_drained, n - NBANK + 1)
                order.append(name)
                where[name] = n
                return banks[:, n % NBANK, :]

            def filled(ins):
                ins.then_inc(psum_filled, 1)

            def slot_done(name):
                used[index[name]] = (psum_filled, len(order))

            def halves(name, k, m):
                i = (split_no[name] * UNITS + k // 4) % SPLITS
                cols = slice((k % 4) * 256 + m * P, (k % 4) * 256 + (m + 1) * P)
                return w_hi[:, i, cols], w_lo[:, i, cols]

            def wait_split(name):
                pe.wait_ge(ev("w_lo_ready"), UNITS * (split_no[name] + 1))

            def dense(slots, x_hi, x_lo, behind=None):
                for s in slots:
                    wait_split(s)
                    for m in range(2):
                        bk = group((s, m))
                        for k in range(KC):
                            hi, lo = halves(s, k, m)
                            for i, (w, x) in enumerate(((hi, x_hi), (hi, x_lo), (lo, x_hi))):
                                mm = pe.matmul(bk[:, 0:T], w, x[:, k, :], start=(k == 0 and i == 0),
                                               stop=(k == KC - 1 and i == 2))
                        filled(mm)
                        if behind is not None:
                            behind(s, m)
                    freed[split_no[s]] = (psum_filled, len(order))

            pending = []

            def ada_rows(layer, j):
                bk = group(("ada", layer, j))
                for half in range(2):
                    name = ("ada", layer, j, half)
                    wait_slot(pe, name)
                    for k in range(KC):
                        r = slice(32 * (k % 4), 32 * (k % 4) + 32)
                        mm = pe.matmul(bk[r, half * 256:(half + 1) * 256], cT[:, k, :], slot_of(name)[:, k, :],
                                       start=(k < 4), stop=(k >= 4), skip_group_check=True)
                    slot_done(name)
                filled(mm)
                pending.append((layer, j))

            def ada_turn():
                layer, j = pending.pop(0)
                i = layer * 12 + j
                pe.wait_ge(ev("ada_row_kept"), i + 1)
                bk = group(("adaT", layer, j))
                for m in range(4):
                    mm = pe.matmul(bk[:, 9 * m:9 * m + 9], arow[:, i % 2, m * P:(m + 1) * P], fold, start=True, stop=True)
                filled(mm)

            def filler():
                layer, j = todo.pop(0)
                ada_rows(layer, j)
                if len(pending) > 1:
                    ada_turn()

            def turn(name, src, parts, n):
                for half in range(2):
                    bk = group((name, half))
                    for i in range(4):
                        mm = pe.transpose(bk[0:parts, i * P:(i + 1) * P], src(half * 4 + i), ident[:, :])
                    filled(mm)

            def mean_chunk(i, z, c):
                pe.wait_ge(ev("ln_chunk_ready"), KC * i + c + 1)
                mm = pe.matmul(stat[:, 0:T], mean_w[:, :], z[:, c, :], start=(c == 0), stop=(c == KC - 1))
                if c == KC - 1:
                    mm.then_inc(ev("stats_filled"), 1)

            def mean_behind(i, z):
                def behind(s, m):
                    n = behind.n
                    behind.n += 1
                    if n >= 2:
                        mean_chunk(i, z, n - 2)
                behind.n = 0
                return behind

            def norm(i, z, s, rest=(KC - 2, KC - 1)):
                for c in rest:
                    mean_chunk(i, z, c)
                for half in range(2):
                    pe.wait_ge(ev("ln_squares_ready"), 2 * i + half + 1)
                    for c in range(4 * half, 4 * half + 4):
                        mm = pe.matmul(stat2[:, 0:T], mean_w[:, :], s[:, c, :], start=(c == 0), stop=(c == KC - 1))
                mm.then_inc(ev("stats_filled"), 1)

            stat, stat2 = banks[:, 6, :], banks[:, 7, :]
            pe.wait_ge(ev("constants_ready"), 1)
            pe.wait_ge(ev("params_loaded"), 16 * 10)
            bk = group("prm")
            for i, r in enumerate((128, 80, 128, 120)):
                mm = pe.transpose(bk[:, i * P:i * P + r], rows[0:r, i, :], ident[0:r, 0:r])
            filled(mm)
            pe.wait_ge(ev("silu_c_ready"), 1)
            bk = group("cT")
            for k in range(KC):
                mm = pe.transpose(bk[:, 9 * k:9 * k + 9], c_rows[:, k * P:(k + 1) * P], ident[0:9, 0:9])
            filled(mm)
            pe.wait_ge(ev("x_loaded"), 16 * 2)
            for k in range(KC):
                bk = group(("xT", k))
                for i, (t0, tn) in enumerate(TILES):
                    src = kx_tok[:, i, k * P:(k + 1) * P] if i < 2 else kx_s[0:NS, k * P:(k + 1) * P]
                    mm = pe.transpose(bk[:, t0:t0 + tn], src, ident[0:tn, 0:tn])
                filled(mm)
            pe.wait_ge(ev("cT_ready"), 1)
            for j in range(4):
                ada_rows(0, j)
                if len(pending) > 1:
                    ada_turn()
            ada_turn()
            pe.wait_ge(ev("h_ready"), 1)
            dense([("qkv", j) for j in range(12)], h_hi, h_lo)
            pe.wait_ge(ev("qkv_ready"), 1)
            for i, (t0, tn) in enumerate(TILES):
                turn(("v_tok", i), lambda c: zT[:, c, t0:t0 + tn], tn, 2)
            for i, (t0, tn) in enumerate(TILES):
                turn(("k_tok", i), lambda c: qkT[:, KC + c, t0:t0 + tn], tn, 2)
            turn("q_s", lambda c: qkT[:, c, TP:T], NS, 2)
            todo = list(fillers)
            for c in range(KC):
                for hh in range(2):
                    bk = group(("qk_scores", c, hh))
                    r = slice(hh * HD, (hh + 1) * HD)
                    pe.matmul(bk[:, 0:P], qkT[r, c, 0:P], qkT[r, KC + c, 0:P], start=True, stop=True)
                    mm = pe.matmul(bk[:, P:P + TP], qkT[r, c, P:TP], qkT[r, KC + c, 0:TP], start=True, stop=True)
                    filled(mm)
                pe.wait_ge(ev("q_s_ready"), 1)
                for half in range(2):
                    bk = group(("q_all", c, half))
                    filled(pe.matmul(bk[:, :], ident[0:NS, c:c + 1].to_broadcast([NS, P]), q_s[:, half * 512:(half + 1) * 512], start=True, stop=True))
                filler()
                for hh in range(2):
                    pe.wait_ge(ev("probs_ready"), 2 * c + hh + 1)
                    bk = group(("probsT", c, hh))
                    pe.transpose(bk[:, 0:P], P_p[:, hh, 0:P], ident[:, :])
                    pe.transpose(bk[:, P:TP], P_p[:, hh, P:TP], ident[:, :])
                    filled(pe.transpose(bk[:, TP:384], P_p[:, hh, TP:384], ident[:, :]))
                pe.wait_ge(ev("probsT_ready"), c + 1)
                bk = group(("attn", c))
                for hh in range(2):
                    r, cols = slice(hh * HD, (hh + 1) * HD), slice((2 * c + hh) * HD, (2 * c + hh + 1) * HD)
                    pe.matmul(bk[r, 0:TP], v_tok[:, 0, cols], PT_p[:, hh, 0:TP], start=True, stop=False)
                    mm = pe.matmul(bk[r, P:TP], v_tok[:, 1, cols], PT_p[:, hh, TP:384], start=False, stop=True)
                filled(mm)
            ada_turn()
            pe.wait_ge(ev("sample_scores_ready"), 1)
            bk = group("scores_s")
            for g in range(PAGES):
                mm = pe.transpose(bk[:, g * P:(g + 1) * P], scT[:, g, :], ident[:, :])
            filled(mm)
            pe.wait_ge(ev("self_scores_ready"), 1)
            bk = group("self_s")
            filled(pe.matmul(bk[:, 0:H], e8T[:, :], ss[:, :], start=True, stop=True))
            pe.wait_ge(ev("sample_probs_ready"), 1)
            bk = group("probsT_s")
            for g in range(PAGES):
                mm = pe.transpose(bk[:, g * P:(g + 1) * P], P_s[:, g * P:(g + 1) * P], ident[:, :])
            filled(mm)
            bk = group("PD")
            filled(pe.matmul(bk[0:NS, 0:P], e8[:, :], diag[:, :], start=True, stop=True))
            pe.wait_ge(ev("sample_probsT_ready"), 1)
            pv = [group(("pv_s", half)) for half in range(2)]
            for half in range(2):
                pe.matmul(pv[half], PD[:, :], v_s[:, half * 512:(half + 1) * 512], start=True, stop=False, skip_group_check=True)
            for e in range(2):
                for n in range(e, NS, 2):
                    wait_slot(pe, ("V", n))
                for half in range(2):
                    for g in range(PAGES):
                        for q in range(4):
                            V = ring[:, index[("V", 2 * q + e)] % RING, :].rearrange("p (g d) -> p g d", g=PAGES)
                            mm = pe.matmul(pv[half][32 * q:32 * q + 32, :], PT_s[:, g, q, e, :], V[:, g, half * 512:(half + 1) * 512],
                                           start=False, stop=(e == 1 and g == PAGES - 1), skip_group_check=True)
                    if e == 0 and half == 1:
                        mm.then_inc(ev("even_values_used"), 1)
                    elif e == 1:
                        filled(mm)
                for n in range(e, NS, 2):
                    used[index[("V", n)]] = (ev("even_values_used"), 1) if e == 0 else (psum_filled, len(order))
            pe.wait_ge(ev("own_pv_ready"), 1)
            bk = group("attn_s")
            for c in range(KC):
                mm = pe.matmul(bk[:, c * NS:(c + 1) * NS], own_pv[:, c * P:(c + 1) * P], e8, start=True, stop=True)
            filled(mm)
            pe.wait_ge(ev("attn_ready"), 1)
            dense([("wo", j) for j in range(4)], h_hi, h_lo, mean_behind(0, zT))
            norm(0, zT, sq)
            pe.wait_ge(ev("h_ready"), 2)
            for j in range(FF // 256):
                dense([("f1", j), ("f3", j)], h_hi, h_lo)
                filler()
            filler()
            ada_turn()
            pe.wait_ge(ev("g_ready"), 1)
            behind = mean_behind(1, zT)
            for cb in range(4):
                two = [group(("f2", cb, m)) for m in range(2)]
                for kb in range(3):
                    name = ("f2", cb, kb)
                    wait_split(name)
                    for m in range(2):
                        for k in range(min(KC, FM - kb * KC)):
                            hi, lo = halves(name, k, m)
                            g = kb * KC + k
                            for i, (w, x) in enumerate(((hi, g_hi_f), (hi, g_lo_f), (lo, g_hi_f))):
                                mm = pe.matmul(two[m][:, 0:T], w, x[:, g, :], start=(g == 0 and i == 0),
                                               stop=(g == FM - 1 and i == 2))
                        if kb == 2:
                            filled(mm)
                    if kb < 2:
                        mm.then_inc(ev("f2_blocks_used"), 1)
                        freed[split_no[name]] = (ev("f2_blocks_used"), 2 * cb + kb + 1)
                    else:
                        freed[split_no[name]] = (psum_filled, len(order))
                        behind(name, 0)
                        behind(name, 1)
            norm(1, zT, sq)
            pe.wait_ge(ev("state_loaded"), 32)
            for k in range(KC):
                bk = group(("stT", k))
                for i in range(2):
                    mm = pe.transpose(bk[:, i * 120:(i + 1) * 120], st_rows[0:120, i, k * P:(k + 1) * P], ident[0:120, 0:120])
                filled(mm)
            pe.wait_ge(ev("h_ready"), 3)
            def taps(c):
                pe.wait_ge(ev("u_chunk_ready"), c // 2 + 1)
                bk = group(("taps", c))
                for i in range(PE_TAPS):
                    pe.wait_ge(ev("diag_ready"), c * PE_TAPS + i + 1)
                    j = CW - PE_TAPS + i
                    mm = pe.matmul(bk[:, 0:TP], dw_diag[:, (c * PE_TAPS + i) % 4, :], up[:, c, j:j + TP],
                                   start=(i == 0), stop=(i == PE_TAPS - 1))
                    if i < PE_TAPS - 1:
                        mm.then_inc(ev("diag_used"), 1)
                filled(mm)

            for j in range(4):
                dense([("p1", j), ("p1g", j)], h_hi, h_lo)
                taps(2 * j)
                taps(2 * j + 1)
            for c in range(KC - 2):
                mean_chunk(2, ydw, c)
            pe.wait_ge(ev("u_ready"), 1)
            turn("u_p", lambda c: up[:, c, TP:TP + CW - 1], CW - 1, 2)
            turn("u_s", lambda c: us[:, c, :, CW - 1], NS, 2)
            norm(2, ydw, sq)
            pe.wait_ge(ev("conv_ready"), 2)
            dense([("p2", j) for j in range(4)], h_hi, h_lo, mean_behind(3, zT))
            norm(3, zT, sq)
            pe.wait_ge(ev("h_ready"), 4)
            pe.wait_ge(ev("router_loaded"), 32)
            bk = group("logits")
            for i, (t0, tn) in enumerate(TILES):
                pe.matmul(bk[0:tn, 8 * i:8 * i + 8], ones[0:1, 0:tn], br[:, :], start=True, stop=False)
                for k in range(KC):
                    mm = pe.matmul(bk[0:tn, 8 * i:8 * i + 8], hT[:, k, t0:t0 + tn], wr[:, k, :], start=False, stop=(k == KC - 1))
            filled(mm)
            for i, (t0, tn) in enumerate(TILES):
                turn(("h_tok", i), lambda c: hT[:, c, t0:t0 + tn], tn, 2)
            pe.wait_ge(ev("selected_ready"), 1)
            bk = group("ranks")
            for i, (t0, tn) in enumerate(TILES):
                for b in range(i):
                    pe.matmul(bk[0:tn, 8 * i:8 * i + 8], ones[:, 0:tn], sel[:, b, :], start=(b == 0), stop=False)
                mm = pe.matmul(bk[0:tn, 8 * i:8 * i + 8], before[0:tn, 0:tn], sel[0:tn, i, :], start=(i == 0), stop=True)
            for i, (t0, tn) in enumerate(TILES):
                mm = pe.matmul(bk[:, 24:32], ones[0:tn, :], sel[0:tn, i, :], start=(i == 0), stop=(i == 2))
            filled(mm)

            h1 = [banks[:, 0, :], banks[:, 2, :]]
            h3 = [banks[:, 1, :], banks[:, 3, :]]
            out_b = banks[:, 4:6, :].rearrange("p b n -> p (b n)")
            gT_b = banks[:, 6, :]
            gs_b = banks[:, 7, :]
            xT_b = banks[:, 2:4, :].rearrange("p b n -> p (b n)")

            def gather():
                for k in range(KC):
                    for i, (t0, tn) in enumerate(TILES):
                        mm = pe.matmul(xT_b[:, k * P:(k + 1) * P], h_tok[0:tn, i, k * P:(k + 1) * P], sel_t[0:tn, i, :],
                                       start=(i == 0), stop=(i == 2))
                mm.then_inc(ev("moe_x_filled"), 1)

            pe.wait_ge(psum_drained, len(order))
            pe.sem_inc(ev("moe_units_used"), SPLITS)
            pe.wait_ge(ev("moe_sel_ready"), 1)
            gather()

            def expert(w, first=False):
                pe.wait_ge(ev("moe_x_lo_ready"), w + 1)
                for s, (kind, j, part) in enumerate(EXPERT_SLOTS):
                    for u in range(2 * part, 2 * part + UNITS):
                        n = s * UNITS + u % UNITS
                        pe.wait_ge(ev("moe_lo_ready"), EU * w + n + 1)
                        hi, lo = w_hi[:, n % SPLITS, :], w_lo[:, n % SPLITS, :]
                        if kind == "w2":
                            if u == 0:
                                pe.wait_ge(ev("moe_g_lo_ready"), EJ * w + j + 1)
                            if u == 0 and j == 0:
                                pe.wait_ge(ev("moe_out_kept"), w + 1)
                            a = slice(u * P, (u + 1) * P)
                            for half in range(2):
                                b = slice(half * 512, (half + 1) * 512)
                                for k, (x, y) in enumerate(((g_hi, hi), (g_hi, lo), (g_lo, hi))):
                                    mm = pe.matmul(out_b[:, b], x[:, j % 2, a], y[:, b], start=(j == 0 and u == 0 and k == 0),
                                                   stop=(j == EJ - 1 and u == 3 and k == 2))
                        else:
                            bk = (h1 if kind == "w1" else h3)[j % 2]
                            if u == 0 and kind == "w1" and j >= 2:
                                pe.wait_ge(ev("moe_g_ready"), EJ * w + j - 1)
                            for kk in range(2):
                                a = slice((2 * u + kk) * P, (2 * u + kk + 1) * P)
                                b = slice(kk * 512, (kk + 1) * 512)
                                for k, (x, y) in enumerate(((x_hi, hi), (x_hi, lo), (x_lo, hi))):
                                    mm = pe.matmul(bk[:, :], x[:, a], y[:, b], start=(u == 0 and kk == 0 and k == 0),
                                                   stop=(u == 3 and kk == 1 and k == 2))
                        mm.then_inc(ev("moe_units_used"), 1)
                        if n == 12:
                            pe.wait_ge(ev("moe_gsel_ready"), w + 2)
                            for i, (t0, tn) in enumerate(TILES):
                                mm = pe.transpose(gs_b[:, t0:t0 + tn], gsel_t[0:tn, i, :], ident[0:tn, 0:tn])
                            mm.then_inc(ev("moe_gs_filled"), 1)
                        for jj in range(EJ):
                            if n == last_unit("w3", jj) + TURN:
                                pe.wait_ge(ev("moe_g_ready"), EJ * w + jj + 1)
                                if jj == 0:
                                    pe.wait_ge(ev("moe_y_added"), KC * w + 1)
                                for i in range(4):
                                    mm = pe.transpose(gT_b[:, i * P:(i + 1) * P], g_tok[:, i * P:(i + 1) * P], ident[:, :])
                                mm.then_inc(ev("moe_gT_filled"), 1)
                pe.wait_ge(ev("moe_sel_ready"), w + 2)
                gather()
                pe.wait_ge(ev("moe_out_kept"), w + 2)
                pe.wait_ge(ev("moe_gs_kept"), w + 1)
                for k in range(KC):
                    if k >= 2:
                        pe.wait_ge(ev("moe_y_added"), KC * w + k)
                    bk = (gT_b, gs_b)[k % 2]
                    pe.matmul(bk[:, 0:T], out_sb[:, k * P:(k + 1) * P], gs[:, :], start=True, stop=True)\
                      .then_inc(ev("moe_y_filled"), 1)

            passes(pe, expert)
            norm(4, zT, hT, range(KC))
            pe.wait_ge(ev("y_ready"), 1)
            for i, (t0, tn) in enumerate(TILES):
                turn(("y", i), lambda c: xT[:, c, t0:t0 + tn], tn, 2)


        @block_.scalar
        def _(act):
            def see(name):
                n = where[name]
                act.wait_ge(psum_filled, n + 1)
                return banks[:, n % NBANK, :]

            def free(name):
                act.wait_ge(psum_drained, where[name] + 1)

            def norm(i, z, s):
                for half in range(2):
                    c = slice(4 * half, 4 * half + 4)
                    act.wait_ge(ev("ln_centered"), 2 * i + half + 1)
                    act.activation(s[:, c, :], z[:, c, :], ACT.Square).then_inc(ev("ln_squares_ready"), 1)
                act.wait_ge(ev("stats_filled"), 2 * i + 2)
                act.activation(std[:, :], banks[:, 7, 0:T], ACT.Sqrt, bias=eps_t[:, 0:1]).then_inc(ev("ln_std_ready"), 1)

            def split(name):
                q, n = split_no[name], index[name]
                wait_slot(act, name)
                if q >= AHEAD:
                    act.wait_ge(*freed[q - AHEAD])
                size = stream[n][1][0][1]
                for u in range(UNITS):
                    o, e = u * UW, min((u + 1) * UW, size)
                    act.copy(w_hi[:, (q * UNITS + u) % SPLITS, 0:e - o], ring[:, n % RING, o:e]).then_inc(ev("w_hi_ready"), 1)

            def split_behind(name):
                q = split_no[name] + AHEAD
                if q < len(splits) and not (name[0] == "qkv" and splits[q][0] == "wo"):
                    split(splits[q])

            def operand(i):
                for half in range(2):
                    c = slice(4 * half, 4 * half + 4)
                    act.wait_ge(ev("h_part_ready"), 2 * i + half + 1)
                    act.copy(h_hi[:, c, :], hT[:, c, :]).then_inc(ev("h_hi_ready"), 1)

            act.wait_ge(ev("c_loaded"), 32)
            act.activation(c_rows, c_rows, ACT.Silu).then_inc(ev("silu_c_ready"), 1)
            split(("qkv", 0))
            split(("qkv", 1))
            operand(0)
            for j in range(12):
                split_behind(("qkv", j))
            for c in range(KC):
                for hh in range(2):
                    act.wait_ge(ev("scores_ready"), 2 * c + hh + 1)
                    for i, cols in enumerate((slice(0, P), slice(P, 384))):
                        k = 2 * hh + i
                        last = act.activation(P_p[:, hh, cols], S_p[:, hh, cols], ACT.Exp, bias=st_p[:, 4 + k:5 + k],
                                              scale=0.125, accum_out=st_p[:, 8 + k:9 + k])
                        last.then_inc(ev("exps_ready"), 1)
            act.wait_ge(ev("sample_max_ready"), 1)
            act.activation(P_s, S_s, ACT.Exp, bias=s_self[:, 3:4], scale=0.125,
                           accum_out=s_self[:, 4:5]).then_inc(ev("sample_exps_ready"), 1)
            act.activation(s_self[:, 5:6], s_self[:, 0:1], ACT.Exp, bias=s_self[:, 3:4],
                           scale=0.125).then_inc(ev("sample_exps_ready"), 1)
            split(("wo", 0))
            split(("wo", 1))
            for j in range(4):
                split_behind(("wo", j))
            norm(0, zT[:, :, :], sq)
            operand(1)
            act.wait_ge(ev("kv_stored"), 64)
            for j in range(FF // 256):
                for m in range(2):
                    if j:
                        free((("f3", j - 1), m))
                    bk = see((("f1", j), m))
                    act.activation(sg[:, m, :], bk[:, 0:T], ACT.Silu).then_inc(ev("silu_ready"), 1)
                split_behind(("f1", j))
                for m in range(2):
                    act.wait_ge(ev("gm_ready"), 2 * j + m + 1)
                    act.copy(g_hi_f[:, 2 * j + m, :], gm[:, m, :]).then_inc(ev("gm_hi_ready"), 1)
                split_behind(("f3", j))
            for cb in range(4):
                for kb in range(3):
                    split_behind(("f2", cb, kb))
            norm(1, zT[:, :, :], sq)
            operand(2)
            for m in range(KC):
                a, g = ("p1", m // 2), ("p1g", m // 2)
                if m >= 2:
                    free((("p1g", m // 2 - 1), m % 2))
                bk = see((g, m % 2))
                act.activation(sgc[:, m % 2, :], bk[:, 0:T], ACT.Sigmoid,
                               bias=prm[:, PRM_PW1 + KC + m:PRM_PW1 + KC + m + 1]).then_inc(ev("sigmoid_ready"), 1)
                if m % 2:
                    split_behind(a)
                    split_behind(g)
                    for c in (m - 1, m):
                        for i in range(PE_TAPS):
                            n = c * PE_TAPS + i
                            if n >= 4:
                                cc, ii = divmod(n - 4, PE_TAPS)
                                if ii == PE_TAPS - 1:
                                    act.wait_ge(psum_filled, where[("taps", cc)] + 1)
                                else:
                                    act.wait_ge(ev("diag_used"), cc * (PE_TAPS - 1) + ii + 1)
                            j = CW - PE_TAPS + i
                            act.activation(dw_diag[:, n % 4, :], ident[:, :], ACT.Copy,
                                           scale=prm[:, PRM_DW + j * KC + c:PRM_DW + j * KC + c + 1]).then_inc(ev("diag_ready"), 1)
            norm(2, ydw, sq)
            for half in range(2):
                act.wait_ge(ev("conv_normed"), half + 1)
                for c in range(4 * half, 4 * half + 4):
                    last = act.activation(hT[:, c, :], ydw[:, c, :], ACT.Silu, scale=prm[:, PRM_CLG + c:PRM_CLG + c + 1],
                                          bias=prm[:, PRM_CLB + c:PRM_CLB + c + 1])
                    last.then_inc(ev("conv_silu_ready"), 1)
                act.wait_ge(ev("conv_silu_ready"), 4 * half + 4)
                act.copy(h_hi[:, 4 * half:4 * half + 4, :], hT[:, 4 * half:4 * half + 4, :]).then_inc(ev("h_hi_ready"), 1)
            for j in range(4):
                split_behind(("p2", j))
            norm(3, zT[:, :, :], sq)
            act.wait_ge(ev("top_ready"), 1)
            act.activation(edif[:, :], dif[:, :], ACT.Exp).then_inc(ev("gate_exps_ready"), 1)

            out_b = banks[:, 4:6, :].rearrange("p b n -> p (b n)")
            xT_b = banks[:, 2:4, :].rearrange("p b n -> p (b n)")

            def gathered(n):
                act.wait_ge(ev("moe_x_filled"), n)
                act.copy(x_hi[:, :], xT_b).then_inc(ev("moe_x_hi_ready"), 1)

            act.wait_ge(ev("u_stored"), 32)
            act.sem_inc(ev("moe_out_kept"), 1)
            gathered(1)

            def tail(w):
                act.wait_ge(ev("moe_units_used"), EU * w + SPLITS + EU)
                act.copy(out_sb, out_b).then_inc(ev("moe_out_kept"), 1)
                gathered(w + 2)

            def expert(w, first=False):
                def unit_used(n):
                    act.wait_ge(ev("moe_units_used"), EU * w + SPLITS + n + 1)

                for n in range(EU):
                    s = n // UNITS
                    if n % UNITS == 0:
                        act.wait_ge(slot_sem[pos_of(s)], w * (16 * ES // RING) + moe_loaded(s))
                    act.wait_ge(ev("moe_units_used"), EU * w + n + 1)
                    o = (n % UNITS) * UW
                    act.copy(w_hi[:, n % SPLITS, :], ring[:, pos_of(s), o:o + UW]).then_inc(ev("moe_hi_ready"), 1)
                    if n == SPLITS - 1 and not first:
                        tail(w - 1)
                    for j in range(EJ):
                        if n == last_unit("w1", j) + SPLITS - 1:
                            unit_used(last_unit("w1", j))
                            act.activation(g_tok[:, :], banks[:, 2 * (j % 2), :], ACT.Silu)\
                               .then_inc(ev("moe_silu_ready"), 1)
                        if n == last_unit("w3", j) + TURN + SPLITS - 1:
                            act.wait_ge(ev("moe_gT_filled"), EJ * w + j + 1)
                            act.copy(g_hi[:, j % 2, :], banks[:, 6, :]).then_inc(ev("moe_g_hi_ready"), 1)

            last_item = passes(act, expert)
            tail(last_item)
            norm(4, zT[:, :, :], hT[:, :, :])

        @block_.vector
        def _(dve):
            step = Steps(dve, ev("vector_step"))
            settle, announce = step.settle, step.announce
            taken = [0]

            def take(name):
                n = taken[0]
                assert order[n] == name, (order[n], name)
                taken[0] += 1
                dve.wait_ge(psum_filled, n + 1)
                return banks[:, n % NBANK, :]

            def drained(ins, by=1):
                step(ins, psum_drained, by)

            def ada_row(layer, j):
                bk = take(("ada", layer, j))
                drained(dve.tensor_copy(arow[:, (layer * 12 + j) % 2, :], bk[:, :]))
                announce("ada_row_kept")
                pending.append((layer, j))

            def ada_turn():
                layer, j = pending.pop(0)
                bk = take(("adaT", layer, j))
                plus = 1.0 if (4 * j // KC) % 3 else 0.0
                bias = prm[:, layer * 48 + 4 * j:layer * 48 + 4 * j + 4].unsqueeze(2).to_broadcast([P, 4, 9])
                drained(dve.scalar_tensor_tensor(adaT[:, layer, 4 * j:4 * j + 4, :], bk[:, 0:36].rearrange("p (m n) -> p m n", n=9),
                                                 plus, bias, ALU.add, ALU.add))

            def filler():
                layer, j = todo.pop(0)
                ada_row(layer, j)
                if len(pending) > 1:
                    ada_turn()

            def col(layer, k, c):
                return adaT[:, layer, k * KC + c, 0:1]

            def cols_s(layer, k):
                return adaT[:, layer, k * KC:(k + 1) * KC, 1:9]

            def split(name):
                q, n = split_no[name], index[name]
                size = stream[n][1][0][1]
                for u in range(UNITS):
                    i, o = (q * UNITS + u) % SPLITS, u * UW
                    e = min(o + UW, size)
                    dve.wait_ge(ev("w_hi_ready"), q * UNITS + u + 1)
                    dve.tensor_tensor(w_lo[:, i, 0:e - o], ring[:, n % RING, o:e], w_hi[:, i, 0:e - o].bitcast(F32),
                                      ALU.subtract).then_inc(ev("w_lo_ready"), 1)

            def split_behind(name):
                q = split_no[name] + AHEAD
                if q < len(splits) and not (name[0] == "qkv" and splits[q][0] == "wo"):
                    split(splits[q])

            def low_halves(i, half):
                c = slice(4 * half, 4 * half + 4)
                dve.wait_ge(ev("h_hi_ready"), 2 * i + half + 1)
                step(dve.tensor_tensor(h_lo[:, c, :], hT[:, c, :], h_hi[:, c, :].bitcast(F32), ALU.subtract))

            def modulate(i, layer, k, part=True):
                settle()
                for half in range(2):
                    s = slice(4 * half, 4 * half + 4)
                    for c in range(4 * half, 4 * half + 4):
                        step(dve.tensor_scalar(hT[:, c, 0:TP], xT[:, c, 0:TP], col(layer, k + 1, c), col(layer, k, c),
                                               ALU.mult, ALU.add))
                    step(dve.tensor_tensor(t8[:, s, :], xT[:, s, TP:T], cols_s(layer, k + 1)[:, s, :], ALU.mult))
                    settle()
                    step(dve.tensor_tensor(hT[:, s, TP:T], t8[:, s, :], cols_s(layer, k)[:, s, :], ALU.add))
                    if part:
                        announce("h_part_ready")
                if part:
                    for half in range(2):
                        low_halves(i, half)
                announce("h_ready")

            def residual_start():
                settle()
                step(dve.tensor_scalar(zT[:, :, :], xT[:, :, :], ALPHA, None, ALU.mult))
                settle()

            def residual_chunk(layer, k, c, src, done):
                step(dve.tensor_tensor(t8[:, c, :], src[:, TP:T], adaT[:, layer, k * KC + c, 1:9], ALU.mult))
                done(dve.scalar_tensor_tensor(zT[:, c, 0:TP], src[:, 0:TP], col(layer, k, c), zT[:, c, 0:TP], ALU.mult, ALU.add))
                settle()
                step(dve.tensor_tensor(zT[:, c, TP:T], zT[:, c, TP:T], t8[:, c, :], ALU.add), ev("ln_chunk_ready"))

            def norm(i, z, g, b, out):
                settle()
                dve.wait_ge(ev("stats_filled"), 2 * i + 1)
                mean, halves = banks[:, 6, 0:T], [slice(0, 4), slice(4, 8)]
                for c in halves:
                    step(dve.tensor_tensor(z[:, c, :], z[:, c, :], mean.unsqueeze(1).to_broadcast([P, 4, T]), ALU.subtract),
                         ev("ln_centered"))
                dve.wait_ge(ev("ln_std_ready"), i + 1)
                step(dve.reciprocal(rstd[:, :], std[:, :]))
                settle()
                for c in halves:
                    step(dve.tensor_tensor(z[:, c, :], z[:, c, :], rstd[:, :].unsqueeze(1).to_broadcast([P, 4, T]), ALU.mult))
                    if out is None:
                        announce("conv_normed")
                settle()
                if out is not None:
                    for c in range(KC):
                        step(dve.tensor_scalar(out[:, c, :], z[:, c, :], prm[:, g + c:g + c + 1], prm[:, b + c:b + c + 1],
                                               ALU.mult, ALU.add))
                announce("ln_done")

            dve.wait_ge(ev("constants_ready"), 1)
            bk = take("prm")
            step(dve.tensor_copy(prm[:, 0:208], bk[:, 0:208]))
            drained(dve.tensor_copy(prm[:, 256:504], bk[:, 256:504]))
            step(dve.tensor_tensor(t16, e16, slope8, ALU.mult))
            settle()
            step(dve.tensor_reduce(slope8_c, t16, AX.X, ALU.add))
            bk = take("cT")
            step(dve.memset(cT, 0.0))
            settle()
            drained(dve.tensor_copy(cT[:, :, 0:9], bk[:, 0:72].rearrange("p (c n) -> p c n", n=9)))
            announce("cT_ready")
            for k in range(KC):
                bk = take(("xT", k))
                drained(dve.tensor_copy(xT[:, k, :], bk[:, 0:T]))
            pending = []
            for j in range(4):
                ada_row(0, j)
                if len(pending) > 1:
                    ada_turn()
            ada_turn()
            split(("qkv", 0))
            split(("qkv", 1))
            modulate(0, 0, 0)
            for j in range(12):
                for m in range(2):
                    bk = take((("qkv", j), m))
                    c = 2 * j + m
                    drained(dve.tensor_copy(qkT[:, c, :] if c < 2 * KC else zT[:, c - 2 * KC, :], bk[:, 0:T]))
                split_behind(("qkv", j))
            announce("qkv_ready")
            for i, (t0, tn) in enumerate(TILES):
                for half in range(2):
                    bk = take((("v_tok", i), half))
                    cols = slice(half * 512, (half + 1) * 512)
                    drained(dve.tensor_copy(v_tok[:, i, cols] if i < 2 else v_s[:, cols], bk[0:tn, :]))
            announce("v_ready")
            for i, (t0, tn) in enumerate(TILES):
                for half in range(2):
                    bk = take((("k_tok", i), half))
                    cols = slice(half * 512, (half + 1) * 512)
                    drained(dve.tensor_copy(kx_tok[:, i, cols] if i < 2 else kx_s[0:NS, cols], bk[0:tn, :]))
            announce("k_ready")
            for half in range(2):
                bk = take(("q_s", half))
                drained(dve.tensor_copy(q_s[:, half * 512:(half + 1) * 512], bk[0:NS, :]))
            announce("q_s_ready")
            todo = list(fillers)
            for c in range(KC):
                for hh in range(2):
                    bk = take(("qk_scores", c, hh))
                    slope = 2.0 ** (-8.0 * (2 * c + hh + 1) / H)
                    drained(dve.scalar_tensor_tensor(S_p[:, hh, :], dist_p, 8.0 * slope, bk[:, 0:384], ALU.mult, ALU.add))
                    settle()
                    for i, cols in enumerate((slice(0, P), slice(P, 384))):
                        k = 2 * hh + i
                        step(dve.tensor_reduce(st_p[:, k:k + 1], S_p[:, hh, cols], AX.X, ALU.max))
                    settle()
                    step(dve.tensor_scalar(st_p[:, 4 + 2 * hh:6 + 2 * hh], st_p[:, 2 * hh:2 * hh + 2], -0.125, None, ALU.mult))
                    announce("scores_ready")
                name = ("K", c)
                wait_slot(dve, name)
                K = ring[:, index[name] % RING, :].rearrange("p (g d) -> p g d", g=PAGES)
                for half in range(2):
                    bk = take(("q_all", c, half))
                    drained(dve.tensor_tensor(prod, K[:, :, half * 512:(half + 1) * 512],
                                              bk.unsqueeze(1).to_broadcast([P, PAGES, 512]), ALU.mult))
                    settle()
                    r = c * H + half * 8
                    ins = dve.tensor_reduce(scT[:, :, r:r + 8], prod.rearrange("p g (h d) -> p g h d", d=HD), AX.X, ALU.add)
                    step(ins, ev("key_slots_used") if half else None)
                    settle()
                for hh in range(2):
                    dve.wait_ge(ev("exps_ready"), 4 * c + 2 * hh + 2)
                    step(dve.reciprocal(st_p[:, 12 + 2 * hh:14 + 2 * hh], st_p[:, 8 + 2 * hh:10 + 2 * hh]))
                    settle()
                    for i, cols in enumerate((slice(0, P), slice(P, 384))):
                        k = 12 + 2 * hh + i
                        step(dve.tensor_scalar(P_p[:, hh, cols], P_p[:, hh, cols], st_p[:, k:k + 1], None, ALU.mult))
                    announce("probs_ready")
                filler()
                for hh in range(2):
                    bk = take(("probsT", c, hh))
                    drained(dve.tensor_copy(PT_p[:, hh, :], bk[:, 0:384]))
                announce("probsT_ready")
                bk = take(("attn", c))
                step(dve.tensor_copy(h_hi[:, c, 0:TP], bk[:, 0:TP]))
                settle()
                drained(dve.tensor_tensor(h_lo[:, c, 0:TP], bk[:, 0:TP], h_hi[:, c, 0:TP].bitcast(F32), ALU.subtract))
            ada_turn()
            settle()
            prod8 = zflat[0:NS, D:2 * D]
            dve.sem_inc(ev("sample_scores_ready"), 1)
            step(dve.tensor_tensor(prod8, q_s, kx_s[0:NS, :], ALU.mult))
            settle()
            step(dve.tensor_reduce(ss, prod8.rearrange("n (h d) -> n h d", d=HD), AX.X, ALU.add))
            announce("self_scores_ready")
            bk = take("scores_s")
            drained(dve.scalar_tensor_tensor(S_s, dist_s, slope8_c, bk[:, 0:PAST], ALU.mult, ALU.add))
            bk = take("self_s")
            drained(dve.tensor_tensor(t16, bk[:, 0:H], e16, ALU.mult))
            settle()
            step(dve.tensor_reduce(s_self[:, 0:1], t16, AX.X, ALU.add))
            step(dve.tensor_reduce(s_self[:, 1:2], S_s, AX.X, ALU.max))
            settle()
            step(dve.tensor_tensor(s_self[:, 2:3], s_self[:, 0:1], s_self[:, 1:2], ALU.max))
            settle()
            step(dve.tensor_scalar(s_self[:, 3:4], s_self[:, 2:3], -0.125, None, ALU.mult))
            announce("sample_max_ready")
            dve.wait_ge(ev("sample_exps_ready"), 2)
            step(dve.tensor_tensor(s_self[:, 6:7], s_self[:, 4:5], s_self[:, 5:6], ALU.add))
            settle()
            step(dve.reciprocal(s_self[:, 7:8], s_self[:, 6:7]))
            settle()
            step(dve.tensor_scalar(P_s, P_s, s_self[:, 7:8], None, ALU.mult))
            step(dve.tensor_tensor(s_self[:, 2:3], s_self[:, 5:6], s_self[:, 7:8], ALU.mult))
            settle()
            step(dve.tensor_scalar(diag, ident[:, :], s_self[:, 2:3], None, ALU.mult))
            announce("sample_probs_ready")
            bk = take("probsT_s")
            step(dve.memset(PT_s, 0.0))
            settle()
            for e in range(2):
                ins = dve.tensor_copy(PT_s[:, :, :, e, e * H:(e + 1) * H],
                                      bk[:, 0:PAST].rearrange("p (g q e h) -> p g q e h", g=PAGES, q=4, e=2)[:, :, :, e, :])
                (drained if e else step)(ins)
            bk = take("PD")
            drained(dve.tensor_copy(PD, bk[0:NS, 0:P]))
            announce("sample_probsT_ready")
            for half in range(2):
                bk = take(("pv_s", half))
                drained(dve.tensor_tensor(own_pv[:, half * 512:(half + 1) * 512].rearrange("p (h d) -> p h d", d=HD),
                                          bk.rearrange("p (h d) -> p h d", d=HD),
                                          e16[:, half * 8:half * 8 + 8].unsqueeze(2).to_broadcast([P, 8, HD]), ALU.mult))
            announce("own_pv_ready")
            bk = take("attn_s").rearrange("p (c n) -> p c n", n=NS)[:, 0:KC, :]
            step(dve.tensor_copy(h_hi[:, :, TP:T], bk))
            settle()
            drained(dve.tensor_tensor(h_lo[:, :, TP:T], bk, h_hi[:, :, TP:T].bitcast(F32), ALU.subtract))
            announce("attn_ready")
            split(("wo", 0))
            split(("wo", 1))
            residual_start()
            for c in range(KC):
                residual_chunk(0, 2, c, take((("wo", c // 2), c % 2)), drained)
                if c % 2:
                    split_behind(("wo", c // 2))
            norm(0, zT[:, :, :], PRM_LNG, PRM_LNB, xT)
            modulate(1, 0, 3)
            dve.wait_ge(ev("kv_stored"), 64)
            for m in range(FM):
                f1, f3 = ("f1", m // 2), ("f3", m // 2)
                if m % 2 == 0:
                    take((f1, 0))
                    take((f1, 1))
                    split_behind(f1)
                bk = take((f3, m % 2))
                dve.wait_ge(ev("silu_ready"), m + 1)
                if m >= 2:
                    dve.wait_ge(ev("gm_hi_ready"), m - 1)
                step(dve.tensor_tensor(gm[:, m % 2, :], sg[:, m % 2, :], bk[:, 0:T], ALU.mult), ev("gm_ready"))
                if m % 2:
                    step.add(psum_drained, 4)
                    split_behind(f3)
                    for mm in (m - 1, m):
                        dve.wait_ge(ev("gm_hi_ready"), mm + 1)
                        step(dve.tensor_tensor(g_lo_f[:, mm, :], gm[:, mm % 2, :], g_hi_f[:, mm, :].bitcast(F32), ALU.subtract))
                    settle()
                    filler()
            filler()
            ada_turn()
            announce("g_ready")
            residual_start()
            for cb in range(4):
                for kb in range(2):
                    split_behind(("f2", cb, kb))
                for m in range(2):
                    residual_chunk(0, 5, 2 * cb + m, take(("f2", cb, m)), drained)
                split_behind(("f2", cb, 2))
            norm(1, zT[:, :, :], PRM_LNG + KC, PRM_LNB + KC, xT)
            step(dve.memset(up[:, :, 0:CW - 1], 0.0))
            for k in range(KC):
                bk = take(("stT", k))
                drained(dve.tensor_copy(us[:, k, :, 0:CW - 1], bk[:, 0:240].rearrange("p (n j) -> p n j", n=NS)))
            modulate(2, 1, 0)

            def w_dw(j, c):
                return prm[:, PRM_DW + j * KC + c:PRM_DW + j * KC + c + 1]

            def tap(j, c):
                ins = dve.scalar_tensor_tensor(ydw[:, c, 0:TP], up[:, c, j:j + TP], w_dw(j, c), ydw[:, c, 0:TP], ALU.mult, ALU.add)
                step(ins)

            for j in range(4):
                pair = (2 * j, 2 * j + 1)
                ba = [take((("p1", j), m)) for m in range(2)]
                for m in range(2):
                    take((("p1g", j), m))
                    c = 2 * j + m
                    dve.wait_ge(ev("sigmoid_ready"), c + 1)
                    bias = prm[:, PRM_PW1 + c:PRM_PW1 + c + 1]
                    step(dve.scalar_tensor_tensor(up[:, c, CW - 1:CW - 1 + TP], ba[m][:, 0:TP], bias, sgc[:, m, 0:TP], ALU.add, ALU.mult))
                    step(dve.scalar_tensor_tensor(us[:, c, :, CW - 1], ba[m][:, TP:T], bias, sgc[:, m, TP:T], ALU.add, ALU.mult))
                step.add(psum_drained, 4)
                dve.sem_inc(ev("u_chunk_ready"), 1)
                split_behind(("p1", j))
                split_behind(("p1g", j))
                for c in pair:
                    b_dw = prm[:, PRM_BDW + c:PRM_BDW + c + 1]
                    taps = prm[:, PRM_DW + c:PRM_DW + c + (CW - 1) * KC + 1:KC].unsqueeze(1).to_broadcast([P, NS, CW])
                    step(dve.tensor_tensor(us_prod, us[:, c, :, :], taps, ALU.mult))
                    step(dve.tensor_scalar(ydw[:, c, 0:TP], up[:, c, 0:TP], w_dw(0, c), b_dw, ALU.mult, ALU.add))
                    settle()
                    step(dve.tensor_reduce(t8[:, c, :], us_prod, AX.X, ALU.add))
                    settle()
                for i in range(1, CW - PE_TAPS):
                    for c in pair:
                        step.reach(1)
                        tap(i, c)
                settle()
                for c in pair:
                    bk = take(("taps", c))
                    drained(dve.tensor_tensor(ydw[:, c, 0:TP], ydw[:, c, 0:TP], bk[:, 0:TP], ALU.add))
                settle()
                for c in pair:
                    step(dve.tensor_scalar(ydw[:, c, TP:T], t8[:, c, :], prm[:, PRM_BDW + c:PRM_BDW + c + 1], None, ALU.add),
                         ev("ln_chunk_ready"))
            announce("u_ready")
            for half in range(2):
                bk = take(("u_p", half))
                drained(dve.tensor_copy(u_p[:, half * 512:(half + 1) * 512], bk[0:CW - 1, :]))
            for half in range(2):
                bk = take(("u_s", half))
                drained(dve.tensor_copy(u_s[:, half * 512:(half + 1) * 512], bk[0:NS, :]))
            announce("u_tok_ready")
            norm(2, ydw, None, None, None)
            for half in range(2):
                low_halves(3, half)
                announce("conv_ready")
            residual_start()
            for c in range(KC):
                bk = take((("p2", c // 2), c % 2))
                drained(dve.tensor_scalar(tmp_c, bk[:, 0:T], prm[:, PRM_PW2 + c:PRM_PW2 + c + 1], None, ALU.add))
                settle()
                residual_chunk(1, 2, c, tmp_c, step)
                if c % 2:
                    split_behind(("p2", c // 2))
            norm(3, zT[:, :, :], PRM_LNG + 2 * KC, PRM_LNB + 2 * KC, xT)
            modulate(None, 1, 3, part=False)
            moe_step = ev("moe_vector_step")

            def select(n, w):
                dve.wait_ge(moe_step, n)
                for i in range(3):
                    last = dve.tensor_scalar(sel_t[:, i, :], iota_slot[:, :], rank_c[:, i:i + 1], None, ALU.is_equal)
                    if i == 2:
                        last.then_inc(ev("moe_sel_ready"), 1)
                    else:
                        last.then_inc(ev("moe_sel_parts"), 1)

            dve.wait_ge(ev("u_stored"), 32)
            step(dve.tensor_scalar(xT[:, :, :], xT[:, :, :], ALPHA, None, ALU.mult))
            step(dve.memset(zT[:, :, :], 0.0), ev("moe_y_added"))
            step(dve.memset(logit[:, :, :], 0.0))
            step(dve.memset(rank_w[:, :, :], -1.0))
            step(dve.memset(gate_w[:, :, :], 0.0))
            settle()
            bk = take("logits")
            for i, (t0, tn) in enumerate(TILES):
                (drained if i == 2 else step)(dve.tensor_copy(logit[0:tn, i, :], bk[0:tn, 8 * i:8 * i + 8]))
            settle()
            for i in range(3):
                step(dve.max(top[:, i, :], logit[:, i, :]))
            settle()
            for i in range(3):
                step(dve.max_index(topi[:, i, :], top[:, i, :], logit[:, i, :]))
            step(dve.tensor_tensor(dif[:, :], top[:, :, 1], top[:, :, 0], ALU.subtract))
            announce("top_ready")
            step(dve.tensor_copy(topf[:, :, :], topi[:, :, 0:2]))
            settle()
            for k in range(2):
                for i in range(3):
                    step(dve.tensor_scalar(oh[:, k, i, :], iota_e[:, :], topf[:, i, k:k + 1], None, ALU.is_equal))
            settle()
            step(dve.tensor_tensor(sel[:, :, :], oh[:, 0, :, :], oh[:, 1, :, :], ALU.add))
            announce("selected_ready")
            dve.wait_ge(ev("gate_exps_ready"), 1)
            step(dve.tensor_scalar(dif[:, :], edif[:, :], 1.0, None, ALU.add))
            settle()
            step(dve.reciprocal(gts[:, :, 0], dif[:, :]))
            settle()
            step(dve.tensor_tensor(gts[:, :, 1], edif[:, :], gts[:, :, 0], ALU.mult))
            settle()
            for i in range(3):
                step(dve.tensor_scalar(gate_w[:, i, 0:NE], oh[:, 0, i, :], gts[:, i, 0:1], None, ALU.mult))
            settle()
            for i in range(3):
                step(dve.scalar_tensor_tensor(gate_w[:, i, 0:NE], oh[:, 1, i, :], gts[:, i, 1:2], gate_w[:, i, 0:NE],
                                              ALU.mult, ALU.add))
            settle()
            for g in range(1, GROUPS):
                step(dve.tensor_copy(gate_w[:, :, g * NE:(g + 1) * NE], gate_w[:, :, 0:NE]))
            for i, (t0, tn) in enumerate(TILES):
                for half in range(2):
                    bk = take((("h_tok", i), half))
                    drained(dve.tensor_copy(h_tok[0:tn, i, half * 512:(half + 1) * 512], bk[0:tn, :]))
            bk = take("ranks")
            for i, (t0, tn) in enumerate(TILES):
                step(dve.scalar_tensor_tensor(rank_w[0:tn, i, 0:NE], bk[0:tn, 8 * i:8 * i + 8], 1.0, sel[0:tn, i, :],
                                              ALU.add, ALU.mult))
            step(dve.memset(scan[:, :, :], 0.0))
            settle()
            for g in range(1, GROUPS):
                (drained if g == GROUPS - 1 else step)(
                    dve.tensor_scalar(more_f[:, (g - 1) * NE:g * NE], bk[:, 24:32], float(P * g), None, ALU.is_gt))
            settle()
            for i, (t0, tn) in enumerate(TILES):
                step(dve.tensor_scalar(rank_w[0:tn, i, 0:NE], rank_w[0:tn, i, 0:NE], -1.0, None, ALU.add))
            settle()
            dve.tensor_copy(rank_c[:, :], rank_w[:, :, 0]).then_inc(moe_step, 1)
            select(1, 0)
            step(dve.tensor_copy(scan[:, 0, MORE:], more_f[:, :]))
            settle()
            a = 0
            while 1 << a < MORE:
                step(dve.tensor_tensor(scan[:, 1 - a % 2, MORE:], scan[:, a % 2, MORE:],
                                       scan[:, a % 2, MORE - (1 << a):2 * MORE - (1 << a)], ALU.add))
                settle()
                a += 1
            total = scan[:, a % 2, MORE:]
            step(dve.tensor_scalar(n_items[:, 0:1], total[:, MORE - 1:MORE], float(NE), None, ALU.add))
            step(dve.tensor_scalar(n_items[:, 1:2], total[:, MORE - 1:MORE], float(NE - 1), None, ALU.add))
            step(dve.scalar_tensor_tensor(place[:, :], total, float(NE), more_f[:, :], ALU.add, ALU.mult))
            settle()
            step(dve.tensor_scalar(place[:, :], place[:, :], -1.0, None, ALU.add))
            step(dve.memset(list_f[:, :, :], 0.0))
            settle()
            step(dve.tensor_tensor(at_place[:, :, :], iota_place[:, :].unsqueeze(2).to_broadcast([P, MORE + 1, MORE]),
                                   place[:, :].unsqueeze(1).to_broadcast([P, MORE + 1, MORE]), ALU.is_equal))
            step(dve.tensor_copy(list_f[:, 0, 0:NE], iota_e[:, :]))
            settle()
            for k, value in ((0, below), (1, expert_v)):
                step(dve.tensor_tensor(at_value[:, :, :], at_place[:, :, :],
                                       value[:, :].unsqueeze(1).to_broadcast([P, MORE + 1, MORE]), ALU.mult))
                settle()
                step(dve.tensor_reduce(list_f[:, k, NE:], at_value[:, :, :], AX.X, ALU.add))
                settle()
            step(dve.tensor_scalar(list_f[:, 0, NE:], list_f[:, 0, NE:], float(ITEMS), None, ALU.add))
            settle()
            step(dve.tensor_copy(column_of[:, :], list_f[:, 0, :]))
            step(dve.tensor_copy(expert_of[:, :], list_f[:, 1, :]))
            for g in range(1, GROUPS):
                step(dve.tensor_scalar(rank_w[:, :, g * NE:(g + 1) * NE], rank_w[:, :, 0:NE], float(-P * g), None, ALU.add))
            announce("moe_list_ready")

            xT_b = banks[:, 2:4, :].rearrange("p b n -> p (b n)")
            def gathered(n):
                dve.wait_ge(ev("moe_x_hi_ready"), n)
                dve.tensor_tensor(x_lo[:, :], xT_b, x_hi[:, :].bitcast(F32), ALU.subtract).then_inc(ev("moe_x_lo_ready"), 1)

            dve.sem_inc(ev("moe_gsel_ready"), 1)
            gathered(1)

            def tail(w):
                gathered(w + 2)
                for k in range(KC):
                    dve.wait_ge(ev("moe_y_filled"), KC * w + k + 1)
                    if k == 0:
                        dve.wait_ge(ev("moe_y_added"), KC * w + 1)
                    dve.tensor_tensor(zT[:, k, :], zT[:, k, :], banks[:, 6 + k % 2, 0:T], ALU.add)\
                       .then_inc(ev("moe_y_added"), 1)

            def expert(w, first=False):
                for n in range(EU):
                    s, o = n // UNITS, (n % UNITS) * UW
                    dve.wait_ge(ev("moe_hi_ready"), EU * w + n + 1)
                    dve.tensor_tensor(w_lo[:, n % SPLITS, :], ring[:, pos_of(s), o:o + UW],
                                      w_hi[:, n % SPLITS, :].bitcast(F32), ALU.subtract).then_inc(ev("moe_lo_ready"), 1)
                    if n == SPLITS - 1 and not first:
                        tail(w - 1)
                    if n == 4:
                        dve.wait_ge(ev("moe_gsel_ready"), w + 1)
                        dve.wait_ge(ev("moe_gsel_parts"), 2 * w + 2)
                        c = dve.value_load(column_of[0:1, bass.ds(w, 1)], min_val=0, max_val=ITEMS)
                        dve.tensor_copy(gate_c[:, :], gate_w[:, :, bass.ds(c, 1)].rearrange("p i o -> p (i o)")).then_inc(moe_step, 1)
                        dve.wait_ge(moe_step, 2 * w + 2)
                        for i in range(3):
                            last = dve.tensor_scalar(gsel_t[:, i, :], iota_slot[:, :], rank_c[:, i:i + 1], gate_c[:, i:i + 1],
                                                     ALU.is_equal, ALU.mult)
                            last.then_inc(ev("moe_gsel_ready" if i == 2 else "moe_gsel_parts"), 1)
                    if n == 12 + SPLITS - 1:
                        dve.wait_ge(ev("moe_gs_filled"), w + 1)
                        dve.tensor_copy(gs, banks[:, 7, 0:T]).then_inc(ev("moe_gs_kept"), 1)
                    if n == 30:
                        dve.wait_ge(ev("moe_gsel_ready"), w + 2)
                        dve.wait_ge(ev("moe_gsel_parts"), 2 * w + 4)
                        dve.wait_ge(ev("moe_sel_parts"), 2 * w + 2)
                        c = dve.value_load(column_of[0:1, bass.ds(w + 1, 1)], min_val=0, max_val=ITEMS)
                        dve.tensor_copy(rank_c[:, :], rank_w[:, :, bass.ds(c, 1)].rearrange("p i o -> p (i o)")).then_inc(moe_step, 1)
                        select(2 * w + 3, w + 1)
                    for j in range(EJ):
                        if n == last_unit("w3", j) + SPLITS - 1:
                            dve.wait_ge(ev("moe_units_used"), EU * w + SPLITS + last_unit("w3", j) + 1)
                            dve.wait_ge(ev("moe_silu_ready"), EJ * w + j + 1)
                            dve.tensor_tensor(g_tok[:, :], g_tok[:, :], banks[:, 2 * (j % 2) + 1, :], ALU.mult)\
                               .then_inc(ev("moe_g_ready"), 1)
                        if n == last_unit("w3", j) + TURN + SPLITS - 1:
                            dve.wait_ge(ev("moe_g_hi_ready"), EJ * w + j + 1)
                            dve.tensor_tensor(g_lo[:, j % 2, :], banks[:, 6, :], g_hi[:, j % 2, :].bitcast(F32), ALU.subtract)\
                               .then_inc(ev("moe_g_lo_ready"), 1)

            dve.sem_inc(ev("moe_gsel_parts"), 2)
            last_item = passes(dve, expert)
            tail(last_item)
            dve.drain()
            for c in range(KC):
                step(dve.tensor_tensor(t8[:, c, :], zT[:, c, TP:T], adaT[:, 1, 5 * KC + c, 1:9], ALU.mult))
                step(dve.scalar_tensor_tensor(zT[:, c, 0:TP], zT[:, c, 0:TP], col(1, 5, c), xT[:, c, 0:TP], ALU.mult, ALU.add))
            settle()
            step(dve.tensor_tensor(zT[:, :, TP:T], xT[:, :, TP:T], t8[:, :, :], ALU.add))
            settle()
            dve.sem_inc(ev("ln_chunk_ready"), KC)
            norm(4, zT[:, :, :], PRM_LNG + 3 * KC, PRM_LNB + 3 * KC, xT)
            dve.sem_inc(ev("y_ready"), 1)
            for i, (t0, tn) in enumerate(TILES):
                for half in range(2):
                    bk = take((("y", i), half))
                    drained(dve.tensor_copy(h_tok[0:tn, i, half * 512:(half + 1) * 512], bk[0:tn, :]))
                announce("y_tok_ready")

        @block_.sync
        def _(sp):
            sp.dma_start(c_rows[0:1, :], c_prompt).then_inc(ev("c_loaded"), 16)
            sp.dma_start(c_rows[1:9, :], c_sample).then_inc(ev("c_loaded"), 16)
            sp.dma_start(pages_sb[:, :], page_table.rearrange("(o n) g -> o (n g)", o=1)).then_inc(ev("pages_loaded"), 16)
            for dst, src in (
                    (rows[0:96, 0, :], ada_b.rearrange("l (r p) -> (l r) p", p=P)),
                    (rows[96:128, 0, :], ln_g.rearrange("l s (c p) -> (l s c) p", p=P)),
                    (rows[0:32, 1, :], ln_b.rearrange("l s (c p) -> (l s c) p", p=P)),
                    (rows[32:48, 1, :], conv_b_pw1.rearrange("l (c p) -> (l c) p", p=P)),
                    (rows[48:56, 1, :], conv_b_dw.rearrange("l (c p) -> (l c) p", p=P)),
                    (rows[56:64, 1, :], conv_ln_g.rearrange("l (c p) -> (l c) p", p=P)),
                    (rows[64:72, 1, :], conv_ln_b.rearrange("l (c p) -> (l c) p", p=P)),
                    (rows[72:80, 1, :], conv_b_pw2.rearrange("l (c p) -> (l c) p", p=P)),
                    (rows[0:128, 2, :], conv_w_dw.rearrange("l j (c p) -> (l j c) p", p=P)[0:128, :]),
                    (rows[0:120, 3, :], conv_w_dw.rearrange("l j (c p) -> (l j c) p", p=P)[128:248, :])):
                sp.dma_start(dst, src).then_inc(ev("params_loaded"), 16)
            sp.dma_start(kx_tok, x_prompt[0].rearrange("(i p) d -> p i d", p=P)).then_inc(ev("x_loaded"), 16)
            sp.dma_start(kx_s[0:NS, :], x_sample[:, 0, :]).then_inc(ev("x_loaded"), 16)
            sp.dma_start(wr[:, :, :], moe_w_router[0].rearrange("(k p) e -> p k e", p=P)).then_inc(ev("router_loaded"), 16)
            sp.dma_start(br[:, :], moe_b_router).then_inc(ev("router_loaded"), 16)

            def ring_free(n):
                if n >= RING:
                    name, _loads, who = stream[n - RING]
                    if who == "dve":
                        sp.wait_ge(ev("key_slots_used"), name[1] + 1)
                    elif who == "split":
                        sp.wait_ge(ev("w_lo_ready"), UNITS * (split_no[name] + 1))
                    else:
                        sp.wait_ge(*used[n - RING])

            phys_of = {}
            for n, (_name, loads, _who) in enumerate(stream):
                ring_free(n)
                for at, width, kn, src, page in loads:
                    if page is None:
                        dst = ring[:, n % RING, at:at + width].rearrange("p (k n) -> p k n", k=kn)
                    else:
                        seq, g = page
                        if (seq, g) not in phys_of:
                            sp.wait_ge(ev("pages_loaded"), 16)
                            i = seq * PAGES + g
                            phys_of[seq, g] = sp.value_load(pages_sb[0:1, i:i + 1], min_val=0, max_val=src.shape[0] - 1)
                        phys = phys_of[seq, g]
                        dst = ring[:, n % RING, at:at + width]
                        src = src[bass.ds(phys, 1)].rearrange("o s h d -> (o s) (h d)")
                    sp.dma_start(dst, src).then_inc(slot_sem[n % RING], 16)

            def expert_load(e, s):
                kind, j, part = EXPERT_SLOTS[s]
                if kind == "w2":
                    src = moe_w2[0][bass.ds(e, 1), j * 512 + part * 256:j * 512 + (part + 1) * 256, :].rearrange("o (k p) n -> p (o k) n", p=P)
                else:
                    w = moe_w1 if kind == "w1" else moe_w3
                    src = w[0][bass.ds(e, 1), part * 512:(part + 1) * 512, j * 512:(j + 1) * 512].rearrange("o (k p) n -> p (o k) n", p=P)
                dst = ring[:, pos_of(s), :].rearrange("p (k n) -> p k n", n=src.shape[-1])
                sp.dma_start(dst, src).then_inc(slot_sem[pos_of(s)], 16)

            def expert(e, w, s):
                sp.wait_ge(ev("moe_lo_ready"), EU * w + UNITS * (s - RING + 1))
                expert_load(e, s)

            for s in range(ES):
                if s < RING:
                    ring_free(NPRE + s)
                    expert_load(0, s)
                else:
                    expert(0, 0, s)
            with sp.Fori(1, NE) as w:
                for s in range(ES):
                    expert(w, w, s)
            sp.wait_ge(ev("moe_list_ready"), 1)
            items = sp.value_load(n_items[0:1, 0:1], min_val=NE, max_val=ITEMS)
            with sp.Fori(NE, ITEMS) as w:
                with sp.If(items > w):
                    e = sp.value_load(expert_of[0:1, bass.ds(w, 1)], min_val=0, max_val=NE - 1)
                    for s in range(ES):
                        expert(e, w, s)
                sp.nop()
            for i, (t0, tn) in enumerate(TILES):
                sp.wait_ge(ev("y_tok_ready"), i + 1)
                dst = y_prompt[0, t0:t0 + tn, :] if i < 2 else y_sample[:, 0, :]
                sp.dma_start(dst, h_tok[0:tn, i, :]).then_inc(ev("y_stored"), 16)
            sp.wait_ge(ev("y_stored"), 16 * 3)

        @block_.gpsimd
        def _(pool):
            step = Steps(pool, ev("pool_step"))

            def do(ins):
                step(ins)
                step.settle()

            do(pool.memset(ident[:, :], 0.0))
            do(pool.affine_select(out=ident[:, :], in_=ident[:, :], compare_op=ALU.not_equal, fill=1.0,
                                  base=0, pattern=[[-1, P]], channel_multiplier=1))
            do(pool.memset(ones[:, :], 1.0))
            do(pool.memset(mean_w[:, :], 1.0 / D))
            do(pool.memset(before[:, :], 1.0))
            do(pool.affine_select(out=before[:, :], in_=before[:, :], compare_op=ALU.is_gt, fill=0.0,
                                  base=0, pattern=[[1, P]], channel_multiplier=-1))
            do(pool.iota(iota_slot[:, :], pattern=[[1, P]], base=0, channel_multiplier=0, allow_small_or_imprecise_dtypes=True))
            do(pool.iota(iota_e[:, :], pattern=[[1, NE]], base=0, channel_multiplier=0, allow_small_or_imprecise_dtypes=True))
            do(pool.iota(iota_place[:, :], pattern=[[1, MORE + 1]], base=NE, channel_multiplier=0, allow_small_or_imprecise_dtypes=True))
            do(pool.iota(below[:, :], pattern=[[1, MORE]], base=NE - ITEMS, channel_multiplier=0, allow_small_or_imprecise_dtypes=True))
            do(pool.iota(expert_v[:, :], pattern=[[0, GROUPS - 1], [1, NE]], base=0, channel_multiplier=0, allow_small_or_imprecise_dtypes=True))
            do(pool.memset(eps_t[:, :], EPS))
            for q0, kn, at in ((0, P, 0), (P, TP, P)):
                d = dist_p[:, at:at + kn]
                do(pool.iota(d, pattern=[[1, kn]], base=-q0, channel_multiplier=-1, allow_small_or_imprecise_dtypes=True))
                do(pool.affine_select(out=d, in_=d, compare_op=ALU.is_ge, fill=MASKED, base=q0, pattern=[[-1, kn]],
                                      channel_multiplier=1))
            do(pool.iota(dist_s, pattern=[[1, PAST]], base=-PAST, channel_multiplier=0, allow_small_or_imprecise_dtypes=True))
            do(pool.memset(e16, 0.0))
            for n in range(NS):
                do(pool.affine_select(out=e16, in_=e16, compare_op=ALU.not_equal, fill=1.0, base=-H * n,
                                      pattern=[[-1, H]], channel_multiplier=1))
            do(pool.memset(fold, 0.0))
            for n in range(4):
                do(pool.affine_select(out=fold, in_=fold, compare_op=ALU.not_equal, fill=1.0, base=-32 * n,
                                      pattern=[[-1, 9]], channel_multiplier=1))
            for m, pattern, mult in ((e8, [[-H, NS]], 1), (e8T, [[1, P]], -H)):
                do(pool.memset(m, 1.0))
                do(pool.affine_select(out=m, in_=m, compare_op=ALU.is_ge, fill=0.0, base=0, pattern=pattern,
                                      channel_multiplier=mult))
                do(pool.affine_select(out=m, in_=m, compare_op=ALU.is_ge, fill=0.0, base=H - 1,
                                      pattern=[[-pattern[0][0], pattern[0][1]]], channel_multiplier=-mult))
            for h in range(H):
                do(pool.memset(slope8[:, h:h + 1], 8.0 * 2.0 ** (-8.0 * (h + 1) / H)))
            for _i in range(1):
                pool.sem_inc(ev("constants_ready"), 1)

            def store(dst, src, name="kv_stored"):
                pool.dma_start(dst, src).then_inc(ev(name), 16)

            store(nc_sample[0, :, 0:CW - 2, :], state_conv[0, :, 1:CW - 1, :], "state_stored")
            pool.wait_ge(ev("v_ready"), 1)
            store(nv_prompt[0, 0].rearrange("(i p) h d -> p i (h d)", p=P), v_tok)
            store(nv_sample[0, :, 0].rearrange("n h d -> n (h d)"), v_s)
            pool.wait_ge(ev("k_ready"), 1)
            store(nk_prompt[0, 0].rearrange("(i p) h d -> p i (h d)", p=P), kx_tok)
            store(nk_sample[0, :, 0].rearrange("n h d -> n (h d)"), kx_s[0:NS, :])
            pool.wait_ge(ev("ln_done"), 2)
            for i in range(2):
                pool.dma_start(st_rows[0:120, i, :], state_conv[0].rearrange("n j d -> (n j) d")[120 * i:120 * (i + 1), :])\
                    .then_inc(ev("state_loaded"), 16)
            pool.wait_ge(ev("u_tok_ready"), 1)
            store(nc_prompt[0, 0], u_p, "u_stored")
            store(nc_sample[0, :, CW - 2, :], u_s, "u_stored")
            pool.wait_ge(ev("state_stored"), 16)
            pool.wait_ge(ev("kv_stored"), 64)
            pool.wait_ge(ev("u_stored"), 32)


_INS = ['x_prompt', 'x_sample', 'cache_k', 'cache_v', 'state_conv', 'page_table', 'c_prompt', 'c_sample',
        'ada_w', 'ada_b', 'ln_g', 'ln_b', 'attn_w_qkv', 'attn_w_o', 'conv_w_pw1', 'conv_b_pw1', 'conv_w_dw',
        'conv_b_dw', 'conv_ln_g', 'conv_ln_b', 'conv_w_pw2', 'conv_b_pw2', 'ffn_w1', 'ffn_w3', 'ffn_w2',
        'moe_w_router', 'moe_b_router', 'moe_w1', 'moe_w3', 'moe_w2']
_OUTS = [((1, TP, D), 'float32'), ((NS, 1, D), 'float32'),
         ((1, 1, TP, H, HD), 'float32'), ((1, 1, TP, H, HD), 'float32'),
         ((1, NS, 1, H, HD), 'float32'), ((1, NS, 1, H, HD), 'float32'),
         ((1, 1, CW - 1, D), 'float32'), ((1, NS, CW - 1, D), 'float32')]


def kernel(**inputs):
    import numpy as _np
    import concourse.bacc as _bacc
    from concourse import mybir as _mybir
    from concourse.bass_utils import run_bass_kernel_spmd as _run

    nc = _bacc.Bacc("TRN2", target_bir_lowering=False, num_devices=1, dynamic_dma_scratch_size=4096)
    arrays, args = {}, []
    for name in _INS:
        a = _np.ascontiguousarray(inputs[name])
        arrays[f"in_{name}_dram"] = a
        args.append(nc.dram_tensor(f"in_{name}_dram", a.shape, _mybir.dt.from_np(a.dtype), kind="ExternalInput").ap())
    for i, (shape, dtype) in enumerate(_OUTS):
        dt = _mybir.dt.from_np(_np.dtype(dtype))
        args.append(nc.dram_tensor(f"out_{i}_dram", shape, dt, kind="ExternalOutput").ap())
    build(nc, *args)
    r = _run(nc, [arrays], core_ids=[0])
    return tuple(r.results[0][f"out_{i}_dram"] for i in range(len(_OUTS)))
```

```python
from contextlib import ExitStack

import concourse.bass as bass
from concourse import mybir

F32 = mybir.dt.float32
F32R = mybir.dt.float32r
I32 = mybir.dt.int32
U32 = mybir.dt.uint32
ALU = mybir.AluOpType
ACT = mybir.ActivationFunctionType
AX = mybir.AxisListType

P = 128
D = 1024
KC = D // P
TP = 256
NS = 8
T = TP + NS
TILES = ((0, 128), (128, 128), (256, NS))
H, HD = 16, 64
PAST = 256
PAGES = PAST // P
CW = 31
FF = 2816
FM = FF // P
NE = 8
FE = 3584
EJ = FE // 512
GROUPS = 3
ITEMS = GROUPS * NE
CANDS = ITEMS + NE
PAIRS = min(2 * T // (P + 1), NE - 1)
MIN_SINGLES = NE - PAIRS
MAX_ITEMS = NE + 1 + 2 * T // (2 * P + 1)
LIST = MAX_ITEMS + PAIRS + 1
PE_TAPS = 13
DIAGS = 12
ALPHA = float(4.0 ** 0.25)
EPS = 1e-5
MASKED = -1e30

RING = 7
SLOTW = 2048
UNITS = 2
UW = SLOTW // UNITS
SPLITS = 4
AHEAD = SPLITS // UNITS
TURN = 2
PARTS = 4
NBANK = 6

PRM_LNG, PRM_LNB, PRM_PW1, PRM_BDW, PRM_CLG, PRM_CLB, PRM_PW2, PRM_DW = 96, 128, 160, 176, 184, 192, 200, 256

EXPERT_SLOTS = []
for _j in range(EJ + 1):
    _kinds = (["w1", "w3"] if _j < EJ else []) + (["w2"] if _j else [])
    EXPERT_SLOTS += [(_k, _j - (_k == "w2"), _h) for _k in _kinds for _h in range(2)]
ES = len(EXPERT_SLOTS)
EU = ES * UNITS


def last_unit(kind, j):
    return UNITS * (EXPERT_SLOTS.index((kind, j, 1)) + 1) - 1


def build(nc, x_prompt, x_sample, cache_k, cache_v, state_conv, page_table, c_prompt, c_sample,
          ada_w, ada_b, ln_g, ln_b, attn_w_qkv, attn_w_o, conv_w_pw1, conv_b_pw1, conv_w_dw,
          conv_b_dw, conv_ln_g, conv_ln_b, conv_w_pw2, conv_b_pw2, ffn_w1, ffn_w3, ffn_w2,
          moe_w_router, moe_b_router, moe_w1, moe_w3, moe_w2,
          y_prompt, y_sample, nk_prompt, nv_prompt, nk_sample, nv_sample, nc_prompt, nc_sample):
    ctx = ExitStack()
    with ctx:
        def sb(name, shape, dt=F32, at=ctx):
            return at.enter_context(nc.sbuf_tensor(name, shape, dt))

        sems = {}

        def ev(name):
            if name not in sems:
                sems[name] = ctx.enter_context(nc.semaphore(name))
            return sems[name]

        ring = sb("ring", [P, RING, SLOTW])
        xT = sb("xT", [P, KC, T])
        hT = sb("hT", [P, KC, T])
        h_hi = sb("h_hi", [P, KC, T], F32R)
        h_lo = sb("h_lo", [P, KC, T], F32R)
        w_hi = sb("w_hi", [P, SPLITS, UW], F32R)
        w_lo = sb("w_lo", [P, SPLITS, UW], F32R)
        zT = sb("zT", [P, KC, T])
        prm = sb("prm", [P, 512])
        adaT = sb("adaT", [P, 2, 48, 9])
        ident = sb("ident", [P, P])
        ones = sb("ones", [P, P])
        mean_w = sb("mean_w", [P, P])
        before = sb("before", [P, P])
        iota_slot = sb("iota_slot", [P, P])
        iota_e = sb("iota_e", [P, NE])
        iota_place = sb("iota_place", [P, LIST])
        column_v = sb("column_v", [P, CANDS])
        expert_v = sb("expert_v", [P, CANDS])
        eps_t = sb("eps_t", [P, 1])
        std = sb("std", [P, T])
        rstd = sb("rstd", [P, T])
        t8 = sb("t8", [P, KC, NS])
        fuse_a = sb("fuse_a", [P, KC, 9])
        fuse_b = sb("fuse_b", [P, KC, 9])
        wr = sb("wr", [P, KC, NE])
        br = sb("br", [1, NE])
        pages_sb = sb("pages_sb", [1, NS * PAGES], I32)
        arow_sb = sb("arow_sb", [P, 2, 512])
        cT_sb = sb("cT_sb", [P, KC * 32])
        cT = cT_sb[:, :].rearrange("p (c n) -> p c n", n=32)
        fold = sb("fold", [P, 9])[:, :]
        banks = ctx.enter_context(nc.psum_tensor("banks", [P, 8, 512], F32))

        pre = ExitStack()
        arena_w = 14900
        arena = sb("arena", [P, arena_w], at=pre)

        def carve(start):
            at = [start]

            def take(n, parts=P):
                a = at[0]
                at[0] += n
                assert at[0] <= arena_end, at[0]
                return arena[0:parts, a:a + n]
            return take

        arow = [arow_sb[:, i, :] for i in range(2)] + [arena[:, arena_w - (i + 1) * 512:arena_w - i * 512] for i in range(2)]
        arena_end = arena_w - 2 * 512

        A = carve(0)
        qkT = A(2 * KC * T).rearrange("p (c t) -> p c t", t=T)
        v_tok = A(2 * D).rearrange("p (i n) -> p i n", i=2)
        v_s = A(D, NS)
        kx = A(2 * D)
        kx_tok = kx.rearrange("p (i n) -> p i n", i=2)
        kx_s = A(D)
        scT = A(2 * P).rearrange("p (g r) -> p g r", g=2)
        S_p = A(2 * 384).rearrange("p (i n) -> p i n", i=2)
        P_p = A(2 * 384).rearrange("p (i n) -> p i n", i=2)
        pt_flat = A(2 * 384)
        PT_p = pt_flat.rearrange("p (i n) -> p i n", i=2)
        dist_p = A(384)
        dist_s = A(PAST)
        e16 = A(16)
        e8 = A(NS)
        e8T = rstd[0:NS, 0:P]
        slope8 = A(H)
        slope8_c = A(1)
        st_p = A(16)
        ss = A(H, NS)
        t16 = A(H)
        s_self = A(8)
        S_s = S_p[:, 0, 0:PAST]
        diag = S_p[:, 1, 0:P]
        P_s = P_p[:, 0, 0:PAST]
        PT_s = pt_flat[:, 0:PAGES * NS * 32].rearrange("p (g q e r) -> p g q e r", g=PAGES, q=4, e=2)
        PD = std[0:NS, 0:P]
        r_off = 2 * KC * T + 2 * D + D + 2 * D + D + 2 * P + 4 * 384
        rows = arena[:, r_off:r_off + 512].rearrange("p (i n) -> p i n", i=4)
        c_off = 2 * KC * T + 2 * D + D + 2 * D + D + 2 * P
        c_rows = arena[0:9, c_off:c_off + D]
        zflat = zT[:, :, :].rearrange("p c t -> p (c t)")
        q_s = zflat[0:NS, 0:D]
        prod = zflat[:, D:2 * D].rearrange("p (g n) -> p g n", g=2)
        own_pv = zflat[:, 0:D]
        sq = arena[:, 0:KC * T].rearrange("p (c t) -> p c t", t=T)

        B = carve(0)
        sg = B(2 * T).rearrange("p (i t) -> p i t", i=2)
        gm = B(2 * T).rearrange("p (i t) -> p i t", i=2)

        C = carve(0)
        st_rows = C(2 * D).rearrange("p (i n) -> p i n", i=2)
        _ = C(KC * T - 2 * D)
        up = C(KC * (CW - 1 + TP)).rearrange("p (c t) -> p c t", c=KC)
        us = C(KC * NS * CW).rearrange("p (c n j) -> p c n j", c=KC, n=NS)
        ydw = C(KC * T).rearrange("p (c t) -> p c t", t=T)
        sgc = C(2 * T).rearrange("p (i t) -> p i t", i=2)
        us_prod = C(NS * CW).rearrange("p (n j) -> p n j", n=NS)
        tmp_c = C(T)
        dw_diag = C(DIAGS * P).rearrange("p (i n) -> p i n", i=DIAGS)
        u_p = C(D, CW - 1)
        u_s = C(D, NS)
        pre.close()

        ffn = ExitStack()
        sb("norm_and_gate_rows", [P, KC * T], at=ffn)
        g_hi_f = sb("g_hi_f", [P, FM, T], F32R, at=ffn)
        g_lo_f = sb("g_lo_f", [P, FM, T], F32R, at=ffn)
        ffn.close()

        moe = ExitStack()
        x_hi2 = sb("x_hi2", [P, KC, 2, P], F32R, at=moe)
        x_lo2 = sb("x_lo2", [P, KC, 2, P], F32R, at=moe)
        g_hi2 = sb("g_hi2", [P, 2, 4, 2 * P], F32R, at=moe)
        g_lo2 = sb("g_lo2", [P, 2, 4, 2 * P], F32R, at=moe)
        x_hi, x_lo = x_hi2[:, :, 0, :], x_lo2[:, :, 0, :]
        g_hi = g_hi2[:, :, :, :].rearrange("p i c n -> p i (c n)")[:, :, 0:512]
        g_lo = g_lo2[:, :, :, :].rearrange("p i c n -> p i (c n)")[:, :, 0:512]
        g2 = sb("g2", [P, 2 * 512], at=moe)
        g_tok = g2[:, 0:512]
        h_tok = sb("h_tok", [P, 3, D], at=moe)
        logit = sb("logit", [P, 3, NE], at=moe)
        top = sb("top", [P, 3, 8], at=moe)
        topi = sb("topi", [P, 3, 8], U32, at=moe)
        topf = sb("topf", [P, 3, 2], at=moe)
        dif = sb("dif", [P, 3], at=moe)
        edif = sb("edif", [P, 3], at=moe)
        gts = sb("gts", [P, 3, 2], at=moe)
        oh = sb("oh", [P, 2, 3, NE], at=moe)
        sel = sb("sel", [P, 3, NE], at=moe)
        rank_w = sb("rank_w", [P, 3, ITEMS + 1], at=moe)
        gate_w = sb("gate_w", [P, 3, ITEMS + 1], at=moe)
        rank_c = sb("rank_c", [P, 3], at=moe)
        gate_c = sb("gate_c", [P, 3], at=moe)
        listed = sb("listed", [P, CANDS], at=moe)
        scan = sb("scan", [P, 2, 2 * CANDS], at=moe)
        place = sb("place", [P, CANDS], at=moe)
        at_place = sb("at_place", [P, LIST, CANDS], at=moe)
        at_value = g2[:, 512:512 + LIST * CANDS].rearrange("p (l c) -> p l c", l=LIST)
        n_items = sb("n_items", [P, 4], I32, at=moe)
        column_of = sb("column_of", [P, LIST], I32, at=moe)
        second_of = sb("second_of", [P, LIST], I32, at=moe)
        expert_of = sb("expert_of", [P, LIST], I32, at=moe)
        list_f = sb("list_f", [P, 2, LIST], at=moe)
        rank_p = sb("rank_p", [P, 2, 3], at=moe)
        gate_p = sb("gate_p", [P, 3], at=moe)
        sel_p = sb("sel_p", [P, 3, 2, P], F32R, at=moe)
        gsel_p = sb("gsel_p", [P, 2, 3, P], at=moe)
        gs_p = sb("gs_p", [P, 2, T], at=moe)
        out_p = sb("out_p", [P, D], at=moe)
        h_tok_hi = [h_hi[:, :, :].rearrange("p c t -> p (c t)")[:, i * D:(i + 1) * D] for i in range(2)]
        h_tok_lo = [h_lo[:, :, :].rearrange("p c t -> p (c t)")[:, i * D:(i + 1) * D] for i in range(2)]
        h_tok_hi.append(sb("h_tok_hi2", [P, D], F32R, at=moe)[:, :])
        h_tok_lo.append(sb("h_tok_lo2", [P, D], F32R, at=moe)[:, :])
        hflat = hT[:, :, :].rearrange("p c t -> p (c t)")
        out_sb = hflat[:, 0:D]
        sel_t = hflat[:, D:D + 384].rearrange("p (i n) -> p i n", i=3)
        gsel_t = hflat[:, D + 384:D + 768].rearrange("p (i n) -> p i n", i=3)
        gs = hflat[:, D + 768:D + 768 + T]
        moe.close()

        stream = []
        w_qkv, w_o = attn_w_qkv[0], attn_w_o[0]

        def block(name, w, c0, k0=0, kn=KC, split=True):
            src = w[k0 * P:(k0 + kn) * P, c0:c0 + 256].rearrange("(k p) n -> p k n", p=P)
            stream.append((name, [(0, kn * 256, kn, src, None)], "split" if split else "pe"))

        def ada(layer, j):
            for half in range(2):
                block(("ada", layer, j, half), ada_w[layer], j * 512 + half * 256, split=False)

        def pages(name, cache, n, consumer):
            stream.append((name, [(g * D, D, 1, cache, (n, g)) for g in range(PAGES)], consumer))

        fillers = [(0, j) for j in range(4, 12)] + [(1, j) for j in range(12)]
        beside_norm = [fillers[KC + 4 * i:KC + 4 * i + 4] for i in range(3)]
        for j in range(4):
            ada(0, j)
        for j in range(12):
            block(("qkv", j), w_qkv, j * 256)
        pages(("K", 0), cache_k[0], 0, "dve")
        for c in range(KC):
            if c + 1 < KC:
                pages(("K", c + 1), cache_k[0], c + 1, "dve")
            ada(*fillers[c])
        for n in (*range(0, NS, 2), *range(1, NS, 2)):
            pages(("V", n), cache_v[0], n, "pe")
        for j in range(4):
            block(("wo", j), w_o, j * 256)
        for j in range(FF // 256):
            block(("f1", j), ffn_w1[0], j * 256)
            block(("f3", j), ffn_w3[0], j * 256)
            if j == 0:
                for f in beside_norm[0]:
                    ada(*f)
        for cb in range(4):
            for kb in range(3):
                block(("f2", cb, kb), ffn_w2[0], cb * 256, kb * KC, min(KC, FM - kb * KC))
        for j in range(4):
            block(("p1", j), conv_w_pw1[0], j * 256)
            block(("p1g", j), conv_w_pw1[0], D + j * 256)
            if j == 0:
                for f in beside_norm[1]:
                    ada(*f)
        for j in range(4):
            block(("p2", j), conv_w_pw2[0], j * 256)
            if j == 1:
                for f in beside_norm[2]:
                    ada(*f)
        NPRE = len(stream)
        index = {s[0]: n for n, s in enumerate(stream)}
        loaded = []
        per_pos = [0] * RING
        splits = [s[0] for s in stream if s[2] == "split"]
        split_no = {name: q for q, name in enumerate(splits)}
        used = {}
        freed = {}
        for n, (_n, loads, _who) in enumerate(stream):
            per_pos[n % RING] += 16 * len(loads)
            loaded.append(per_pos[n % RING])
        slot_sem = [ev(f"slot{i}_loaded") for i in range(RING)]

        def pos_of(k):
            return (NPRE + k) % RING

        def moe_loaded(k):
            return per_pos[pos_of(k)] + 16 * (k // RING + 1)

        def slot_of(name, w=256):
            return ring[:, index[name] % RING, :].rearrange("p (k n) -> p k n", n=w)

        def wait_slot(eng, name):
            n = index[name]
            eng.wait_ge(slot_sem[n % RING], loaded[n])

        psum_filled, psum_drained = ev("psum_filled"), ev("psum_drained")
        order = []
        where = {}

        block_ = ctx.enter_context(nc.Block())

        def passes(eng, item, pair, between):
            item(0, first=True)
            eng.wait_ge(ev("moe_list_ready"), 1)
            singles = eng.value_load(n_items[0:1, 1:2], min_val=MIN_SINGLES, max_val=MAX_ITEMS)
            with eng.Fori(1, MAX_ITEMS) as w:
                with eng.If(singles > w):
                    item(w)
                eng.nop()
            between(eng.value_load(n_items[0:1, 2:3], min_val=MIN_SINGLES - 1, max_val=MAX_ITEMS - 1))
            pairs = eng.value_load(n_items[0:1, 3:4], min_val=0, max_val=PAIRS)
            with eng.Fori(0, PAIRS) as d:
                with eng.If(pairs > d):
                    pair(d, eng.value_load(n_items[0:1, 1:2], min_val=MIN_SINGLES, max_val=MAX_ITEMS) + d)
                eng.nop()

        class Steps:

            def __init__(self, eng, sem):
                self.eng, self.sem, self.n, self.open = eng, sem, {}, {}

            def __call__(self, ins, sem=None, by=1):
                sem = self.sem if sem is None else sem
                ins.then_inc(sem, by)
                key = id(sem)
                self.n[key] = self.n.get(key, 0) + by
                self.open[key] = sem

            def add(self, sem, by):
                self.settle()
                self.eng.sem_inc(sem, by)
                self.n[id(sem)] = self.n.get(id(sem), 0) + by

            def reach(self, behind):
                self.eng.wait_ge(self.sem, self.n[id(self.sem)] - behind)

            def settle(self):
                for key, sem in self.open.items():
                    self.eng.wait_ge(sem, self.n[key])
                self.open = {}

            def announce(self, name):
                self.settle()
                self.eng.sem_inc(ev(name), 1)

        @block_.tensor
        def _(pe):
            def group(name):
                n = len(order)
                if n >= NBANK:
                    pe.wait_ge(psum_drained, n - NBANK + 1)
                order.append(name)
                where[name] = n
                return banks[:, n % NBANK, :]

            def filled(ins):
                ins.then_inc(psum_filled, 1)

            def slot_done(name):
                used[index[name]] = (psum_filled, len(order))

            def halves(name, k, m):
                i = (split_no[name] * UNITS + k // 4) % SPLITS
                cols = slice((k % 4) * 256 + m * P, (k % 4) * 256 + (m + 1) * P)
                return w_hi[:, i, cols], w_lo[:, i, cols]

            def wait_split(name):
                pe.wait_ge(ev("w_lo_ready"), UNITS * (split_no[name] + 1))

            def dense(slots, x_hi, x_lo, behind=None):
                for s in slots:
                    wait_split(s)
                    for m in range(2):
                        bk = group((s, m))
                        for k in range(KC):
                            hi, lo = halves(s, k, m)
                            for i, (w, x) in enumerate(((hi, x_hi), (hi, x_lo), (lo, x_hi))):
                                mm = pe.matmul(bk[:, 0:T], w, x[:, k, :], start=(k == 0 and i == 0),
                                               stop=(k == KC - 1 and i == 2))
                        filled(mm)
                        if behind is not None:
                            behind(s, m)
                    freed[split_no[s]] = (psum_filled, len(order))

            pending = []

            def ada_rows(layer, j):
                bk = group(("ada", layer, j))
                for half in range(2):
                    name = ("ada", layer, j, half)
                    wait_slot(pe, name)
                    for k in range(KC):
                        r = slice(32 * (k % 4), 32 * (k % 4) + 32)
                        mm = pe.matmul(bk[r, half * 256:(half + 1) * 256], cT[:, k, :], slot_of(name)[:, k, :],
                                       start=(k < 4), stop=(k >= 4), skip_group_check=True)
                    slot_done(name)
                filled(mm)
                pending.append((layer, j))

            def ada_turn():
                layer, j = pending.pop(0)
                i = layer * 12 + j
                pe.wait_ge(ev("ada_row_kept"), i + 1)
                bk = group(("adaT", layer, j))
                for m in range(4):
                    mm = pe.matmul(bk[:, 9 * m:9 * m + 9], arow[i % 4][:, m * P:(m + 1) * P], fold, start=True, stop=True)
                filled(mm)

            def filler():
                layer, j = todo.pop(0)
                ada_rows(layer, j)
                if len(pending) > 1:
                    ada_turn()

            def turn(name, src, parts, n):
                for half in range(2):
                    bk = group((name, half))
                    for i in range(4):
                        mm = pe.transpose(bk[0:parts, i * P:(i + 1) * P], src(half * 4 + i), ident[:, :])
                    filled(mm)

            def mean_chunk(i, z, c):
                pe.wait_ge(ev("ln_chunk_ready"), KC * i + c + 1)
                mm = pe.matmul(stat[:, 0:T], mean_w[:, :], z[:, c, :], start=(c == 0), stop=(c == KC - 1))
                if c == KC - 1:
                    mm.then_inc(ev("stats_filled"), 1)

            def mean_behind(i, z):
                def behind(s, m):
                    n = behind.n
                    behind.n += 1
                    if n >= 2:
                        mean_chunk(i, z, n - 2)
                behind.n = 0
                return behind

            def norm(i, z, s, rest=(KC - 2, KC - 1), beside=()):
                for c in rest:
                    mean_chunk(i, z, c)
                for f in beside[:1]:
                    ada_rows(*f)
                for part in range(PARTS):
                    pe.wait_ge(ev("ln_squares_ready"), PARTS * i + part + 1)
                    for c in range(KC)[part * KC // PARTS:(part + 1) * KC // PARTS]:
                        mm = pe.matmul(stat2[:, 0:T], mean_w[:, :], s[:, c, :], start=(c == 0), stop=(c == KC - 1))
                mm.then_inc(ev("stats_filled"), 1)
                for f in beside[1:]:
                    ada_rows(*f)

            stat, stat2 = banks[:, 6, :], banks[:, 7, :]
            pe.wait_ge(ev("constants_ready"), 1)
            pe.wait_ge(ev("params_loaded"), 16 * 10)
            bk = group("prm")
            for i, r in enumerate((128, 80, 128, 120)):
                mm = pe.transpose(bk[:, i * P:i * P + r], rows[0:r, i, :], ident[0:r, 0:r])
            filled(mm)
            pe.wait_ge(ev("silu_c_ready"), 1)
            bk = group("cT")
            for k in range(KC):
                mm = pe.transpose(bk[:, 9 * k:9 * k + 9], c_rows[:, k * P:(k + 1) * P], ident[0:9, 0:9])
            filled(mm)
            pe.wait_ge(ev("x_loaded"), 16 * 2)
            for k in range(KC):
                bk = group(("xT", k))
                for i, (t0, tn) in enumerate(TILES):
                    src = kx_tok[:, i, k * P:(k + 1) * P] if i < 2 else kx_s[0:NS, k * P:(k + 1) * P]
                    mm = pe.transpose(bk[:, t0:t0 + tn], src, ident[0:tn, 0:tn])
                filled(mm)
            pe.wait_ge(ev("cT_ready"), 1)
            for j in range(4):
                ada_rows(0, j)
                if len(pending) > 1:
                    ada_turn()
            ada_turn()
            pe.wait_ge(ev("h_ready"), 1)
            dense([("qkv", j) for j in range(12)], h_hi, h_lo)
            pe.wait_ge(ev("qkv_ready"), 1)
            for i, (t0, tn) in enumerate(TILES):
                turn(("v_tok", i), lambda c: zT[:, c, t0:t0 + tn], tn, 2)
            for i, (t0, tn) in enumerate(TILES):
                turn(("k_tok", i), lambda c: qkT[:, KC + c, t0:t0 + tn], tn, 2)
            turn("q_s", lambda c: qkT[:, c, TP:T], NS, 2)
            todo = list(fillers)
            def scores(c):
                for hh in range(2):
                    bk = group(("qk_scores", c, hh))
                    r = slice(hh * HD, (hh + 1) * HD)
                    pe.matmul(bk[:, 0:P], qkT[r, c, 0:P], qkT[r, KC + c, 0:P], start=True, stop=True)
                    mm = pe.matmul(bk[:, P:P + TP], qkT[r, c, P:TP], qkT[r, KC + c, 0:TP], start=True, stop=True)
                    filled(mm)
                pe.wait_ge(ev("q_s_ready"), 1)
                for half in range(2):
                    bk = group(("q_all", c, half))
                    filled(pe.matmul(bk[:, :], ident[0:NS, c:c + 1].to_broadcast([NS, P]), q_s[:, half * 512:(half + 1) * 512], start=True, stop=True))

            scores(0)
            for c in range(KC):
                if c + 1 < KC:
                    scores(c + 1)
                filler()
                for hh in range(2):
                    pe.wait_ge(ev("probs_ready"), 2 * c + hh + 1)
                    bk = group(("probsT", c, hh))
                    pe.transpose(bk[:, 0:P], P_p[:, hh, 0:P], ident[:, :])
                    pe.transpose(bk[:, P:TP], P_p[:, hh, P:TP], ident[:, :])
                    filled(pe.transpose(bk[:, TP:384], P_p[:, hh, TP:384], ident[:, :]))
                pe.wait_ge(ev("probsT_kept"), 2 * c + 2)
                bk = group(("attn", c))
                for hh in range(2):
                    r, cols = slice(hh * HD, (hh + 1) * HD), slice((2 * c + hh) * HD, (2 * c + hh + 1) * HD)
                    pe.matmul(bk[r, 0:TP], v_tok[:, 0, cols], PT_p[:, hh, 0:TP], start=True, stop=False)
                    mm = pe.matmul(bk[r, P:TP], v_tok[:, 1, cols], PT_p[:, hh, TP:384], start=False, stop=True)
                filled(mm)
            ada_turn()
            pe.wait_ge(ev("sample_scores_ready"), 1)
            bk = group("scores_s")
            for g in range(PAGES):
                mm = pe.transpose(bk[:, g * P:(g + 1) * P], scT[:, g, :], ident[:, :])
            filled(mm)
            pe.wait_ge(ev("self_scores_ready"), 1)
            bk = group("self_s")
            filled(pe.matmul(bk[:, 0:H], e8T[:, :], ss[:, :], start=True, stop=True))
            pe.wait_ge(ev("sample_probs_ready"), 1)
            bk = group("probsT_s")
            for g in range(PAGES):
                mm = pe.transpose(bk[:, g * P:(g + 1) * P], P_s[:, g * P:(g + 1) * P], ident[:, :])
            filled(mm)
            bk = group("PD")
            filled(pe.matmul(bk[0:NS, 0:P], e8[:, :], diag[:, :], start=True, stop=True))
            pe.wait_ge(ev("sample_probsT_ready"), 1)
            pv = [group(("pv_s", half)) for half in range(2)]
            for half in range(2):
                pe.matmul(pv[half], PD[:, :], v_s[:, half * 512:(half + 1) * 512], start=True, stop=False, skip_group_check=True)
            for e in range(2):
                for n in range(e, NS, 2):
                    wait_slot(pe, ("V", n))
                for half in range(2):
                    for g in range(PAGES):
                        for q in range(4):
                            V = ring[:, index[("V", 2 * q + e)] % RING, :].rearrange("p (g d) -> p g d", g=PAGES)
                            mm = pe.matmul(pv[half][32 * q:32 * q + 32, :], PT_s[:, g, q, e, :], V[:, g, half * 512:(half + 1) * 512],
                                           start=False, stop=(e == 1 and g == PAGES - 1), skip_group_check=True)
                    if e == 0 and half == 1:
                        mm.then_inc(ev("even_values_used"), 1)
                    elif e == 1:
                        filled(mm)
                for n in range(e, NS, 2):
                    used[index[("V", n)]] = (ev("even_values_used"), 1) if e == 0 else (psum_filled, len(order))
            pe.wait_ge(ev("own_pv_ready"), 1)
            bk = group("attn_s")
            for c in range(KC):
                mm = pe.matmul(bk[:, c * NS:(c + 1) * NS], own_pv[:, c * P:(c + 1) * P], e8, start=True, stop=True)
            filled(mm)
            pe.wait_ge(ev("attn_ready"), 1)
            dense([("wo", j) for j in range(4)], h_hi, h_lo, mean_behind(0, zT))
            norm(0, zT, sq, beside=beside_norm[0])
            pe.wait_ge(ev("h_ready"), 2)
            for j in range(FF // 256):
                dense([("f1", j), ("f3", j)], h_hi, h_lo)
                if j == 0:
                    while pending:
                        ada_turn()
            behind = mean_behind(1, zT)
            for cb in range(4):
                two = [group(("f2", cb, m)) for m in range(2)]
                for kb in range(3):
                    name = ("f2", cb, kb)
                    wait_split(name)
                    if cb == 0:
                        pe.wait_ge(ev("g_pairs_ready"), min((kb + 1) * KC, FM) // 2)
                    for m in range(2):
                        for k in range(min(KC, FM - kb * KC)):
                            hi, lo = halves(name, k, m)
                            g = kb * KC + k
                            for i, (w, x) in enumerate(((hi, g_hi_f), (hi, g_lo_f), (lo, g_hi_f))):
                                mm = pe.matmul(two[m][:, 0:T], w, x[:, g, :], start=(g == 0 and i == 0),
                                               stop=(g == FM - 1 and i == 2))
                        if kb == 2:
                            filled(mm)
                    if kb < 2:
                        mm.then_inc(ev("f2_blocks_used"), 1)
                        freed[split_no[name]] = (ev("f2_blocks_used"), 2 * cb + kb + 1)
                    else:
                        freed[split_no[name]] = (psum_filled, len(order))
                        behind(name, 0)
                        behind(name, 1)
            norm(1, zT, sq, beside=beside_norm[1])
            pe.wait_ge(ev("h_ready"), 3)
            def taps(c):
                pe.wait_ge(ev("u_chunk_ready"), c // 2 + 1)
                bk = group(("taps", c))
                for i in range(PE_TAPS):
                    pe.wait_ge(ev("diag_ready"), c * PE_TAPS + i + 1)
                    j = CW - PE_TAPS + i
                    mm = pe.matmul(bk[:, 0:TP], dw_diag[:, (c * PE_TAPS + i) % DIAGS, :], up[:, c, j:j + TP],
                                   start=(i == 0), stop=(i == PE_TAPS - 1))
                    if i < PE_TAPS - 1:
                        mm.then_inc(ev("diag_used"), 1)
                filled(mm)

            for j in range(4):
                dense([("p1", j), ("p1g", j)], h_hi, h_lo)
                if j == 0:
                    pe.wait_ge(ev("state_loaded"), 32)
                    for k in range(KC):
                        bk = group(("stT", k))
                        for i in range(2):
                            mm = pe.transpose(bk[:, i * 120:(i + 1) * 120], st_rows[0:120, i, k * P:(k + 1) * P], ident[0:120, 0:120])
                        filled(mm)
                    while pending:
                        ada_turn()
                if j:
                    taps(2 * j - 2)
                    taps(2 * j - 1)
            taps(KC - 2)
            taps(KC - 1)
            for c in range(KC - 2):
                mean_chunk(2, ydw, c)
            pe.wait_ge(ev("u_ready"), 1)
            turn("u_p", lambda c: up[:, c, TP:TP + CW - 1], CW - 1, 2)
            turn("u_s", lambda c: us[:, c, :, CW - 1], NS, 2)
            norm(2, ydw, sq, beside=beside_norm[2])
            pe.wait_ge(ev("conv_ready"), 2)
            behind = mean_behind(3, zT)
            dense([("p2", 0)], h_hi, h_lo, behind)
            while pending:
                ada_turn()
            dense([("p2", j) for j in range(1, 4)], h_hi, h_lo, behind)
            norm(3, zT, sq)
            pe.wait_ge(ev("h_ready"), 4)
            pe.wait_ge(ev("router_loaded"), 32)
            bk = group("logits")
            for i, (t0, tn) in enumerate(TILES):
                pe.matmul(bk[0:tn, 8 * i:8 * i + 8], ones[0:1, 0:tn], br[:, :], start=True, stop=False)
                for k in range(KC):
                    mm = pe.matmul(bk[0:tn, 8 * i:8 * i + 8], hT[:, k, t0:t0 + tn], wr[:, k, :], start=False, stop=(k == KC - 1))
            filled(mm)
            for i, (t0, tn) in enumerate(TILES):
                turn(("h_tok", i), lambda c: hT[:, c, t0:t0 + tn], tn, 2)
            pe.wait_ge(ev("selected_ready"), 1)
            bk = group("ranks")
            for i, (t0, tn) in enumerate(TILES):
                for b in range(i):
                    pe.matmul(bk[0:tn, 8 * i:8 * i + 8], ones[:, 0:tn], sel[:, b, :], start=(b == 0), stop=False)
                mm = pe.matmul(bk[0:tn, 8 * i:8 * i + 8], before[0:tn, 0:tn], sel[0:tn, i, :], start=(i == 0), stop=True)
            for i, (t0, tn) in enumerate(TILES):
                mm = pe.matmul(bk[:, 24:32], ones[0:tn, :], sel[0:tn, i, :], start=(i == 0), stop=(i == 2))
            filled(mm)

            h1 = [banks[:, 0, :], banks[:, 2, :]]
            h3 = [banks[:, 1, :], banks[:, 3, :]]
            out_b = banks[:, 4:6, :].rearrange("p b n -> p (b n)")
            gT_b = banks[:, 6, :]
            gs_b = banks[:, 7, :]
            xT_b = banks[:, 2:4, :].rearrange("p b n -> p (b n)")

            def gather():
                for k in range(KC):
                    for i, (t0, tn) in enumerate(TILES):
                        mm = pe.matmul(xT_b[:, k * P:(k + 1) * P], h_tok[0:tn, i, k * P:(k + 1) * P], sel_t[0:tn, i, :],
                                       start=(i == 0), stop=(i == 2))
                    if k % 4 == 3:
                        mm.then_inc(ev("moe_x_filled"), 1)

            pe.wait_ge(psum_drained, len(order))
            pe.sem_inc(ev("moe_units_used"), SPLITS)
            pe.wait_ge(ev("moe_sel_ready"), 1)
            gather()

            def expert(w, first=False):
                for s, (kind, j, part) in enumerate(EXPERT_SLOTS):
                    for u in range(2 * part, 2 * part + UNITS):
                        n = s * UNITS + u % UNITS
                        if n in (0, 2):
                            pe.wait_ge(ev("moe_x_lo_ready"), 2 * w + 1 + n // 2)
                        pe.wait_ge(ev("moe_lo_ready"), EU * w + n + 1)
                        hi, lo = w_hi[:, n % SPLITS, :], w_lo[:, n % SPLITS, :]
                        if kind == "w2":
                            if u == 0:
                                pe.wait_ge(ev("moe_g_lo_ready"), EJ * w + j + 1)
                            if u == 0 and j == 0:
                                pe.wait_ge(ev("moe_out_kept"), w + 1)
                            a = slice(u * P, (u + 1) * P)
                            for half in range(2):
                                b = slice(half * 512, (half + 1) * 512)
                                for k, (x, y) in enumerate(((g_hi, hi), (g_hi, lo), (g_lo, hi))):
                                    mm = pe.matmul(out_b[:, b], x[:, j % 2, a], y[:, b], start=(j == 0 and u == 0 and k == 0),
                                                   stop=(j == EJ - 1 and u == 3 and k == 2))
                        else:
                            bk = (h1 if kind == "w1" else h3)[j % 2]
                            if u == 0 and kind == "w1" and j >= 2:
                                pe.wait_ge(ev("moe_g_ready"), EJ * w + j - 1)
                            for kk in range(2):
                                b = slice(kk * 512, (kk + 1) * 512)
                                for k, (x, y) in enumerate(((x_hi, hi), (x_hi, lo), (x_lo, hi))):
                                    mm = pe.matmul(bk[:, :], x[:, 2 * u + kk, :], y[:, b], start=(u == 0 and kk == 0 and k == 0),
                                                   stop=(u == 3 and kk == 1 and k == 2))
                        mm.then_inc(ev("moe_units_used"), 1)
                        if n == 12:
                            pe.wait_ge(ev("moe_gsel_ready"), w + 2)
                            for i, (t0, tn) in enumerate(TILES):
                                mm = pe.transpose(gs_b[:, t0:t0 + tn], gsel_t[0:tn, i, :], ident[0:tn, 0:tn])
                            mm.then_inc(ev("moe_gs_filled"), 1)
                        for jj in range(EJ):
                            if n == last_unit("w3", jj) + TURN:
                                pe.wait_ge(ev("moe_g_ready"), EJ * w + jj + 1)
                                if jj == 0:
                                    pe.wait_ge(ev("moe_y_added"), KC * w + 1)
                                for i in range(4):
                                    mm = pe.transpose(gT_b[:, i * P:(i + 1) * P], g_tok[:, i * P:(i + 1) * P], ident[:, :])
                                mm.then_inc(ev("moe_gT_filled"), 1)
                pe.wait_ge(ev("moe_sel_ready"), w + 2)
                gather()
                pe.wait_ge(ev("moe_out_kept"), w + 2)
                pe.wait_ge(ev("moe_gs_kept"), w + 1)
                for k in range(KC):
                    if k >= 2:
                        pe.wait_ge(ev("moe_y_added"), KC * w + k)
                    bk = (gT_b, gs_b)[k % 2]
                    pe.matmul(bk[:, 0:T], out_sb[:, k * P:(k + 1) * P], gs[:, :], start=True, stop=True)\
                      .then_inc(ev("moe_y_filled"), 1)

            def gather_pair(d):
                pe.wait_ge(ev("pair_sel_ready"), d + 1)
                for k in range(KC):
                    bk = banks[:, k // 2, (k % 2) * 256:(k % 2) * 256 + 256]
                    for i, (t0, tn) in enumerate(TILES):
                        for j, h in enumerate((h_tok_hi[i], h_tok_lo[i])):
                            mm = pe.matmul(bk, h[0:tn, k * P:(k + 1) * P], sel_p[0:tn, i, :, :].rearrange("p g n -> p (g n)"),
                                           start=(i == 0 and j == 0), stop=(i == 2 and j == 1))
                    if k % 4 == 3:
                        mm.then_inc(ev("pair_x_filled"), 1)

            def pair(d, w):
                out_p_b = [out_b, banks[:, 6:8, :].rearrange("p b n -> p (b n)")]
                for s, (kind, j, part) in enumerate(EXPERT_SLOTS):
                    for u in range(2 * part, 2 * part + UNITS):
                        n = s * UNITS + u % UNITS
                        if n in (0, 2):
                            pe.wait_ge(ev("pair_x_lo_ready"), 2 * d + 1 + n // 2)
                        pe.wait_ge(ev("moe_lo_ready"), EU * w + n + 1)
                        hi, lo = w_hi[:, n % SPLITS, :], w_lo[:, n % SPLITS, :]
                        if kind == "w2":
                            if u == 0:
                                pe.wait_ge(ev("pair_g_lo_ready"), EJ * d + j + 1)
                            if u == 0 and j == 0:
                                pe.wait_ge(ev("pair_gs_kept"), d + 1)
                            for g in range(2):
                                a = slice(g * P, (g + 1) * P)
                                for half in range(2):
                                    b = slice(half * 512, (half + 1) * 512)
                                    for k, (x, y) in enumerate(((g_hi2, hi), (g_hi2, lo), (g_lo2, hi))):
                                        mm = pe.matmul(out_p_b[g][:, b], x[:, j % 2, u, a], y[:, b], start=(j == 0 and u == 0 and k == 0),
                                                       stop=(j == EJ - 1 and u == 3 and k == 2))
                        else:
                            if u == 0 and kind == "w1" and j >= 1:
                                pe.wait_ge(ev("pair_silu_ready"), EJ * d + j)
                            if u == 0 and kind == "w3" and j >= 1:
                                pe.wait_ge(ev("pair_g_ready"), EJ * d + j)
                            for kk in range(2):
                                for m in range(4):
                                    bk = banks[:, (0 if kind == "w1" else 2) + m // 2, (m % 2) * 256:(m % 2) * 256 + 256]
                                    a = slice(kk * 512 + m * P, kk * 512 + (m + 1) * P)
                                    for k, (x, y) in enumerate(((hi, x_hi2), (hi, x_lo2), (lo, x_hi2))):
                                        mm = pe.matmul(bk, x[:, a], y[:, 2 * u + kk, :, :].rearrange("p g n -> p (g n)"),
                                                       start=(u == 0 and kk == 0 and k == 0 and m % 2 == 0),
                                                       stop=(u == 3 and kk == 1 and k == 2),
                                                       skip_group_check=True)
                        mm.then_inc(ev("moe_units_used"), 1)
                        if n == 4:
                            pe.wait_ge(ev("pair_gsel_ready"), d + 1)
                            pe.wait_ge(ev("pair_y_added"), KC * d + 1)
                            for g in range(2):
                                for i, (t0, tn) in enumerate(TILES):
                                    mm = pe.transpose(banks[:, 4 + g, t0:t0 + tn], gsel_p[0:tn, g, i, :], ident[0:tn, 0:tn])
                            mm.then_inc(ev("pair_gs_filled"), 1)
                        if n == EU - 5:
                            pe.wait_ge(ev("pair_g_ready"), EJ * d + EJ)
                            gather_pair(d + 1)
                pe.wait_ge(ev("pair_out_kept"), 2 * d + 2)
                for k in range(KC):
                    if k >= 4:
                        pe.wait_ge(ev("pair_y_added"), KC * d + k - 2)
                    bk = banks[:, 4 + k % 4, 0:T]
                    pe.matmul(bk, out_sb[:, k * P:(k + 1) * P], gs_p[:, 0, :], start=True, stop=False)
                    pe.matmul(bk, out_p[:, k * P:(k + 1) * P], gs_p[:, 1, :], start=False, stop=True)\
                      .then_inc(ev("pair_y_filled"), 1)

            passes(pe, expert, pair, lambda last: gather_pair(0))
            norm(4, zT, hT, range(KC))
            for half in range(2):
                pe.wait_ge(ev("y_ready"), half + 1)
                for i, (t0, tn) in enumerate(TILES):
                    bk = group(("y", half, i))
                    for c in range(4):
                        mm = pe.transpose(bk[0:tn, c * P:(c + 1) * P], xT[:, 4 * half + c, t0:t0 + tn], ident[:, :])
                    filled(mm)

        @block_.scalar
        def _(act):
            def see(name):
                n = where[name]
                act.wait_ge(psum_filled, n + 1)
                return banks[:, n % NBANK, :]

            def free(name):
                act.wait_ge(psum_drained, where[name] + 1)

            def norm(i, z, s):
                for part in range(PARTS):
                    c = slice(part * KC // PARTS, (part + 1) * KC // PARTS)
                    act.wait_ge(ev("ln_centered"), PARTS * i + part + 1)
                    act.activation(s[:, c, :], z[:, c, :], ACT.Square).then_inc(ev("ln_squares_ready"), 1)
                act.wait_ge(ev("stats_filled"), 2 * i + 2)
                act.activation(std[:, :], banks[:, 7, 0:T], ACT.Sqrt, bias=eps_t[:, 0:1]).then_inc(ev("ln_std_ready"), 1)

            def split(name):
                q, n = split_no[name], index[name]
                wait_slot(act, name)
                if q >= AHEAD:
                    act.wait_ge(*freed[q - AHEAD])
                size = stream[n][1][0][1]
                for u in range(UNITS):
                    o, e = u * UW, min((u + 1) * UW, size)
                    act.copy(w_hi[:, (q * UNITS + u) % SPLITS, 0:e - o], ring[:, n % RING, o:e]).then_inc(ev("w_hi_ready"), 1)

            def split_behind(name):
                q = split_no[name] + AHEAD
                if q < len(splits) and not (name[0] == "qkv" and splits[q][0] == "wo"):
                    split(splits[q])

            def operand(i):
                for half in range(2):
                    c = slice(4 * half, 4 * half + 4)
                    act.wait_ge(ev("h_part_ready"), 2 * i + half + 1)
                    act.copy(h_hi[:, c, :], hT[:, c, :]).then_inc(ev("h_hi_ready"), 1)

            act.wait_ge(ev("c_loaded"), 32)
            act.activation(c_rows, c_rows, ACT.Silu).then_inc(ev("silu_c_ready"), 1)
            split(("qkv", 0))
            split(("qkv", 1))
            operand(0)
            for j in range(12):
                split_behind(("qkv", j))
            def exps(c):
                for hh in range(2):
                    act.wait_ge(ev("scores_ready"), 2 * c + hh + 1)
                    for i, cols in enumerate((slice(0, P), slice(P, 384))):
                        k = 2 * hh + i
                        last = act.activation(P_p[:, hh, cols], S_p[:, hh, cols], ACT.Exp, bias=st_p[:, 4 + k:5 + k],
                                              scale=0.125, accum_out=st_p[:, 8 + k:9 + k])
                        last.then_inc(ev("exps_ready"), 1)

            exps(0)
            for c in range(KC):
                for hh in range(2):
                    act.copy(PT_p[:, hh, :], see(("probsT", c, hh))[:, 0:384]).then_inc(ev("probsT_kept"), 1)
                if c + 1 < KC:
                    exps(c + 1)
                act.copy(h_hi[:, c, 0:TP], see(("attn", c))[:, 0:TP]).then_inc(ev("attn_hi_ready"), 1)
            act.wait_ge(ev("sample_max_ready"), 1)
            act.activation(P_s, S_s, ACT.Exp, bias=s_self[:, 3:4], scale=0.125,
                           accum_out=s_self[:, 4:5]).then_inc(ev("sample_exps_ready"), 1)
            act.activation(s_self[:, 5:6], s_self[:, 0:1], ACT.Exp, bias=s_self[:, 3:4],
                           scale=0.125).then_inc(ev("sample_exps_ready"), 1)
            split(("wo", 0))
            split(("wo", 1))
            for j in range(4):
                split_behind(("wo", j))
            norm(0, zT[:, :, :], sq)
            operand(1)
            act.wait_ge(ev("kv_stored"), 64)
            for j in range(FF // 256):
                for m in range(2):
                    if j:
                        free((("f3", j - 1), m))
                    bk = see((("f1", j), m))
                    act.activation(sg[:, m, :], bk[:, 0:T], ACT.Silu).then_inc(ev("silu_ready"), 1)
                split_behind(("f1", j))
                for m in range(2):
                    act.wait_ge(ev("gm_ready"), 2 * j + m + 1)
                    act.copy(g_hi_f[:, 2 * j + m, :], gm[:, m, :]).then_inc(ev("gm_hi_ready"), 1)
                split_behind(("f3", j))
            for cb in range(4):
                for kb in range(3):
                    split_behind(("f2", cb, kb))
            norm(1, zT[:, :, :], sq)
            operand(2)

            def diagonals(n0, n1):
                for n in range(n0, n1):
                    c, i = divmod(n, PE_TAPS)
                    if n >= DIAGS:
                        cc, ii = divmod(n - DIAGS, PE_TAPS)
                        if ii == PE_TAPS - 1:
                            act.wait_ge(psum_filled, where[("taps", cc)] + 1)
                        else:
                            act.wait_ge(ev("diag_used"), cc * (PE_TAPS - 1) + ii + 1)
                    j = CW - PE_TAPS + i
                    act.activation(dw_diag[:, n % DIAGS, :], ident[:, :], ACT.Copy,
                                   scale=prm[:, PRM_DW + j * KC + c:PRM_DW + j * KC + c + 1]).then_inc(ev("diag_ready"), 1)

            for m in range(KC):
                a, g = ("p1", m // 2), ("p1g", m // 2)
                if m >= 2:
                    free((("p1g", m // 2 - 1), m % 2))
                bk = see((g, m % 2))
                act.activation(sgc[:, m % 2, :], bk[:, 0:T], ACT.Sigmoid,
                               bias=prm[:, PRM_PW1 + KC + m:PRM_PW1 + KC + m + 1]).then_inc(ev("sigmoid_ready"), 1)
                if m % 2:
                    split_behind(a)
                    split_behind(g)
                    if m > 1:
                        diagonals((m - 3) * PE_TAPS + DIAGS, (m - 1) * PE_TAPS)
                    diagonals((m - 1) * PE_TAPS, (m - 1) * PE_TAPS + DIAGS)
            diagonals((KC - 2) * PE_TAPS + DIAGS, KC * PE_TAPS)
            norm(2, ydw, sq)
            for half in range(2):
                act.wait_ge(ev("conv_normed"), half + 1)
                for c in range(4 * half, 4 * half + 4):
                    last = act.activation(hT[:, c, :], ydw[:, c, :], ACT.Silu, scale=prm[:, PRM_CLG + c:PRM_CLG + c + 1],
                                          bias=prm[:, PRM_CLB + c:PRM_CLB + c + 1])
                    last.then_inc(ev("conv_silu_ready"), 1)
                act.wait_ge(ev("conv_silu_ready"), 4 * half + 4)
                act.copy(h_hi[:, 4 * half:4 * half + 4, :], hT[:, 4 * half:4 * half + 4, :]).then_inc(ev("h_hi_ready"), 1)
            for j in range(4):
                split_behind(("p2", j))
            norm(3, zT[:, :, :], sq)
            for i, (t0, tn) in enumerate(TILES):
                for half in range(2):
                    bk = see((("h_tok", i), half))
                    act.copy(h_tok[0:tn, i, half * 512:(half + 1) * 512], bk[0:tn, :]).then_inc(ev("h_tok_kept"), 1)
                if i == 0:
                    act.wait_ge(ev("top_ready"), 1)
                    act.activation(edif[:, :], dif[:, :], ACT.Exp).then_inc(ev("gate_exps_ready"), 1)

            out_b = banks[:, 4:6, :].rearrange("p b n -> p (b n)")
            xT_b = banks[:, 2:4, :].rearrange("p b (k n) -> p (b k) n", n=P)

            def gathered(n):
                for half in range(2):
                    c = slice(4 * half, 4 * half + 4)
                    act.wait_ge(ev("moe_x_filled"), 2 * n - 1 + half)
                    act.copy(x_hi[:, c, :], xT_b[:, c, :]).then_inc(ev("moe_x_hi_ready"), 1)

            act.wait_ge(ev("u_stored"), 32)
            act.sem_inc(ev("moe_out_kept"), 1)
            gathered(1)

            def tail(w):
                act.wait_ge(ev("moe_units_used"), EU * w + SPLITS + EU)
                act.copy(out_sb, out_b).then_inc(ev("moe_out_kept"), 1)
                gathered(w + 2)

            def expert(w, first=False):
                def unit_used(n):
                    act.wait_ge(ev("moe_units_used"), EU * w + SPLITS + n + 1)

                for n in range(EU):
                    s = n // UNITS
                    if n % UNITS == 0:
                        act.wait_ge(slot_sem[pos_of(s)], w * (16 * ES // RING) + moe_loaded(s))
                    act.wait_ge(ev("moe_units_used"), EU * w + n + 1)
                    o = (n % UNITS) * UW
                    act.copy(w_hi[:, n % SPLITS, :], ring[:, pos_of(s), o:o + UW]).then_inc(ev("moe_hi_ready"), 1)
                    if n == SPLITS - 1 and not first:
                        tail(w - 1)
                    if first and n in (20, 28, 36):
                        i = (n - 20) // 8
                        tn = TILES[i][1]
                        act.copy(h_tok_hi[i][0:tn, :], h_tok[0:tn, i, :]).then_inc(ev("h_tok_hi_ready"), 1)
                    for j in range(EJ):
                        if n == last_unit("w1", j) + SPLITS - 1:
                            unit_used(last_unit("w1", j))
                            act.activation(g_tok[:, :], banks[:, 2 * (j % 2), :], ACT.Silu)\
                               .then_inc(ev("moe_silu_ready"), 1)
                        if n == last_unit("w3", j) + TURN + SPLITS - 1:
                            act.wait_ge(ev("moe_gT_filled"), EJ * w + j + 1)
                            act.copy(g_hi[:, j % 2, :], banks[:, 6, :]).then_inc(ev("moe_g_hi_ready"), 1)

            def gathered_pair(d):
                for half in range(2):
                    act.wait_ge(ev("pair_x_filled"), 2 * d + half + 1)
                    act.copy(x_hi2[:, 4 * half:4 * half + 4, :, :].rearrange("p k g n -> p (k g n)"),
                             banks[:, 2 * half:2 * half + 2, :].rearrange("p b n -> p (b n)")).then_inc(ev("pair_x_hi_ready"), 1)

            def pair(d, w):
                for n in range(EU):
                    s = n // UNITS
                    if n % UNITS == 0:
                        act.wait_ge(slot_sem[pos_of(s)], w * (16 * ES // RING) + moe_loaded(s))
                    act.wait_ge(ev("moe_units_used"), EU * w + n + 1)
                    o = (n % UNITS) * UW
                    act.copy(w_hi[:, n % SPLITS, :], ring[:, pos_of(s), o:o + UW]).then_inc(ev("moe_hi_ready"), 1)
                    for j in range(EJ):
                        if n == last_unit("w1", j) + SPLITS - 1:
                            act.wait_ge(ev("moe_units_used"), EU * w + SPLITS + last_unit("w1", j) + 1)
                            if j:
                                act.wait_ge(ev("pair_g_lo_ready"), EJ * d + j)
                            act.activation(g2[:, :], banks[:, 0:2, :].rearrange("p b n -> p (b n)"), ACT.Silu)\
                               .then_inc(ev("pair_silu_ready"), 1)
                        if n == last_unit("w3", j) + SPLITS:
                            act.wait_ge(ev("pair_g_ready"), EJ * d + j + 1)
                            act.copy(g_hi2[:, j % 2, :, :].rearrange("p c n -> p (c n)"), g2[:, :]).then_inc(ev("pair_g_hi_ready"), 1)
                gathered_pair(d + 1)
                act.wait_ge(ev("moe_units_used"), EU * w + SPLITS + EU)
                act.copy(out_sb, out_b).then_inc(ev("pair_out_kept"), 1)

            def between(last):
                tail(last)
                gathered_pair(0)

            passes(act, expert, pair, between)
            norm(4, zT[:, :, :], hT[:, :, :])
            for half in range(2):
                for i, (t0, tn) in enumerate(TILES):
                    act.copy(h_tok[0:tn, i, half * 512:(half + 1) * 512], see(("y", half, i))[0:tn, :]).then_inc(ev("y_tok_ready"), 1)

        @block_.vector
        def _(dve):
            step = Steps(dve, ev("vector_step"))
            settle, announce = step.settle, step.announce
            taken = [0]

            def take(name):
                n = taken[0]
                assert order[n] == name, (order[n], name)
                taken[0] += 1
                dve.wait_ge(psum_filled, n + 1)
                return banks[:, n % NBANK, :]

            def drained(ins, by=1):
                step(ins, psum_drained, by)

            def ada_row(layer, j):
                bk = take(("ada", layer, j))
                drained(dve.tensor_copy(arow[(layer * 12 + j) % 4], bk[:, :]))
                announce("ada_row_kept")
                pending.append((layer, j))

            def ada_turn():
                layer, j = pending.pop(0)
                bk = take(("adaT", layer, j))
                plus = 1.0 if (4 * j // KC) % 3 else 0.0
                bias = prm[:, layer * 48 + 4 * j:layer * 48 + 4 * j + 4].unsqueeze(2).to_broadcast([P, 4, 9])
                drained(dve.scalar_tensor_tensor(adaT[:, layer, 4 * j:4 * j + 4, :], bk[:, 0:36].rearrange("p (m n) -> p m n", n=9),
                                                 plus, bias, ALU.add, ALU.add))

            def filler():
                layer, j = todo.pop(0)
                ada_row(layer, j)
                if len(pending) > 1:
                    ada_turn()

            def col(layer, k, c):
                return adaT[:, layer, k * KC + c, 0:1]

            def cols_s(layer, k):
                return adaT[:, layer, k * KC:(k + 1) * KC, 1:9]

            def split(name):
                q, n = split_no[name], index[name]
                size = stream[n][1][0][1]
                for u in range(UNITS):
                    i, o = (q * UNITS + u) % SPLITS, u * UW
                    e = min(o + UW, size)
                    dve.wait_ge(ev("w_hi_ready"), q * UNITS + u + 1)
                    dve.tensor_tensor(w_lo[:, i, 0:e - o], ring[:, n % RING, o:e], w_hi[:, i, 0:e - o].bitcast(F32),
                                      ALU.subtract).then_inc(ev("w_lo_ready"), 1)

            def split_behind(name):
                q = split_no[name] + AHEAD
                if q < len(splits) and not (name[0] == "qkv" and splits[q][0] == "wo"):
                    split(splits[q])

            def low_halves(i, half):
                c = slice(4 * half, 4 * half + 4)
                dve.wait_ge(ev("h_hi_ready"), 2 * i + half + 1)
                step(dve.tensor_tensor(h_lo[:, c, :], hT[:, c, :], h_hi[:, c, :].bitcast(F32), ALU.subtract))

            def modulate(i, layer, k):
                settle()
                for half in range(2):
                    s = slice(4 * half, 4 * half + 4)
                    for c in range(4 * half, 4 * half + 4):
                        step(dve.tensor_scalar(hT[:, c, 0:TP], xT[:, c, 0:TP], col(layer, k + 1, c), col(layer, k, c),
                                               ALU.mult, ALU.add))
                    step(dve.tensor_tensor(t8[:, s, :], xT[:, s, TP:T], cols_s(layer, k + 1)[:, s, :], ALU.mult))
                    settle()
                    step(dve.tensor_tensor(hT[:, s, TP:T], t8[:, s, :], cols_s(layer, k)[:, s, :], ALU.add))
                    announce("h_part_ready")
                for half in range(2):
                    low_halves(i, half)
                announce("h_ready")

            def fuse(g, b, layer, k):
                scale, shift = (adaT[:, layer, kk * KC:(kk + 1) * KC, :] for kk in (k + 1, k))
                settle()
                for out, v in ((fuse_a, g), (fuse_b, b)):
                    step(dve.tensor_tensor(out[:, :, :], scale, prm[:, v:v + KC].unsqueeze(2).to_broadcast([P, KC, 9]), ALU.mult))
                settle()
                step(dve.tensor_tensor(fuse_b[:, :, :], fuse_b[:, :, :], shift, ALU.add))

            def norm_modulate(n, z, g, b, i, beside=()):
                rstd_ready(n, z)
                for half in range(2):
                    s = slice(4 * half, 4 * half + 4)
                    step(dve.tensor_tensor(z[:, s, :], z[:, s, :], rstd[:, :].unsqueeze(1).to_broadcast([P, 4, T]), ALU.mult))
                    settle()
                    if half and i is not None:
                        low_halves(i, 0)
                    for c in range(4 * half, 4 * half + 4):
                        step(dve.tensor_scalar(hT[:, c, 0:TP], z[:, c, 0:TP], fuse_a[:, c, 0:1], fuse_b[:, c, 0:1], ALU.mult, ALU.add))
                    step(dve.tensor_tensor(t8[:, s, :], z[:, s, TP:T], fuse_a[:, s, 1:9], ALU.mult))
                    settle()
                    step(dve.tensor_tensor(hT[:, s, TP:T], t8[:, s, :], fuse_b[:, s, 1:9], ALU.add))
                    if i is not None:
                        announce("h_part_ready")
                if i is not None:
                    low_halves(i, 1)
                announce("h_ready")
                for f in beside:
                    ada_row(*f)
                affine(z, g, b)

            def residual_start():
                settle()
                step(dve.tensor_scalar(zT[:, :, :], xT[:, :, :], ALPHA, None, ALU.mult))
                settle()

            def residual_chunk(layer, k, c, src, done):
                step(dve.tensor_tensor(t8[:, c, :], src[:, TP:T], adaT[:, layer, k * KC + c, 1:9], ALU.mult))
                done(dve.scalar_tensor_tensor(zT[:, c, 0:TP], src[:, 0:TP], col(layer, k, c), zT[:, c, 0:TP], ALU.mult, ALU.add))
                settle()
                step(dve.tensor_tensor(zT[:, c, TP:T], zT[:, c, TP:T], t8[:, c, :], ALU.add), ev("ln_chunk_ready"))

            def rstd_ready(i, z):
                settle()
                dve.wait_ge(ev("stats_filled"), 2 * i + 1)
                mean = banks[:, 6, 0:T]
                for part in range(PARTS):
                    c = slice(part * KC // PARTS, (part + 1) * KC // PARTS)
                    step(dve.tensor_tensor(z[:, c, :], z[:, c, :], mean.unsqueeze(1).to_broadcast([P, KC // PARTS, T]), ALU.subtract),
                         ev("ln_centered"))
                dve.wait_ge(ev("ln_std_ready"), i + 1)
                step(dve.reciprocal(rstd[:, :], std[:, :]))
                settle()

            def affine(z, g, b):
                for c in range(KC):
                    step(dve.tensor_scalar(xT[:, c, :], z[:, c, :], prm[:, g + c:g + c + 1], prm[:, b + c:b + c + 1],
                                           ALU.mult, ALU.add))
                announce("ln_done")

            dve.wait_ge(ev("constants_ready"), 1)
            bk = take("prm")
            step(dve.tensor_copy(prm[:, 0:208], bk[:, 0:208]))
            drained(dve.tensor_copy(prm[:, 256:504], bk[:, 256:504]))
            step(dve.tensor_tensor(t16, e16, slope8, ALU.mult))
            settle()
            step(dve.tensor_reduce(slope8_c, t16, AX.X, ALU.add))
            bk = take("cT")
            step(dve.memset(cT, 0.0))
            settle()
            drained(dve.tensor_copy(cT[:, :, 0:9], bk[:, 0:72].rearrange("p (c n) -> p c n", n=9)))
            announce("cT_ready")
            for k in range(KC):
                bk = take(("xT", k))
                drained(dve.tensor_copy(xT[:, k, :], bk[:, 0:T]))
            pending = []
            for j in range(4):
                ada_row(0, j)
                if len(pending) > 1:
                    ada_turn()
            ada_turn()
            split(("qkv", 0))
            modulate(0, 0, 0)
            split(("qkv", 1))
            for j in range(12):
                for m in range(2):
                    bk = take((("qkv", j), m))
                    c = 2 * j + m
                    drained(dve.tensor_copy(qkT[:, c, :] if c < 2 * KC else zT[:, c - 2 * KC, :], bk[:, 0:T]))
                split_behind(("qkv", j))
            announce("qkv_ready")
            for i, (t0, tn) in enumerate(TILES):
                for half in range(2):
                    bk = take((("v_tok", i), half))
                    cols = slice(half * 512, (half + 1) * 512)
                    drained(dve.tensor_copy(v_tok[:, i, cols] if i < 2 else v_s[:, cols], bk[0:tn, :]))
            announce("v_ready")
            for i, (t0, tn) in enumerate(TILES):
                for half in range(2):
                    bk = take((("k_tok", i), half))
                    cols = slice(half * 512, (half + 1) * 512)
                    drained(dve.tensor_copy(kx_tok[:, i, cols] if i < 2 else kx_s[0:NS, cols], bk[0:tn, :]))
            announce("k_ready")
            for half in range(2):
                bk = take(("q_s", half))
                drained(dve.tensor_copy(q_s[:, half * 512:(half + 1) * 512], bk[0:NS, :]))
            announce("q_s_ready")
            todo = list(fillers)
            def scores(c):
                for hh in range(2):
                    bk = take(("qk_scores", c, hh))
                    slope = 2.0 ** (-8.0 * (2 * c + hh + 1) / H)
                    drained(dve.scalar_tensor_tensor(S_p[:, hh, :], dist_p, 8.0 * slope, bk[:, 0:384], ALU.mult, ALU.add))
                    settle()
                    for i, cols in enumerate((slice(0, P), slice(P, 384))):
                        k = 2 * hh + i
                        step(dve.tensor_reduce(st_p[:, k:k + 1], S_p[:, hh, cols], AX.X, ALU.max))
                    settle()
                    step(dve.tensor_scalar(st_p[:, 4 + 2 * hh:6 + 2 * hh], st_p[:, 2 * hh:2 * hh + 2], -0.125, None, ALU.mult))
                    announce("scores_ready")

            def sample_scores(c):
                name = ("K", c)
                wait_slot(dve, name)
                K = ring[:, index[name] % RING, :].rearrange("p (g d) -> p g d", g=PAGES)
                for half in range(2):
                    bk = take(("q_all", c, half))
                    drained(dve.tensor_tensor(prod, K[:, :, half * 512:(half + 1) * 512],
                                              bk.unsqueeze(1).to_broadcast([P, PAGES, 512]), ALU.mult))
                    settle()
                    r = c * H + half * 8
                    ins = dve.tensor_reduce(scT[:, :, r:r + 8], prod.rearrange("p g (h d) -> p g h d", d=HD), AX.X, ALU.add)
                    step(ins, ev("key_slots_used") if half else None)
                    settle()

            scores(0)
            sample_scores(0)
            for c in range(KC):
                for hh in range(2):
                    dve.wait_ge(ev("exps_ready"), 4 * c + 2 * hh + 2)
                    step(dve.reciprocal(st_p[:, 12 + 2 * hh:14 + 2 * hh], st_p[:, 8 + 2 * hh:10 + 2 * hh]))
                    settle()
                    for i, cols in enumerate((slice(0, P), slice(P, 384))):
                        k = 12 + 2 * hh + i
                        step(dve.tensor_scalar(P_p[:, hh, cols], P_p[:, hh, cols], st_p[:, k:k + 1], None, ALU.mult))
                    announce("probs_ready")
                if c + 1 < KC:
                    scores(c + 1)
                    sample_scores(c + 1)
                filler()
                for hh in range(2):
                    take(("probsT", c, hh))
                dve.wait_ge(ev("probsT_kept"), 2 * c + 2)
                step.add(psum_drained, 2)
                bk = take(("attn", c))
                dve.wait_ge(ev("attn_hi_ready"), c + 1)
                drained(dve.tensor_tensor(h_lo[:, c, 0:TP], bk[:, 0:TP], h_hi[:, c, 0:TP].bitcast(F32), ALU.subtract))
            ada_turn()
            settle()
            prod8 = zflat[0:NS, D:2 * D]
            dve.sem_inc(ev("sample_scores_ready"), 1)
            step(dve.tensor_tensor(prod8, q_s, kx_s[0:NS, :], ALU.mult))
            settle()
            step(dve.tensor_reduce(ss, prod8.rearrange("n (h d) -> n h d", d=HD), AX.X, ALU.add))
            announce("self_scores_ready")
            bk = take("scores_s")
            drained(dve.scalar_tensor_tensor(S_s, dist_s, slope8_c, bk[:, 0:PAST], ALU.mult, ALU.add))
            bk = take("self_s")
            drained(dve.tensor_tensor(t16, bk[:, 0:H], e16, ALU.mult))
            settle()
            step(dve.tensor_reduce(s_self[:, 0:1], t16, AX.X, ALU.add))
            step(dve.tensor_reduce(s_self[:, 1:2], S_s, AX.X, ALU.max))
            settle()
            step(dve.tensor_tensor(s_self[:, 2:3], s_self[:, 0:1], s_self[:, 1:2], ALU.max))
            settle()
            step(dve.tensor_scalar(s_self[:, 3:4], s_self[:, 2:3], -0.125, None, ALU.mult))
            announce("sample_max_ready")
            dve.wait_ge(ev("sample_exps_ready"), 2)
            step(dve.tensor_tensor(s_self[:, 6:7], s_self[:, 4:5], s_self[:, 5:6], ALU.add))
            settle()
            step(dve.reciprocal(s_self[:, 7:8], s_self[:, 6:7]))
            settle()
            step(dve.tensor_scalar(P_s, P_s, s_self[:, 7:8], None, ALU.mult))
            step(dve.tensor_tensor(s_self[:, 2:3], s_self[:, 5:6], s_self[:, 7:8], ALU.mult))
            settle()
            step(dve.tensor_scalar(diag, ident[:, :], s_self[:, 2:3], None, ALU.mult))
            announce("sample_probs_ready")
            bk = take("probsT_s")
            step(dve.memset(PT_s, 0.0))
            settle()
            for e in range(2):
                ins = dve.tensor_copy(PT_s[:, :, :, e, e * H:(e + 1) * H],
                                      bk[:, 0:PAST].rearrange("p (g q e h) -> p g q e h", g=PAGES, q=4, e=2)[:, :, :, e, :])
                (drained if e else step)(ins)
            bk = take("PD")
            drained(dve.tensor_copy(PD, bk[0:NS, 0:P]))
            announce("sample_probsT_ready")
            split(("wo", 0))
            split(("wo", 1))
            for half in range(2):
                bk = take(("pv_s", half))
                drained(dve.tensor_tensor(own_pv[:, half * 512:(half + 1) * 512].rearrange("p (h d) -> p h d", d=HD),
                                          bk.rearrange("p (h d) -> p h d", d=HD),
                                          e16[:, half * 8:half * 8 + 8].unsqueeze(2).to_broadcast([P, 8, HD]), ALU.mult))
            announce("own_pv_ready")
            bk = take("attn_s").rearrange("p (c n) -> p c n", n=NS)[:, 0:KC, :]
            step(dve.tensor_copy(h_hi[:, :, TP:T], bk))
            settle()
            drained(dve.tensor_tensor(h_lo[:, :, TP:T], bk, h_hi[:, :, TP:T].bitcast(F32), ALU.subtract))
            announce("attn_ready")
            residual_start()
            fuse(PRM_LNG, PRM_LNB, 0, 3)
            for c in range(KC):
                residual_chunk(0, 2, c, take((("wo", c // 2), c % 2)), drained)
                if c % 2:
                    split_behind(("wo", c // 2))
            norm_modulate(0, zT[:, :, :], PRM_LNG, PRM_LNB, 1, beside_norm[0])
            dve.wait_ge(ev("kv_stored"), 64)
            for m in range(FM):
                f1, f3 = ("f1", m // 2), ("f3", m // 2)
                if m % 2 == 0:
                    take((f1, 0))
                    take((f1, 1))
                    split_behind(f1)
                bk = take((f3, m % 2))
                dve.wait_ge(ev("silu_ready"), m + 1)
                if m >= 2:
                    dve.wait_ge(ev("gm_hi_ready"), m - 1)
                step(dve.tensor_tensor(gm[:, m % 2, :], sg[:, m % 2, :], bk[:, 0:T], ALU.mult), ev("gm_ready"))
                if m % 2:
                    step.add(psum_drained, 4)
                    split_behind(f3)
                    for mm in (m - 1, m):
                        dve.wait_ge(ev("gm_hi_ready"), mm + 1)
                        step(dve.tensor_tensor(g_lo_f[:, mm, :], gm[:, mm % 2, :], g_hi_f[:, mm, :].bitcast(F32), ALU.subtract))
                    announce("g_pairs_ready")
                if m == 1:
                    while pending:
                        ada_turn()
            residual_start()
            fuse(PRM_LNG + KC, PRM_LNB + KC, 1, 0)
            for cb in range(4):
                for kb in range(2):
                    split_behind(("f2", cb, kb))
                for m in range(2):
                    residual_chunk(0, 5, 2 * cb + m, take(("f2", cb, m)), drained)
                split_behind(("f2", cb, 2))
            norm_modulate(1, zT[:, :, :], PRM_LNG + KC, PRM_LNB + KC, 2, beside_norm[1])
            step(dve.memset(up[:, :, 0:CW - 1], 0.0))

            def w_dw(j, c):
                return prm[:, PRM_DW + j * KC + c:PRM_DW + j * KC + c + 1]

            def tap(j, c):
                ins = dve.scalar_tensor_tensor(ydw[:, c, 0:TP], up[:, c, j:j + TP], w_dw(j, c), ydw[:, c, 0:TP], ALU.mult, ALU.add)
                step(ins)

            def join(c0):
                for c in (c0, c0 + 1):
                    bk = take(("taps", c))
                    drained(dve.tensor_tensor(ydw[:, c, 0:TP], ydw[:, c, 0:TP], bk[:, 0:TP], ALU.add))
                settle()
                for c in (c0, c0 + 1):
                    step(dve.tensor_scalar(ydw[:, c, TP:T], t8[:, c, :], prm[:, PRM_BDW + c:PRM_BDW + c + 1], None, ALU.add),
                         ev("ln_chunk_ready"))

            for j in range(4):
                pair = (2 * j, 2 * j + 1)
                ba = [take((("p1", j), m)) for m in range(2)]
                for m in range(2):
                    take((("p1g", j), m))
                    c = 2 * j + m
                    dve.wait_ge(ev("sigmoid_ready"), c + 1)
                    bias = prm[:, PRM_PW1 + c:PRM_PW1 + c + 1]
                    step(dve.scalar_tensor_tensor(up[:, c, CW - 1:CW - 1 + TP], ba[m][:, 0:TP], bias, sgc[:, m, 0:TP], ALU.add, ALU.mult))
                    step(dve.scalar_tensor_tensor(us[:, c, :, CW - 1], ba[m][:, TP:T], bias, sgc[:, m, TP:T], ALU.add, ALU.mult))
                step.add(psum_drained, 4)
                dve.sem_inc(ev("u_chunk_ready"), 1)
                split_behind(("p1", j))
                split_behind(("p1g", j))
                if j == 0:
                    for k in range(KC):
                        bk = take(("stT", k))
                        drained(dve.tensor_copy(us[:, k, :, 0:CW - 1], bk[:, 0:240].rearrange("p (n j) -> p n j", n=NS)))
                    while pending:
                        ada_turn()
                    settle()
                for c in pair:
                    b_dw = prm[:, PRM_BDW + c:PRM_BDW + c + 1]
                    taps = prm[:, PRM_DW + c:PRM_DW + c + (CW - 1) * KC + 1:KC].unsqueeze(1).to_broadcast([P, NS, CW])
                    step(dve.tensor_tensor(us_prod, us[:, c, :, :], taps, ALU.mult))
                    step(dve.tensor_scalar(ydw[:, c, 0:TP], up[:, c, 0:TP], w_dw(0, c), b_dw, ALU.mult, ALU.add))
                    settle()
                    step(dve.tensor_reduce(t8[:, c, :], us_prod, AX.X, ALU.add))
                    settle()
                for i in range(1, CW - PE_TAPS):
                    for c in pair:
                        step.reach(1)
                        tap(i, c)
                settle()
                if j:
                    join(2 * j - 2)
            join(KC - 2)
            announce("u_ready")
            for half in range(2):
                bk = take(("u_p", half))
                drained(dve.tensor_copy(u_p[:, half * 512:(half + 1) * 512], bk[0:CW - 1, :]))
            for half in range(2):
                bk = take(("u_s", half))
                drained(dve.tensor_copy(u_s[:, half * 512:(half + 1) * 512], bk[0:NS, :]))
            announce("u_tok_ready")
            rstd_ready(2, ydw)
            for c in (slice(0, 4), slice(4, 8)):
                step(dve.tensor_tensor(ydw[:, c, :], ydw[:, c, :], rstd[:, :].unsqueeze(1).to_broadcast([P, 4, T]), ALU.mult))
                announce("conv_normed")
            announce("ln_done")
            for half in range(2):
                low_halves(3, half)
                announce("conv_ready")
            for f in beside_norm[2]:
                ada_row(*f)
            residual_start()
            for c in range(KC):
                bk = take((("p2", c // 2), c % 2))
                drained(dve.tensor_scalar(tmp_c, bk[:, 0:T], prm[:, PRM_PW2 + c:PRM_PW2 + c + 1], None, ALU.add))
                settle()
                residual_chunk(1, 2, c, tmp_c, step)
                if c == 1:
                    while pending:
                        ada_turn()
                    fuse(PRM_LNG + 2 * KC, PRM_LNB + 2 * KC, 1, 3)
                if c % 2:
                    split_behind(("p2", c // 2))
            norm_modulate(3, zT[:, :, :], PRM_LNG + 2 * KC, PRM_LNB + 2 * KC, None)
            moe_step = ev("moe_vector_step")

            def select(n, w):
                dve.wait_ge(moe_step, n)
                for i in range(3):
                    last = dve.tensor_scalar(sel_t[:, i, :], iota_slot[:, :], rank_c[:, i:i + 1], None, ALU.is_equal)
                    if i == 2:
                        last.then_inc(ev("moe_sel_ready"), 1)
                    else:
                        last.then_inc(ev("moe_sel_parts"), 1)

            dve.wait_ge(ev("u_stored"), 32)
            step(dve.memset(logit[:, :, :], 0.0))
            step(dve.memset(rank_w[:, :, :], -1.0))
            step(dve.memset(gate_w[:, :, :], 0.0))
            settle()
            bk = take("logits")
            for i, (t0, tn) in enumerate(TILES):
                (drained if i == 2 else step)(dve.tensor_copy(logit[0:tn, i, :], bk[0:tn, 8 * i:8 * i + 8]))
            settle()
            for i in range(3):
                step(dve.max(top[:, i, :], logit[:, i, :]))
            settle()
            for i in range(3):
                step(dve.max_index(topi[:, i, :], top[:, i, :], logit[:, i, :]))
            step(dve.tensor_tensor(dif[:, :], top[:, :, 1], top[:, :, 0], ALU.subtract))
            announce("top_ready")
            step(dve.tensor_copy(topf[:, :, :], topi[:, :, 0:2]))
            settle()
            for k in range(2):
                for i in range(3):
                    step(dve.tensor_scalar(oh[:, k, i, :], iota_e[:, :], topf[:, i, k:k + 1], None, ALU.is_equal))
            settle()
            step(dve.tensor_tensor(sel[:, :, :], oh[:, 0, :, :], oh[:, 1, :, :], ALU.add))
            announce("selected_ready")
            dve.wait_ge(ev("gate_exps_ready"), 1)
            step(dve.tensor_scalar(dif[:, :], edif[:, :], 1.0, None, ALU.add))
            settle()
            step(dve.reciprocal(gts[:, :, 0], dif[:, :]))
            settle()
            step(dve.tensor_tensor(gts[:, :, 1], edif[:, :], gts[:, :, 0], ALU.mult))
            settle()
            for i in range(3):
                step(dve.tensor_scalar(gate_w[:, i, 0:NE], oh[:, 0, i, :], gts[:, i, 0:1], None, ALU.mult))
            settle()
            for i in range(3):
                step(dve.scalar_tensor_tensor(gate_w[:, i, 0:NE], oh[:, 1, i, :], gts[:, i, 1:2], gate_w[:, i, 0:NE],
                                              ALU.mult, ALU.add))
            settle()
            for g in range(1, GROUPS):
                step(dve.tensor_copy(gate_w[:, :, g * NE:(g + 1) * NE], gate_w[:, :, 0:NE]))
            step(dve.tensor_scalar(xT[:, :, :], xT[:, :, :], ALPHA, None, ALU.mult))
            for i in range(3):
                for half in range(2):
                    take((("h_tok", i), half))
                    dve.wait_ge(ev("h_tok_kept"), 2 * i + half + 1)
                    step.add(psum_drained, 1)
            bk = take("ranks")
            for i, (t0, tn) in enumerate(TILES):
                step(dve.scalar_tensor_tensor(rank_w[0:tn, i, 0:NE], bk[0:tn, 8 * i:8 * i + 8], 1.0, sel[0:tn, i, :],
                                              ALU.add, ALU.mult))
            step(dve.memset(scan[:, :, :], 0.0))
            step(dve.memset(listed[:, :], 0.0))
            settle()
            counts = bk[:, 24:32]
            step(dve.tensor_scalar(listed[:, 1:NE], counts[:, 1:NE], float(P), None, ALU.is_le))
            step(dve.tensor_scalar(listed[:, NE:NE + 1], counts[:, 0:1], float(P), None, ALU.is_gt))
            step(dve.tensor_scalar(listed[:, 2 * NE:3 * NE], counts, float(2 * P), None, ALU.is_gt))
            step(dve.memset(listed[:, 0:1], 1.0))
            drained(dve.tensor_scalar(listed[:, ITEMS + 1:], counts[:, 1:NE], float(P), None, ALU.is_gt))
            settle()
            for i, (t0, tn) in enumerate(TILES):
                step(dve.tensor_scalar(rank_w[0:tn, i, 0:NE], rank_w[0:tn, i, 0:NE], -1.0, None, ALU.add))
            settle()
            dve.tensor_copy(rank_c[:, :], rank_w[:, :, 0]).then_inc(moe_step, 1)
            select(1, 0)
            step(dve.tensor_copy(scan[:, 0, CANDS:], listed[:, :]))
            settle()
            a = 0
            while 1 << a < CANDS:
                step(dve.tensor_tensor(scan[:, 1 - a % 2, CANDS:], scan[:, a % 2, CANDS:],
                                       scan[:, a % 2, CANDS - (1 << a):2 * CANDS - (1 << a)], ALU.add))
                settle()
                a += 1
            total = scan[:, a % 2, CANDS:]
            items, singles = total[:, CANDS - 1:CANDS], total[:, ITEMS - 1:ITEMS]
            step(dve.tensor_copy(n_items[:, 0:1], items))
            step(dve.tensor_copy(n_items[:, 1:2], singles))
            step(dve.tensor_scalar(n_items[:, 2:3], singles, -1.0, None, ALU.add))
            step(dve.tensor_tensor(n_items[:, 3:4], items, singles, ALU.subtract))
            step(dve.tensor_tensor(place[:, :], total, listed[:, :], ALU.mult))
            settle()
            step(dve.tensor_scalar(place[:, :], place[:, :], -1.0, None, ALU.add))
            settle()
            step(dve.tensor_tensor(at_place[:, :, :], iota_place[:, :].unsqueeze(2).to_broadcast([P, LIST, CANDS]),
                                   place[:, :].unsqueeze(1).to_broadcast([P, LIST, CANDS]), ALU.is_equal))
            settle()
            for k, value in ((0, column_v), (1, expert_v)):
                step(dve.tensor_tensor(at_value[:, :, :], at_place[:, :, :],
                                       value[:, :].unsqueeze(1).to_broadcast([P, LIST, CANDS]), ALU.mult))
                settle()
                step(dve.tensor_reduce(list_f[:, k, :], at_value[:, :, :], AX.X, ALU.add))
                settle()
            step(dve.tensor_copy(column_of[:, :], list_f[:, 0, :]))
            step(dve.tensor_scalar(second_of[:, :], list_f[:, 0, :], float(NE), float(ITEMS), ALU.add, ALU.min))
            step(dve.tensor_copy(expert_of[:, :], list_f[:, 1, :]))
            for g in range(1, GROUPS):
                step(dve.tensor_scalar(rank_w[:, :, g * NE:(g + 1) * NE], rank_w[:, :, 0:NE], float(-P * g), None, ALU.add))
            announce("moe_list_ready")

            xT_b = banks[:, 2:4, :].rearrange("p b (k n) -> p (b k) n", n=P)

            def gathered(n):
                for half in range(2):
                    c = slice(4 * half, 4 * half + 4)
                    dve.wait_ge(ev("moe_x_hi_ready"), 2 * n - 1 + half)
                    dve.tensor_tensor(x_lo[:, c, :], xT_b[:, c, :], x_hi[:, c, :].bitcast(F32), ALU.subtract)\
                       .then_inc(ev("moe_x_lo_ready"), 1)

            dve.sem_inc(ev("moe_gsel_ready"), 1)
            gathered(1)

            def tail(w):
                gathered(w + 2)
                for k in range(KC):
                    dve.wait_ge(ev("moe_y_filled"), KC * w + k + 1)
                    if k == 0:
                        dve.wait_ge(ev("moe_y_added"), KC * w + 1)
                    dve.tensor_tensor(zT[:, k, :], zT[:, k, :], banks[:, 6 + k % 2, 0:T], ALU.add)\
                       .then_inc(ev("moe_y_added"), 1)

            def expert(w, first=False):
                for n in range(EU):
                    s, o = n // UNITS, (n % UNITS) * UW
                    dve.wait_ge(ev("moe_hi_ready"), EU * w + n + 1)
                    dve.tensor_tensor(w_lo[:, n % SPLITS, :], ring[:, pos_of(s), o:o + UW],
                                      w_hi[:, n % SPLITS, :].bitcast(F32), ALU.subtract).then_inc(ev("moe_lo_ready"), 1)
                    if n == SPLITS - 1 and not first:
                        tail(w - 1)
                    if first and n in (24, 32, 40):
                        i = (n - 24) // 8
                        tn = TILES[i][1]
                        dve.wait_ge(ev("h_tok_hi_ready"), i + 1)
                        dve.tensor_tensor(h_tok_lo[i][0:tn, :], h_tok[0:tn, i, :], h_tok_hi[i][0:tn, :].bitcast(F32), ALU.subtract)
                    if n == 4:
                        dve.wait_ge(ev("moe_gsel_ready"), w + 1)
                        dve.wait_ge(ev("moe_gsel_parts"), 2 * w + 2)
                        c = dve.value_load(column_of[0:1, bass.ds(w, 1)], min_val=0, max_val=ITEMS)
                        dve.tensor_copy(gate_c[:, :], gate_w[:, :, bass.ds(c, 1)].rearrange("p i o -> p (i o)")).then_inc(moe_step, 1)
                        dve.wait_ge(moe_step, 2 * w + 2)
                        for i in range(3):
                            last = dve.tensor_scalar(gsel_t[:, i, :], iota_slot[:, :], rank_c[:, i:i + 1], gate_c[:, i:i + 1],
                                                     ALU.is_equal, ALU.mult)
                            last.then_inc(ev("moe_gsel_ready" if i == 2 else "moe_gsel_parts"), 1)
                    if n == 12 + SPLITS - 1:
                        dve.wait_ge(ev("moe_gs_filled"), w + 1)
                        dve.tensor_copy(gs, banks[:, 7, 0:T]).then_inc(ev("moe_gs_kept"), 1)
                    if n == 30:
                        dve.wait_ge(ev("moe_gsel_ready"), w + 2)
                        dve.wait_ge(ev("moe_gsel_parts"), 2 * w + 4)
                        dve.wait_ge(ev("moe_sel_parts"), 2 * w + 2)
                        c = dve.value_load(column_of[0:1, bass.ds(w + 1, 1)], min_val=0, max_val=ITEMS)
                        dve.tensor_copy(rank_c[:, :], rank_w[:, :, bass.ds(c, 1)].rearrange("p i o -> p (i o)")).then_inc(moe_step, 1)
                        select(2 * w + 3, w + 1)
                    for j in range(EJ):
                        if n == last_unit("w3", j) + SPLITS - 1:
                            dve.wait_ge(ev("moe_units_used"), EU * w + SPLITS + last_unit("w3", j) + 1)
                            dve.wait_ge(ev("moe_silu_ready"), EJ * w + j + 1)
                            dve.tensor_tensor(g_tok[:, :], g_tok[:, :], banks[:, 2 * (j % 2) + 1, :], ALU.mult)\
                               .then_inc(ev("moe_g_ready"), 1)
                        if n == last_unit("w3", j) + TURN + SPLITS - 1:
                            dve.wait_ge(ev("moe_g_hi_ready"), EJ * w + j + 1)
                            dve.tensor_tensor(g_lo[:, j % 2, :], banks[:, 6, :], g_hi[:, j % 2, :].bitcast(F32), ALU.subtract)\
                               .then_inc(ev("moe_g_lo_ready"), 1)

            def select_pair(d, w):
                c = dve.value_load(column_of[0:1, bass.ds(w, 1)], min_val=0, max_val=ITEMS)
                c2 = dve.value_load(second_of[0:1, bass.ds(w, 1)], min_val=0, max_val=ITEMS)
                for g, cc in enumerate((c, c2)):
                    dve.tensor_copy(rank_p[:, g, :], rank_w[:, :, bass.ds(cc, 1)].rearrange("p i o -> p (i o)"))\
                       .then_inc(ev("pair_step"), 1)
                dve.tensor_copy(gate_p[:, :], gate_w[:, :, bass.ds(c, 1)].rearrange("p i o -> p (i o)")).then_inc(ev("pair_step"), 1)
                dve.wait_ge(ev("pair_step"), 3 * d + 3)
                for g in range(2):
                    for i in range(3):
                        last = dve.tensor_scalar(sel_p[:, i, g, :], iota_slot[:, :], rank_p[:, g, i:i + 1], None, ALU.is_equal)
                last.then_inc(ev("pair_sel_ready"), 1)
                for g in range(2):
                    for i in range(3):
                        last = dve.tensor_scalar(gsel_p[:, g, i, :], iota_slot[:, :], rank_p[:, g, i:i + 1], gate_p[:, i:i + 1],
                                                 ALU.is_equal, ALU.mult)
                last.then_inc(ev("pair_gsel_ready"), 1)

            def gathered_pair(d):
                for half in range(2):
                    dve.wait_ge(ev("pair_x_hi_ready"), 2 * d + half + 1)
                    hi, lo = (x[:, 4 * half:4 * half + 4, :, :].rearrange("p k g n -> p (k g n)") for x in (x_hi2, x_lo2))
                    dve.tensor_tensor(lo, banks[:, 2 * half:2 * half + 2, :].rearrange("p b n -> p (b n)"), hi.bitcast(F32),
                                      ALU.subtract).then_inc(ev("pair_x_lo_ready"), 1)

            def pair(d, w):
                for n in range(EU):
                    s, o = n // UNITS, (n % UNITS) * UW
                    dve.wait_ge(ev("moe_hi_ready"), EU * w + n + 1)
                    dve.tensor_tensor(w_lo[:, n % SPLITS, :], ring[:, pos_of(s), o:o + UW],
                                      w_hi[:, n % SPLITS, :].bitcast(F32), ALU.subtract).then_inc(ev("moe_lo_ready"), 1)
                    if n == 4 + SPLITS + 1:
                        dve.wait_ge(ev("pair_gs_filled"), d + 1)
                        dve.tensor_copy(gs_p[:, :, :], banks[:, 4:6, 0:T]).then_inc(ev("pair_gs_kept"), 1)
                    if n == 30:
                        select_pair(d + 1, w + 1)
                    for j in range(EJ):
                        if n == last_unit("w3", j) + SPLITS - 1:
                            dve.wait_ge(ev("moe_units_used"), EU * w + SPLITS + last_unit("w3", j) + 1)
                            dve.wait_ge(ev("pair_silu_ready"), EJ * d + j + 1)
                            dve.tensor_tensor(g2[:, :], g2[:, :], banks[:, 2:4, :].rearrange("p b n -> p (b n)"), ALU.mult)\
                               .then_inc(ev("pair_g_ready"), 1)
                        if n == last_unit("w3", j) + SPLITS:
                            dve.wait_ge(ev("pair_g_hi_ready"), EJ * d + j + 1)
                            g_j = g_hi2[:, j % 2, :, :].rearrange("p c n -> p (c n)")
                            dve.tensor_tensor(g_lo2[:, j % 2, :, :].rearrange("p c n -> p (c n)"), g2[:, :], g_j.bitcast(F32),
                                              ALU.subtract).then_inc(ev("pair_g_lo_ready"), 1)
                gathered_pair(d + 1)
                dve.wait_ge(ev("moe_units_used"), EU * w + SPLITS + EU)
                dve.tensor_copy(out_p[:, :], banks[:, 6:8, :].rearrange("p b n -> p (b n)")).then_inc(ev("pair_out_kept"), 1)
                for k in range(KC):
                    dve.wait_ge(ev("pair_y_filled"), KC * d + k + 1)
                    dve.tensor_tensor(zT[:, k, :], zT[:, k, :], banks[:, 4 + k % 4, 0:T], ALU.add).then_inc(ev("pair_y_added"), 1)

            dve.sem_inc(ev("moe_gsel_parts"), 2)

            def between(last):
                tail(last)
                dve.sem_inc(ev("pair_y_added"), 1)
                select_pair(0, last + 1)
                gathered_pair(0)

            passes(dve, expert, pair, between)
            dve.drain()
            step(dve.tensor_tensor(t8[:, :, :], zT[:, :, TP:T], adaT[:, 1, 5 * KC:6 * KC, 1:9], ALU.mult))
            settle()
            for c in range(KC):
                step(dve.scalar_tensor_tensor(zT[:, c, 0:TP], zT[:, c, 0:TP], col(1, 5, c), xT[:, c, 0:TP], ALU.mult, ALU.add))
                step(dve.tensor_tensor(zT[:, c, TP:T], xT[:, c, TP:T], t8[:, c, :], ALU.add), ev("ln_chunk_ready"))
            rstd_ready(4, zT[:, :, :])
            for half in range(2):
                s = slice(4 * half, 4 * half + 4)
                step(dve.tensor_tensor(zT[:, s, :], zT[:, s, :], rstd[:, :].unsqueeze(1).to_broadcast([P, 4, T]), ALU.mult))
                settle()
                for c in range(4 * half, 4 * half + 4):
                    g, b = PRM_LNG + 3 * KC + c, PRM_LNB + 3 * KC + c
                    step(dve.tensor_scalar(xT[:, c, :], zT[:, c, :], prm[:, g:g + 1], prm[:, b:b + 1], ALU.mult, ALU.add))
                announce("y_ready")

        @block_.sync
        def _(sp):
            sp.dma_start(c_rows[0:1, :], c_prompt).then_inc(ev("c_loaded"), 16)
            sp.dma_start(c_rows[1:9, :], c_sample).then_inc(ev("c_loaded"), 16)
            sp.dma_start(pages_sb[:, :], page_table.rearrange("(o n) g -> o (n g)", o=1)).then_inc(ev("pages_loaded"), 16)
            for dst, src in (
                    (rows[0:96, 0, :], ada_b.rearrange("l (r p) -> (l r) p", p=P)),
                    (rows[96:128, 0, :], ln_g.rearrange("l s (c p) -> (l s c) p", p=P)),
                    (rows[0:32, 1, :], ln_b.rearrange("l s (c p) -> (l s c) p", p=P)),
                    (rows[32:48, 1, :], conv_b_pw1.rearrange("l (c p) -> (l c) p", p=P)),
                    (rows[48:56, 1, :], conv_b_dw.rearrange("l (c p) -> (l c) p", p=P)),
                    (rows[56:64, 1, :], conv_ln_g.rearrange("l (c p) -> (l c) p", p=P)),
                    (rows[64:72, 1, :], conv_ln_b.rearrange("l (c p) -> (l c) p", p=P)),
                    (rows[72:80, 1, :], conv_b_pw2.rearrange("l (c p) -> (l c) p", p=P)),
                    (rows[0:128, 2, :], conv_w_dw.rearrange("l j (c p) -> (l j c) p", p=P)[0:128, :]),
                    (rows[0:120, 3, :], conv_w_dw.rearrange("l j (c p) -> (l j c) p", p=P)[128:248, :])):
                sp.dma_start(dst, src).then_inc(ev("params_loaded"), 16)
            sp.dma_start(kx_tok, x_prompt[0].rearrange("(i p) d -> p i d", p=P)).then_inc(ev("x_loaded"), 16)
            sp.dma_start(kx_s[0:NS, :], x_sample[:, 0, :]).then_inc(ev("x_loaded"), 16)
            sp.dma_start(wr[:, :, :], moe_w_router[0].rearrange("(k p) e -> p k e", p=P)).then_inc(ev("router_loaded"), 16)
            sp.dma_start(br[:, :], moe_b_router).then_inc(ev("router_loaded"), 16)

            def ring_free(n):
                if n >= RING:
                    name, _loads, who = stream[n - RING]
                    if who == "dve":
                        sp.wait_ge(ev("key_slots_used"), name[1] + 1)
                    elif who == "split":
                        sp.wait_ge(ev("w_lo_ready"), UNITS * (split_no[name] + 1))
                    else:
                        sp.wait_ge(*used[n - RING])

            phys_of = {}
            for n, (_name, loads, _who) in enumerate(stream):
                ring_free(n)
                for at, width, kn, src, page in loads:
                    if page is None:
                        dst = ring[:, n % RING, at:at + width].rearrange("p (k n) -> p k n", k=kn)
                    else:
                        seq, g = page
                        if (seq, g) not in phys_of:
                            sp.wait_ge(ev("pages_loaded"), 16)
                            i = seq * PAGES + g
                            phys_of[seq, g] = sp.value_load(pages_sb[0:1, i:i + 1], min_val=0, max_val=src.shape[0] - 1)
                        phys = phys_of[seq, g]
                        dst = ring[:, n % RING, at:at + width]
                        src = src[bass.ds(phys, 1)].rearrange("o s h d -> (o s) (h d)")
                    sp.dma_start(dst, src).then_inc(slot_sem[n % RING], 16)

            def expert_load(e, s):
                kind, j, part = EXPERT_SLOTS[s]
                if kind == "w2":
                    src = moe_w2[0][bass.ds(e, 1), j * 512 + part * 256:j * 512 + (part + 1) * 256, :].rearrange("o (k p) n -> p (o k) n", p=P)
                else:
                    w = moe_w1 if kind == "w1" else moe_w3
                    src = w[0][bass.ds(e, 1), part * 512:(part + 1) * 512, j * 512:(j + 1) * 512].rearrange("o (k p) n -> p (o k) n", p=P)
                dst = ring[:, pos_of(s), :].rearrange("p (k n) -> p k n", n=src.shape[-1])
                sp.dma_start(dst, src).then_inc(slot_sem[pos_of(s)], 16)

            def expert(e, w, s):
                sp.wait_ge(ev("moe_lo_ready"), EU * w + UNITS * (s - RING + 1))
                expert_load(e, s)

            for s in range(ES):
                if s < RING:
                    ring_free(NPRE + s)
                    expert_load(0, s)
                else:
                    expert(0, 0, s)
            sp.wait_ge(ev("moe_list_ready"), 1)
            items = sp.value_load(n_items[0:1, 0:1], min_val=NE, max_val=MAX_ITEMS)
            with sp.Fori(1, MAX_ITEMS) as w:
                with sp.If(items > w):
                    e = sp.value_load(expert_of[0:1, bass.ds(w, 1)], min_val=0, max_val=NE - 1)
                    for s in range(ES):
                        expert(e, w, s)
                sp.nop()
            for half in range(2):
                cols = slice(half * 512, (half + 1) * 512)
                for i, (t0, tn) in enumerate(TILES):
                    sp.wait_ge(ev("y_tok_ready"), 3 * half + i + 1)
                    dst = y_prompt[0, t0:t0 + tn, cols] if i < 2 else y_sample[:, 0, cols]
                    sp.dma_start(dst, h_tok[0:tn, i, cols]).then_inc(ev("y_stored"), 16)
            sp.wait_ge(ev("y_stored"), 16 * 6)

        @block_.gpsimd
        def _(pool):
            step = Steps(pool, ev("pool_step"))

            def do(ins):
                step(ins)
                step.settle()

            do(pool.memset(ident[:, :], 0.0))
            do(pool.affine_select(out=ident[:, :], in_=ident[:, :], compare_op=ALU.not_equal, fill=1.0,
                                  base=0, pattern=[[-1, P]], channel_multiplier=1))
            do(pool.memset(ones[:, :], 1.0))
            do(pool.memset(mean_w[:, :], 1.0 / D))
            do(pool.memset(before[:, :], 1.0))
            do(pool.affine_select(out=before[:, :], in_=before[:, :], compare_op=ALU.is_gt, fill=0.0,
                                  base=0, pattern=[[1, P]], channel_multiplier=-1))
            do(pool.iota(iota_slot[:, :], pattern=[[1, P]], base=0, channel_multiplier=0, allow_small_or_imprecise_dtypes=True))
            do(pool.iota(iota_e[:, :], pattern=[[1, NE]], base=0, channel_multiplier=0, allow_small_or_imprecise_dtypes=True))
            do(pool.iota(iota_place[:, :], pattern=[[1, LIST]], base=0, channel_multiplier=0, allow_small_or_imprecise_dtypes=True))
            do(pool.iota(column_v[:, 0:ITEMS], pattern=[[1, ITEMS]], base=0, channel_multiplier=0, allow_small_or_imprecise_dtypes=True))
            do(pool.iota(column_v[:, ITEMS:], pattern=[[1, NE]], base=0, channel_multiplier=0, allow_small_or_imprecise_dtypes=True))
            do(pool.iota(expert_v[:, :], pattern=[[0, GROUPS + 1], [1, NE]], base=0, channel_multiplier=0, allow_small_or_imprecise_dtypes=True))
            do(pool.memset(eps_t[:, :], EPS))
            for q0, kn, at in ((0, P, 0), (P, TP, P)):
                d = dist_p[:, at:at + kn]
                do(pool.iota(d, pattern=[[1, kn]], base=-q0, channel_multiplier=-1, allow_small_or_imprecise_dtypes=True))
                do(pool.affine_select(out=d, in_=d, compare_op=ALU.is_ge, fill=MASKED, base=q0, pattern=[[-1, kn]],
                                      channel_multiplier=1))
            do(pool.iota(dist_s, pattern=[[1, PAST]], base=-PAST, channel_multiplier=0, allow_small_or_imprecise_dtypes=True))
            do(pool.memset(e16, 0.0))
            for n in range(NS):
                do(pool.affine_select(out=e16, in_=e16, compare_op=ALU.not_equal, fill=1.0, base=-H * n,
                                      pattern=[[-1, H]], channel_multiplier=1))
            do(pool.memset(fold, 0.0))
            for n in range(4):
                do(pool.affine_select(out=fold, in_=fold, compare_op=ALU.not_equal, fill=1.0, base=-32 * n,
                                      pattern=[[-1, 9]], channel_multiplier=1))
            for m, pattern, mult in ((e8, [[-H, NS]], 1), (e8T, [[1, P]], -H)):
                do(pool.memset(m, 1.0))
                do(pool.affine_select(out=m, in_=m, compare_op=ALU.is_ge, fill=0.0, base=0, pattern=pattern,
                                      channel_multiplier=mult))
                do(pool.affine_select(out=m, in_=m, compare_op=ALU.is_ge, fill=0.0, base=H - 1,
                                      pattern=[[-pattern[0][0], pattern[0][1]]], channel_multiplier=-mult))
            for h in range(H):
                do(pool.memset(slope8[:, h:h + 1], 8.0 * 2.0 ** (-8.0 * (h + 1) / H)))
            pool.sem_inc(ev("constants_ready"), 1)

            def store(dst, src, name="kv_stored"):
                pool.dma_start(dst, src).then_inc(ev(name), 16)

            store(nc_sample[0, :, 0:CW - 2, :], state_conv[0, :, 1:CW - 1, :], "state_stored")
            pool.wait_ge(ev("v_ready"), 1)
            store(nv_prompt[0, 0].rearrange("(i p) h d -> p i (h d)", p=P), v_tok)
            store(nv_sample[0, :, 0].rearrange("n h d -> n (h d)"), v_s)
            pool.wait_ge(ev("k_ready"), 1)
            store(nk_prompt[0, 0].rearrange("(i p) h d -> p i (h d)", p=P), kx_tok)
            store(nk_sample[0, :, 0].rearrange("n h d -> n (h d)"), kx_s[0:NS, :])
            pool.wait_ge(ev("ln_done"), 2)
            for i in range(2):
                pool.dma_start(st_rows[0:120, i, :], state_conv[0].rearrange("n j d -> (n j) d")[120 * i:120 * (i + 1), :])\
                    .then_inc(ev("state_loaded"), 16)
            pool.wait_ge(ev("u_tok_ready"), 1)
            store(nc_prompt[0, 0], u_p, "u_stored")
            store(nc_sample[0, :, CW - 2, :], u_s, "u_stored")
            pool.wait_ge(ev("ln_done"), 4)
            pool.memset(zT[:, :, :], 0.0).then_inc(ev("moe_y_added"), 1)
            pool.wait_ge(ev("state_stored"), 16)
            pool.wait_ge(ev("kv_stored"), 64)
            pool.wait_ge(ev("u_stored"), 32)


_INS = ['x_prompt', 'x_sample', 'cache_k', 'cache_v', 'state_conv', 'page_table', 'c_prompt', 'c_sample',
        'ada_w', 'ada_b', 'ln_g', 'ln_b', 'attn_w_qkv', 'attn_w_o', 'conv_w_pw1', 'conv_b_pw1', 'conv_w_dw',
        'conv_b_dw', 'conv_ln_g', 'conv_ln_b', 'conv_w_pw2', 'conv_b_pw2', 'ffn_w1', 'ffn_w3', 'ffn_w2',
        'moe_w_router', 'moe_b_router', 'moe_w1', 'moe_w3', 'moe_w2']
_OUTS = [((1, TP, D), 'float32'), ((NS, 1, D), 'float32'),
         ((1, 1, TP, H, HD), 'float32'), ((1, 1, TP, H, HD), 'float32'),
         ((1, NS, 1, H, HD), 'float32'), ((1, NS, 1, H, HD), 'float32'),
         ((1, 1, CW - 1, D), 'float32'), ((1, NS, CW - 1, D), 'float32')]


def kernel(**inputs):
    import numpy as _np
    import concourse.bacc as _bacc
    from concourse import mybir as _mybir
    from concourse.bass_utils import run_bass_kernel_spmd as _run

    nc = _bacc.Bacc("TRN2", target_bir_lowering=False, num_devices=1, dynamic_dma_scratch_size=4096)
    arrays, args = {}, []
    for name in _INS:
        a = _np.ascontiguousarray(inputs[name])
        arrays[f"in_{name}_dram"] = a
        args.append(nc.dram_tensor(f"in_{name}_dram", a.shape, _mybir.dt.from_np(a.dtype), kind="ExternalInput").ap())
    for i, (shape, dtype) in enumerate(_OUTS):
        dt = _mybir.dt.from_np(_np.dtype(dtype))
        args.append(nc.dram_tensor(f"out_{i}_dram", shape, dt, kind="ExternalOutput").ap())
    build(nc, *args)
    r = _run(nc, [arrays], core_ids=[0])
    return tuple(r.results[0][f"out_{i}_dram"] for i in range(len(_OUTS)))
```
